# Optimizing a Trainium2 kernel written in Bass

```python
import math
import jax
import jax.numpy as jnp
from jax import lax
import numpy as np

D_MODEL = 1024
BATCH = 1
SEQ = 256
DEPTH = 2
DEC_BATCH = 8
DEC_SEQ = 4
PAST_LEN = 256
PAGE_SIZE = 128

NSA_HEADS = 8
NSA_KV_HEADS = 2
NSA_GROUP = NSA_HEADS // NSA_KV_HEADS
HEAD_DIM = 64
NSA_WIDTH = NSA_HEADS * HEAD_DIM
KV_WIDTH = NSA_KV_HEADS * HEAD_DIM
CMP_BLOCK = 32
CMP_STRIDE = 16
CMP_HIDDEN = 128
SEL_BLOCK = 64
SEL_TOP_N = 16
SEL_FORCE = 1e4
WINDOW = 512
WIN_Q_BLOCK = 128
SEL_Q_BLOCK = 64
REL_BUCKETS = 32
REL_MAX_DIST = 128
M_HEADS = 4
M_HEAD_DIM = 128
M_WIDTH = M_HEADS * M_HEAD_DIM
CONV_W = 4
M_CHUNK = 64
D_FF = 2816
N_EXPERTS = 8
TOP_K = 2
MOE_BLOCK = 128
EPS = 1e-6
IN_WIDTHS = (NSA_WIDTH, KV_WIDTH, KV_WIDTH, KV_WIDTH, KV_WIDTH, KV_WIDTH, KV_WIDTH, 3 * NSA_HEADS, M_WIDTH, M_WIDTH, 2 * M_HEADS, D_MODEL, D_MODEL)
IN_COLS = NSA_WIDTH + 6 * KV_WIDTH + 3 * NSA_HEADS + 2 * M_WIDTH + 2 * M_HEADS + 2 * D_MODEL

kernel_name = 'nsa_mlstm_gated_hybrid_step'

def rmsnorm(x, g):
    xf = x.astype(jnp.float32)
    y = xf * lax.rsqrt(jnp.mean(xf * xf, axis=-1, keepdims=True) + EPS)
    return (y * g.astype(jnp.float32)).astype(x.dtype)

def split_cols(z):
    offs = np.cumsum((0,) + IN_WIDTHS)
    return [z[..., int(offs[i]):int(offs[i + 1])] for i in range(len(IN_WIDTHS))]

def rel_bucket(dist):
    d = jnp.maximum(dist, 0)
    exact = REL_BUCKETS // 2
    log_part = exact + (jnp.log(jnp.maximum(d, 1).astype(jnp.float32) / exact)
                        / math.log(REL_MAX_DIST / exact) * (REL_BUCKETS - exact)).astype(jnp.int32)
    return jnp.where(d < exact, d, jnp.minimum(log_part, REL_BUCKETS - 1))

def rel_bias(table, dist):
    return table[rel_bucket(dist)].astype(jnp.float32)

def masked_softmax(s, mask):
    p = jax.nn.softmax(jnp.where(mask, s, -1e30), axis=-1)
    return jnp.where(mask, p, 0.0)

def compress(kv, pe, w1, w2):
    b, t = kv.shape[:2]
    n_chunk = t // CMP_STRIDE
    ch = kv[:, :n_chunk * CMP_STRIDE].reshape(b, n_chunk, CMP_STRIDE, NSA_KV_HEADS, HEAD_DIM)
    blocks = jnp.concatenate([ch[:, :-1], ch[:, 1:]], axis=2) + pe[:, None, :]
    hid = jax.nn.gelu(jnp.einsum('bnlhd,lde->bnhe', blocks, w1))
    return jnp.einsum('bnhe,ed->bnhd', hid, w2)

def cmp_attn(q, kc, vc, q_pos, table):
    nq, nc = q_pos.shape[0], kc.shape[1]
    block_end = jnp.arange(nc) * CMP_STRIDE + (CMP_BLOCK - 1)
    dist = q_pos[:, None] - block_end[None, :]
    bias = jnp.moveaxis(rel_bias(table, dist).reshape(nq, nc, NSA_KV_HEADS, NSA_GROUP), 1, 3)
    s = jnp.einsum('bqhgd,bnhd->bqhgn', q, kc).astype(jnp.float32) + bias
    p = masked_softmax(s, (dist >= 0)[:, None, None, :])
    return jnp.einsum('bqhgn,bnhd->bqhgd', p.astype(vc.dtype), vc), p

def select_blocks(p_cmp, q_pos, n_sel):
    nc = p_cmp.shape[-1]
    c0 = jnp.arange(nc) * CMP_STRIDE
    s0 = jnp.arange(n_sel) * SEL_BLOCK
    ov = jnp.clip(jnp.minimum(c0[:, None] + CMP_BLOCK, s0[None, :] + SEL_BLOCK)
                  - jnp.maximum(c0[:, None], s0[None, :]), 0, CMP_BLOCK).astype(jnp.float32) / CMP_BLOCK
    imp = jnp.einsum('bqhgn,ns->bqhs', p_cmp, ov)
    cur = q_pos // SEL_BLOCK
    j = jnp.arange(n_sel)
    valid = (j[None, :] <= cur[:, None])[:, None, :]
    forced = ((j[None, :] == 0) | (j[None, :] == cur[:, None]) | (j[None, :] == cur[:, None] - 1))[:, None, :]
    score = jnp.where(valid, imp + jnp.where(forced, SEL_FORCE, 0.0), -1.0)
    top_s, idx = lax.top_k(score, min(SEL_TOP_N, n_sel))
    return idx, top_s >= 0.0

def to_blocks(kv):
    b, t = kv.shape[:2]
    n_sel = -(-t // SEL_BLOCK)
    kv = jnp.pad(kv, ((0, 0), (0, n_sel * SEL_BLOCK - t), (0, 0), (0, 0)))
    return kv.reshape(b, n_sel, SEL_BLOCK, NSA_KV_HEADS, HEAD_DIM).transpose(0, 3, 1, 2, 4)

def sel_attn(q, ks_b, vs_b, idx, ok, q_pos, table):
    b = q.shape[0]
    bi = jnp.arange(b)[:, None, None, None]
    hi = jnp.arange(NSA_KV_HEADS)[None, None, :, None]
    kg = ks_b[bi, hi, idx]
    vg = vs_b[bi, hi, idx]
    k_pos = idx[..., None] * SEL_BLOCK + jnp.arange(SEL_BLOCK)
    dist = q_pos[None, :, None, None, None] - k_pos
    mask = (dist >= 0) & ok[..., None]
    table_g = table.reshape(REL_BUCKETS, NSA_KV_HEADS, NSA_GROUP)
    bias = jnp.moveaxis(table_g[rel_bucket(dist), hi[..., None]].astype(jnp.float32), -1, 3)
    s = jnp.einsum('bqhgd,bqhnsd->bqhgns', q, kg).astype(jnp.float32) + bias
    sh = s.shape
    p = masked_softmax(s.reshape(sh[:4] + (-1,)), mask.reshape(mask.shape[:3] + (1, -1)))
    return jnp.einsum('bqhgns,bqhnsd->bqhgd', p.reshape(sh).astype(vg.dtype), vg)

def window_attn(q, k, v, q_pos, k_pos, table):
    nq, nk = q_pos.shape[0], k_pos.shape[0]
    dist = q_pos[:, None] - k_pos[None, :]
    mask = (dist >= 0) & (dist < WINDOW) & (k_pos[None, :] >= 0)
    bias = jnp.moveaxis(rel_bias(table, dist).reshape(nq, nk, NSA_KV_HEADS, NSA_GROUP), 1, 3)
    s = jnp.einsum('bqhgd,bkhd->bqhgk', q, k).astype(jnp.float32) + bias
    p = masked_softmax(s, mask[:, None, None, :])
    return jnp.einsum('bqhgk,bkhd->bqhgd', p.astype(v.dtype), v)

def window_prompt(q, k, v, table):
    b, t = q.shape[:2]
    pad = ((0, 0), (WINDOW, 0), (0, 0), (0, 0))
    kp, vp = jnp.pad(k, pad), jnp.pad(v, pad)
    n_qb = t // WIN_Q_BLOCK
    qb = q.reshape((b, n_qb, WIN_Q_BLOCK) + q.shape[2:])

    def one_block(i):
        start = i * WIN_Q_BLOCK
        qi = lax.dynamic_index_in_dim(qb, i, axis=1, keepdims=False)
        ki = lax.dynamic_slice_in_dim(kp, start, WINDOW + WIN_Q_BLOCK, axis=1)
        vi = lax.dynamic_slice_in_dim(vp, start, WINDOW + WIN_Q_BLOCK, axis=1)
        q_pos = start + jnp.arange(WIN_Q_BLOCK)
        k_pos = start - WINDOW + jnp.arange(WINDOW + WIN_Q_BLOCK)
        return window_attn(qi, ki, vi, q_pos, k_pos, table)

    out = lax.map(one_block, jnp.arange(n_qb))
    return jnp.moveaxis(out, 0, 1).reshape(q.shape)

def nsa_core(q, kc_all, vc_all, ks_all, vs_all, q_pos, table, pe, w1, w2):
    kcc = compress(kc_all, pe[0], w1[0], w2[0])
    vcc = compress(vc_all, pe[1], w1[1], w2[1])
    o_cmp, p_cmp = cmp_attn(q, kcc, vcc, q_pos, table)
    ks_b, vs_b = to_blocks(ks_all), to_blocks(vs_all)
    idx, ok = select_blocks(p_cmp, q_pos, ks_b.shape[2])
    nq = q.shape[1]
    if nq > SEL_Q_BLOCK and nq % SEL_Q_BLOCK == 0:
        n_qb = nq // SEL_Q_BLOCK

        def blk(a):
            return jnp.moveaxis(a.reshape((a.shape[0], n_qb, SEL_Q_BLOCK) + a.shape[2:]), 1, 0)

        o = lax.map(lambda a: sel_attn(a[0], ks_b, vs_b, a[1], a[2], a[3], table),
                    (blk(q), blk(idx), blk(ok), q_pos.reshape(n_qb, SEL_Q_BLOCK)))
        o_sel = jnp.moveaxis(o, 0, 1).reshape(q.shape)
    else:
        o_sel = sel_attn(q, ks_b, vs_b, idx, ok, q_pos, table)
    return o_cmp, o_sel

def mlstm_chunk(state, inp):
    c0, n0, m0 = state
    q, k, v, li, lf = inp
    L = q.shape[1]
    bcum = jnp.cumsum(lf, axis=1)
    log_d = bcum[:, :, None, :] - bcum[:, None, :, :] + li[:, None, :, :]
    causal = jnp.tril(jnp.ones((L, L), dtype=bool))
    log_d = jnp.where(causal[None, :, :, None], log_d, -jnp.inf)
    log_inter = bcum + m0[:, None, :]
    m = jnp.maximum(log_inter, jnp.max(log_d, axis=2))
    dw = jnp.exp(log_d - m[:, :, None, :])
    w_inter = jnp.exp(log_inter - m)
    s = jnp.einsum('bthd,bshd->btsh', q, k) * dw
    num = jnp.einsum('btsh,bshe->bthe', s, v) + w_inter[..., None] * jnp.einsum('bthd,bhde->bthe', q, c0)
    den = jnp.sum(s, axis=2) + w_inter * jnp.einsum('bthd,bhd->bth', q, n0)
    h = num / jnp.maximum(jnp.abs(den), jnp.exp(-m))[..., None]
    b_last = bcum[:, -1]
    log_s = b_last[:, None, :] - bcum + li
    m_new = jnp.maximum(b_last + m0, jnp.max(log_s, axis=1))
    ws = jnp.exp(log_s - m_new[:, None, :])
    wc = jnp.exp(b_last + m0 - m_new)
    c_new = wc[..., None, None] * c0 + jnp.einsum('bsh,bshd,bshe->bhde', ws, k, v)
    n_new = wc[..., None] * n0 + jnp.einsum('bsh,bshd->bhd', ws, k)
    return (c_new, n_new, m_new), h

def mlstm_scan(q, k, v, li, lf, state):
    b, t = q.shape[:2]
    if t % M_CHUNK == 0:
        n_ch = t // M_CHUNK

        def chunks(a):
            return jnp.moveaxis(a.reshape((b, n_ch, M_CHUNK) + a.shape[2:]), 1, 0)

        new_state, h = lax.scan(mlstm_chunk, state, (chunks(q), chunks(k), chunks(v), chunks(li), chunks(lf)))
        h = jnp.moveaxis(h, 0, 1).reshape(v.shape)
    else:
        new_state, h = mlstm_chunk(state, (q, k, v, li, lf))
    return h, new_state

def mlstm_branch(u, o_pre, if_pre, conv_prev, state, conv_w, conv_b, m_qkv, gate_b, norm_g):
    b, t, _ = u.shape
    ext = jnp.concatenate([conv_prev.astype(u.dtype), u], axis=1)
    conv = conv_b
    for j in range(CONV_W):
        conv = conv + ext[:, j:j + t] * conv_w[j]
    uc = jax.nn.silu(conv).reshape(b, t, M_HEADS, M_HEAD_DIM)
    uh = u.reshape(b, t, M_HEADS, M_HEAD_DIM)
    q = jnp.einsum('bthd,hde->bthe', uc, m_qkv[0]).astype(jnp.float32) * (M_HEAD_DIM ** -0.5)
    k = jnp.einsum('bthd,hde->bthe', uc, m_qkv[1]).astype(jnp.float32)
    v = jnp.einsum('bthd,hde->bthe', uh, m_qkv[2]).astype(jnp.float32)
    li = (if_pre[..., :M_HEADS] + gate_b[0]).astype(jnp.float32)
    lf = jax.nn.log_sigmoid((if_pre[..., M_HEADS:] + gate_b[1]).astype(jnp.float32))
    h, new_state = mlstm_scan(q, k, v, li, lf, state)
    hn = h * lax.rsqrt(jnp.mean(h * h, axis=-1, keepdims=True) + EPS)
    out = jax.nn.sigmoid(o_pre.astype(jnp.float32)) * hn.reshape(b, t, M_WIDTH) * norm_g.astype(jnp.float32)
    return out.astype(u.dtype), new_state, ext[:, t:]

def mixer(h, prm, past):
    b, t, _ = h.shape
    table = prm['table']
    (q, kc, vc, ks, vs, kw, vw, g_nsa, u, o_pre, if_pre, g_a, g_b) = split_cols(h @ prm['w_in'])
    q = q.reshape(b, t, NSA_KV_HEADS, NSA_GROUP, HEAD_DIM) * (HEAD_DIM ** -0.5)
    kc, vc, ks, vs, kw, vw = (a.reshape(b, t, NSA_KV_HEADS, HEAD_DIM) for a in (kc, vc, ks, vs, kw, vw))
    new_cmp = jnp.stack([kc, vc], axis=2)
    new_slc = jnp.stack([ks, vs], axis=2)
    win_rows = jnp.stack([kw, vw], axis=2)
    if past is None:
        q_pos = jnp.arange(t)
        kc_all, vc_all, ks_all, vs_all = kc, vc, ks, vs
        o_win = window_prompt(q, kw, vw, table)
        new_win = win_rows[:, t - min(WINDOW, t):]
        conv_prev = jnp.zeros((b, CONV_W - 1, M_WIDTH), u.dtype)
        m_state = (jnp.zeros((b, M_HEADS, M_HEAD_DIM, M_HEAD_DIM), jnp.float32),
                   jnp.zeros((b, M_HEADS, M_HEAD_DIM), jnp.float32),
                   jnp.zeros((b, M_HEADS), jnp.float32))
    else:
        pt = past['page_table']
        past_len = pt.shape[1] * past['cmp'].shape[1]
        pc = past['cmp'][pt].reshape((b, past_len) + past['cmp'].shape[2:])
        psl = past['slc'][pt].reshape((b, past_len) + past['slc'].shape[2:])
        kc_all = jnp.concatenate([pc[:, :, 0], kc], axis=1)
        vc_all = jnp.concatenate([pc[:, :, 1], vc], axis=1)
        ks_all = jnp.concatenate([psl[:, :, 0], ks], axis=1)
        vs_all = jnp.concatenate([psl[:, :, 1], vs], axis=1)
        q_pos = past_len + jnp.arange(t)
        w_buf = past['win'].shape[1]
        win_all = jnp.concatenate([past['win'].astype(win_rows.dtype), win_rows], axis=1)
        k_pos = past_len - w_buf + jnp.arange(w_buf + t)
        o_win = window_attn(q, win_all[:, :, 0], win_all[:, :, 1], q_pos, k_pos, table)
        new_win = win_all[:, t:]
        conv_prev = past['conv']
        m_state = (past['C'].astype(jnp.float32), past['n'].astype(jnp.float32), past['m'].astype(jnp.float32))
    o_cmp, o_sel = nsa_core(q, kc_all, vc_all, ks_all, vs_all, q_pos, table, prm['cmp_pe'], prm['cmp_w1'], prm['cmp_w2'])
    g = jax.nn.sigmoid(g_nsa.reshape(b, t, NSA_KV_HEADS, NSA_GROUP, 3))
    o_nsa = (g[..., 0:1] * o_cmp + g[..., 1:2] * o_sel + g[..., 2:3] * o_win).reshape(b, t, NSA_WIDTH)
    o_m, (c_new, n_new, m_new), conv_new = mlstm_branch(u, o_pre, if_pre, conv_prev, m_state, prm['conv_w'],
                                                        prm['conv_b'], prm['m_qkv'], prm['gate_b'], prm['m_norm'])
    merged = jax.nn.sigmoid(g_a) * (o_nsa @ prm['w_up_a']) + jax.nn.sigmoid(g_b) * (o_m @ prm['w_up_b'])
    return merged @ prm['w_out'], (new_cmp, new_slc, new_win, c_new, n_new, m_new, conv_new)

def swiglu(h, w1, w3, w2):
    return (jax.nn.silu(h @ w1) * (h @ w3)) @ w2

def moe_swiglu(h, router, w1, w3, w2):
    b, t, d = h.shape
    n = b * t
    x = h.reshape(n, d)
    logits = (x @ router).astype(jnp.float32)
    top_val, top_idx = lax.top_k(logits, TOP_K)
    gate = jax.nn.softmax(top_val, axis=-1).reshape(-1)
    e_flat = top_idx.reshape(-1)
    tok = jnp.arange(n * TOP_K) // TOP_K
    order = jnp.argsort(e_flat)
    e_sorted = e_flat[order]
    counts = jnp.bincount(e_flat, length=N_EXPERTS)
    padded = (counts + MOE_BLOCK - 1) // MOE_BLOCK * MOE_BLOCK
    pad_end = jnp.cumsum(padded)
    pad_start = pad_end - padded
    start = jnp.cumsum(counts) - counts
    dest = pad_start[e_sorted] + jnp.arange(n * TOP_K) - start[e_sorted]
    n_blocks = (n * TOP_K + N_EXPERTS * (MOE_BLOCK - 1) + MOE_BLOCK - 1) // MOE_BLOCK
    xd = jnp.zeros((n_blocks * MOE_BLOCK, d), x.dtype).at[dest].set(x[tok[order]])
    blk_e = jnp.minimum(jnp.searchsorted(pad_end, jnp.arange(n_blocks) * MOE_BLOCK, side='right'), N_EXPERTS - 1)
    yd = lax.map(lambda a: swiglu(a[0], w1[a[1]], w3[a[1]], w2[a[1]]),
                 (xd.reshape(n_blocks, MOE_BLOCK, d), blk_e))
    contrib = yd.reshape(-1, d)[dest] * gate[order][:, None].astype(yd.dtype)
    return jax.ops.segment_sum(contrib, tok[order], num_segments=n).reshape(b, t, d)

def channel_mixer(h, l, ffn_w1, ffn_w3, ffn_w2, moe_router, moe_w1, moe_w3, moe_w2):
    i = l // 2
    if l % 2 == 0:
        return swiglu(h, ffn_w1[i], ffn_w3[i], ffn_w2[i])
    return moe_swiglu(h, moe_router[i], moe_w1[i], moe_w3[i], moe_w2[i])

def setup_inputs(seed: int = 0) -> dict:
    key = jax.random.key(seed)
    ks = jax.random.split(key, 40)

    def nrm(i, shape, scale):
        return jax.random.normal(ks[i], shape, jnp.float32) * scale

    n_pages = PAST_LEN // PAGE_SIZE
    n_used = DEC_BATCH * n_pages
    n_phys = n_used + max(1, n_used // 4)
    w_buf = min(WINDOW, PAST_LEN)
    n_dense = (DEPTH + 1) // 2
    n_moe = DEPTH // 2
    kv_row = (2, NSA_KV_HEADS, HEAD_DIM)
    page_table = jax.random.permutation(ks[0], n_phys)[:n_used].reshape(DEC_BATCH, n_pages).astype(jnp.int32)
    gate_bias = jnp.stack([nrm(21, (DEPTH, M_HEADS), 0.1),
                           jnp.linspace(3.0, 6.0, M_HEADS)[None, :] + nrm(33, (DEPTH, M_HEADS), 0.1)], axis=1)
    return {
        'x_prompt': nrm(1, (BATCH, SEQ, D_MODEL), 1.0),
        'x_sample': nrm(2, (DEC_BATCH, DEC_SEQ, D_MODEL), 1.0),
        'cache_cmp_kv': nrm(3, (DEPTH, n_phys, PAGE_SIZE) + kv_row, 1.0),
        'cache_slc_kv': nrm(4, (DEPTH, n_phys, PAGE_SIZE) + kv_row, 1.0),
        'cache_win_kv': nrm(5, (DEPTH, DEC_BATCH, w_buf) + kv_row, 1.0),
        'state_mlstm_C': nrm(6, (DEPTH, DEC_BATCH, M_HEADS, M_HEAD_DIM, M_HEAD_DIM), 0.5),
        'state_mlstm_n': nrm(7, (DEPTH, DEC_BATCH, M_HEADS, M_HEAD_DIM), 0.5),
        'state_mlstm_m': jax.random.uniform(ks[8], (DEPTH, DEC_BATCH, M_HEADS), jnp.float32, 0.0, 2.0),
        'state_mlstm_conv': nrm(9, (DEPTH, DEC_BATCH, CONV_W - 1, M_WIDTH), 1.0),
        'page_table': page_table,
        'rel_bias_table': nrm(10, (REL_BUCKETS, NSA_HEADS), 0.5),
        'norm_mix': 1.0 + nrm(11, (DEPTH, D_MODEL), 0.05),
        'norm_ffn': 1.0 + nrm(12, (DEPTH, D_MODEL), 0.05),
        'norm_final': 1.0 + nrm(13, (D_MODEL,), 0.05),
        'w_in': nrm(14, (DEPTH, D_MODEL, IN_COLS), D_MODEL ** -0.5),
        'cmp_pe': nrm(15, (DEPTH, 2, CMP_BLOCK, HEAD_DIM), 0.1),
        'cmp_w1': nrm(16, (DEPTH, 2, CMP_BLOCK, HEAD_DIM, CMP_HIDDEN), (CMP_BLOCK * HEAD_DIM) ** -0.5),
        'cmp_w2': nrm(17, (DEPTH, 2, CMP_HIDDEN, HEAD_DIM), CMP_HIDDEN ** -0.5),
        'm_conv_w': nrm(18, (DEPTH, CONV_W, M_WIDTH), CONV_W ** -0.5),
        'm_conv_b': nrm(19, (DEPTH, M_WIDTH), 0.01),
        'm_qkv': nrm(20, (DEPTH, 3, M_HEADS, M_HEAD_DIM, M_HEAD_DIM), M_HEAD_DIM ** -0.5),
        'm_gate_bias': gate_bias,
        'm_norm': 1.0 + nrm(22, (DEPTH, M_WIDTH), 0.05),
        'w_up_a': nrm(23, (DEPTH, NSA_WIDTH, D_MODEL), NSA_WIDTH ** -0.5),
        'w_up_b': nrm(24, (DEPTH, M_WIDTH, D_MODEL), M_WIDTH ** -0.5),
        'w_out': nrm(25, (DEPTH, D_MODEL, D_MODEL), D_MODEL ** -0.5),
        'ffn_w1': nrm(26, (n_dense, D_MODEL, D_FF), D_MODEL ** -0.5),
        'ffn_w3': nrm(27, (n_dense, D_MODEL, D_FF), D_MODEL ** -0.5),
        'ffn_w2': nrm(28, (n_dense, D_FF, D_MODEL), D_FF ** -0.5),
        'moe_router': nrm(29, (n_moe, D_MODEL, N_EXPERTS), D_MODEL ** -0.5),
        'moe_w1': nrm(30, (n_moe, N_EXPERTS, D_MODEL, D_FF), D_MODEL ** -0.5),
        'moe_w3': nrm(31, (n_moe, N_EXPERTS, D_MODEL, D_FF), D_MODEL ** -0.5),
        'moe_w2': nrm(32, (n_moe, N_EXPERTS, D_FF, D_MODEL), D_FF ** -0.5),
    }

def reference(x_prompt, x_sample, cache_cmp_kv, cache_slc_kv, cache_win_kv, state_mlstm_C, state_mlstm_n,
              state_mlstm_m, state_mlstm_conv, page_table, rel_bias_table, norm_mix, norm_ffn, norm_final,
              w_in, cmp_pe, cmp_w1, cmp_w2, m_conv_w, m_conv_b, m_qkv, m_gate_bias, m_norm, w_up_a, w_up_b,
              w_out, ffn_w1, ffn_w3, ffn_w2, moe_router, moe_w1, moe_w3, moe_w2):
    xp, xs = x_prompt, x_sample
    prompt_states, sample_states = [], []
    for l in range(DEPTH):
        prm = {'table': rel_bias_table, 'w_in': w_in[l], 'cmp_pe': cmp_pe[l], 'cmp_w1': cmp_w1[l],
               'cmp_w2': cmp_w2[l], 'conv_w': m_conv_w[l], 'conv_b': m_conv_b[l], 'm_qkv': m_qkv[l],
               'gate_b': m_gate_bias[l], 'm_norm': m_norm[l], 'w_up_a': w_up_a[l], 'w_up_b': w_up_b[l],
               'w_out': w_out[l]}
        past = {'cmp': cache_cmp_kv[l], 'slc': cache_slc_kv[l], 'win': cache_win_kv[l],
                'C': state_mlstm_C[l], 'n': state_mlstm_n[l], 'm': state_mlstm_m[l],
                'conv': state_mlstm_conv[l], 'page_table': page_table}
        dp, st_p = mixer(rmsnorm(xp, norm_mix[l]), prm, None)
        ds, st_s = mixer(rmsnorm(xs, norm_mix[l]), prm, past)
        xp = xp + dp
        xs = xs + ds
        xp = xp + channel_mixer(rmsnorm(xp, norm_ffn[l]), l, ffn_w1, ffn_w3, ffn_w2, moe_router, moe_w1, moe_w3, moe_w2)
        xs = xs + channel_mixer(rmsnorm(xs, norm_ffn[l]), l, ffn_w1, ffn_w3, ffn_w2, moe_router, moe_w1, moe_w3, moe_w2)
        prompt_states.append(st_p)
        sample_states.append(st_s)
    y_prompt = rmsnorm(xp, norm_final)
    y_sample = rmsnorm(xs, norm_final)
    ps = [jnp.stack([s[i] for s in prompt_states]) for i in range(7)]
    ss = [jnp.stack([s[i] for s in sample_states]) for i in range(7)]
    return (y_prompt, y_sample, ps[0], ps[1], ps[2], ps[3], ps[4], ps[5], ps[6],
            ss[0], ss[1], ss[2], ss[3], ss[4], ss[5], ss[6])


_drawn_inputs = setup_inputs


def setup_inputs(seed=0):
    import zlib

    import numpy as np

    out = dict(_drawn_inputs(seed))
    spreads = {}
    factors = {'m_conv_b': 2.717}
    for name, (base, spread) in spreads.items():
        noise = np.random.default_rng([zlib.crc32(name.encode()), seed]).standard_normal(out[name].shape)
        drawn = base * np.exp(spread * noise) if base else spread * noise
        out[name] = jnp.asarray(drawn.astype(out[name].dtype))
    for name, factor in factors.items():
        out[name] = (out[name] * factor).astype(out[name].dtype)
    return out
```

```python
from contextlib import ExitStack

import numpy as np

import concourse.bass as bass
from concourse import mybir

ALU = mybir.AluOpType
ACT = mybir.ActivationFunctionType
F32 = mybir.dt.float32
I32 = mybir.dt.int32
AX = mybir.AxisListType

P = 128
D = 1024
KD = D // P
T = 256
NB, TS = 8, 4
NS = NB * TS
N = T + NS
ROWS = (P, P, NS)
PAST = 256
H, KVH, HD = 8, 2, 64
G = H // KVH
MH, MD = 4, 128
EPS = 1e-6
NBUCKET, MAX_DIST = 32, 128
NC_BLK = 15
FF = 2816
NE = 8
NEG = -1e30
DIM0 = 259
WB = 544

OFF_KV = 512
OFF_G = OFF_KV + 768
OFF_U = OFF_G + 24
OFF_O = OFF_U + 512
OFF_IF = OFF_O + 512
OFF_GA = OFF_IF + 8
OFF_GB = OFF_GA + D
KV_HALF = 396
UE = T + 3 + NB * 7

NITEM = 12
MOE = 1
FCH = FF // 256


def constants():
    cols = {}
    parts = []

    def put(name, a):
        a = np.asarray(a, np.float32)
        full = np.zeros((P, a.shape[1]), np.float32)
        full[:a.shape[0]] = a
        cols[name] = (sum(p.shape[1] for p in parts), a.shape[1])
        parts.append(full)

    r = np.arange(P)
    put("ident", np.eye(P))
    put("rev", np.eye(P)[::-1])
    put("ones", np.ones((P, P)))
    put("causal", np.where(r[:, None] > r[None, :], -NEG, 0.0))
    q = np.arange(NS)
    same = q[:, None] // TS == q[None, :] // TS
    put("causal_s", np.where(same & (q[:, None] <= q[None, :]), 0.0, -NEG))
    put("headsel", np.repeat(np.eye(MH), P, axis=1))
    start = np.ones(N)
    first = np.concatenate([[0], T + TS * np.arange(NB)])
    start[first] = 0.0
    put("keep", np.tile(start, (MH, 1)))
    put("reset", np.tile(np.where(start == 0.0, NEG, 0.0), (MH, 1)))
    put("hrow", np.repeat(np.eye(H), 16, axis=0))
    put("cvalid", np.stack([r >= 31, np.ones(P)], axis=1))
    put("bsel", np.repeat(np.eye(NB), TS, axis=0))
    put("iota", np.tile(r, (P, 1)))
    put("tri", np.where(r[:, None] < r[None, :], 1.0, 0.0))
    e = np.arange(NE)
    put("elow", np.tile((e[None, :] < e[:, None]).astype(np.float32).reshape(1, 64), (P, 1)))
    put("etri", (e[:, None] < e[None, :]).astype(np.float32))
    put("valid", np.stack([np.ones(P), np.ones(P), r < NS], axis=1))
    put("item", np.tile(np.arange(NITEM), (NE, 1)))
    put("eidx", e[:, None])
    keep_cols = sum(p.shape[1] for p in parts)
    sel = np.zeros((H, TS, P))
    for row in range(P):
        sel[row % H, (row // H) % TS, row] = 1.0
    put("rowsel", sel.reshape(H, TS * P))
    dist = DIM0 - np.arange(WB)
    d = np.maximum(dist, 0)
    exact = NBUCKET // 2
    logp = exact + (np.log(np.maximum(d, 1).astype(np.float32) / exact)
                    / np.float32(np.log(MAX_DIST / exact)) * (NBUCKET - exact)).astype(np.int32)
    bucket = np.where(d < exact, d, np.minimum(logp, NBUCKET - 1))
    put("bucket", (bucket[None, :] == np.arange(NBUCKET)[:, None]).astype(np.float32))
    put("future", np.tile(np.where(dist < 0, NEG, 0.0), (H, 1)))
    own = np.zeros((P, 2, NS))
    for tile in range(2):
        for row in range(P):
            own[row, tile] = np.where(np.arange(NS) // TS == tile * 4 + row // 32, 0.0, NEG)
    put("own", own.reshape(P, 2 * NS))
    return np.ascontiguousarray(np.concatenate(parts, axis=1)), cols, keep_cols


CONST, CC, NKEEP = constants()


class Event:

    def __init__(self, sem, per, first=0, n=None):
        self.sem, self.per, self.first, self.n = sem, per, first, per if n is None else n

    def at(self, l, k=None):
        return l * self.per + self.first + (self.n if k is None else k)

    def steps(self, *counts):
        firsts = [sum(counts[:i]) for i in range(len(counts))]
        return [Event(self.sem, self.per, f, n) for f, n in zip(firsts, counts)]


def build(nc, a, outs):
    with ExitStack() as ctx:
        ctx.enter_context(nc.allow_non_contiguous_dma(reason="small state vectors"))
        NCOL = CONST.shape[1]
        SLOT = 6144
        MIX = 4160
        XN, YN = 4620, 4608
        TOT = 53100
        arena = ctx.enter_context(nc.sbuf_tensor("arena", [P, TOT], F32))
        pos = [0]

        def take(n, at=None):
            if at is None:
                at = pos[0]
                pos[0] += n
                assert pos[0] <= TOT, pos[0]
            return arena[:, at:at + n]

        cst = take(NKEEP)

        def c(name):
            o, n = CC[name]
            if o + n <= NKEEP:
                return cst[:, o:o + n]
            return cset[:, o - NKEEP:o - NKEEP + n]

        xT = take(KD * N).rearrange("p (k n) -> p k n", k=KD)
        hT = take(KD * N).rearrange("p (k n) -> p k n", k=KD)
        vT = take(152)
        gbias = take(4)
        biasP = take(H * T).rearrange("p (h x) -> p h x", h=H)
        biasC = take(2 * H * NC_BLK).rearrange("p (m h n) -> p m h n", m=2, h=H)
        biasS = take(2 * N).rearrange("p (m x) -> p m x", m=2)
        biasSc = take(NC_BLK)
        small = take(160)
        pti = ctx.enter_context(nc.sbuf_tensor("pages", [1, 16], I32))
        itemi = ctx.enter_context(nc.sbuf_tensor("items", [1, 16], I32))
        ring0 = pos[0]
        take(3 * SLOT)
        slot = [take(SLOT, ring0 + s * SLOT) for s in range(3)]
        gap = [ring0 + s * SLOT + MIX for s in range(3)]
        work0 = pos[0]
        qT_at = pos[0]
        qT = take(G * N).rearrange("p (g n) -> p g n", g=G)
        omT = take(G * N, qT_at).rearrange("p (g n) -> p g n", g=G)
        kv = take(3 * 792).rearrange("p (m c) -> p m c", m=3)
        oT = take(MH * N).rearrange("p (h n) -> p h n", h=MH)
        uext = take(MH * UE).rearrange("p (h n) -> p h n", h=MH)
        X_at = pos[0]
        take(XN)
        cmpN = take(9 * 512, X_at).rearrange("p (s c) -> p s c", s=9)
        sw = take(4096, X_at).rearrange("p (r b g c) -> p r b g c", r=2, b=4, g=2)
        mk = take(3 * 512, X_at).rearrange("p (m h e) -> p m h e", m=3, h=MH)
        mv = take(3 * 516, X_at + 1536).rearrange("p (m h e) -> p m h e", m=3, h=MH)
        hm = take(3 * 512, X_at + 3084).rearrange("p (m h e) -> p m h e", m=3, h=MH)
        Y_at = pos[0]
        take(YN)
        kvT2 = take(4 * 9 * P, Y_at).rearrange("p (v s x) -> p v s x", v=2, s=18)
        C0 = take(NB * MH * 129, Y_at).rearrange("p (b h e) -> p b h e", b=NB, h=MH)
        cvp_at = Y_at + 4096
        cvp = take(512, cvp_at)
        Z_at = pos[0]
        take(KD * N)
        kTs = take(2048, Z_at).rearrange("p (r b x) -> p r b x", r=2, b=4)
        hsq = take(1536, Z_at).rearrange("p (m h e) -> p m h e", m=3, h=MH)
        merged = take(KD * N, Z_at).rearrange("p (k n) -> p k n", k=KD)
        B_at = pos[0]
        take(2960)
        Pb = take(1024, B_at).rearrange("p (i r x) -> p i r x", i=2, r=2)
        PT = take(1024, B_at + 1024).rearrange("p (i r k x) -> p i r k x", i=2, r=2, k=2)
        PTn = take(384, B_at + 2048)
        pc = take(256, B_at + 2432).rearrange("p (i x) -> p i x", i=2)
        PcT = take(256, B_at + 2688).rearrange("p (i x) -> p i x", i=2)
        Ps = take(2 * N, B_at).rearrange("p (r x) -> p r x", r=2)
        Psc = take(16, B_at + 2 * N)
        rows = take(2880, B_at).rearrange("p (i n) -> p i n", i=10)
        Db = take(416, B_at)
        Ab = take(416, B_at + 416)
        mvz = take(NB * 129, B_at + 832).rearrange("p (b e) -> p b e", b=NB)
        Cp = take(516, B_at + 1864).rearrange("p (h e) -> p h e", h=MH)
        nout = take(256, B_at + 2380)
        stmp = take(132, B_at + 2636)
        cvo = take(512, B_at)
        VcS_at = pos[0]
        VcS = take(NB * P).rearrange("p (b c) -> p b c", b=NB)
        mqz = take(MH * NB * NS, VcS_at).rearrange("p (h b t) -> p h b t", h=MH, b=NB)
        oNT = take(G * N).rearrange("p (g n) -> p g n", g=G)
        Qz = take(2 * P).rearrange("p (m r) -> p m r", m=2)
        RT = take(3 * P).rearrange("p (m r) -> p m r", m=3)
        R = take(N)
        Mrow = take(N)
        wcb = take(MH * NB).rearrange("p (h b) -> p h b", h=MH)
        gS = take(6).rearrange("p (m c) -> p m c", m=2)
        nld = take(P)
        ssum = take(12).rearrange("p (m h) -> p m h", m=3)
        ssr = take(12).rearrange("p (m h) -> p m h", m=3)
        ssi = take(12).rearrange("p (m h) -> p m h", m=3)
        srow = take(N)
        hidr = take(KVH * G * 16).rearrange("p (h x) -> p h x", h=KVH)
        us = take(MH * NS).rearrange("p (h t) -> p h t", h=MH)
        cstage = take(MH * 27).rearrange("p (h t) -> p h t", h=MH)
        ucT = take(MH * N, gap[0]).rearrange("p (h n) -> p h n", h=MH)
        hid = take(2 * KVH * 9 * 16, gap[0] + 1152).rearrange("p (v s x) -> p v s x", v=2, s=18)
        mqT = take(MH * N, gap[1]).rearrange("p (h n) -> p h n", h=MH)
        kTp = take(512, gap[1] + 1152).rearrange("p (r x) -> p r x", r=2)
        kTn = take(64, gap[1] + 1664).rearrange("p (r x) -> p r x", r=2)
        mkT = take(MH * N, gap[2]).rearrange("p (h n) -> p h n", h=MH)
        VcZ = take(512, gap[2] + 1152).rearrange("p (h d) -> p h d", h=H)
        KcT = take(144, gap[2] + 1664).rearrange("p (s x) -> p s x", s=9)
        cset = take(NCOL - NKEEP, ring0 + 2 * SLOT)
        w8 = take(WB, ring0 + 2 * SLOT + 2100)
        tab = take(8, ring0 + 2 * SLOT + 2700)
        vrow = take(2 * P, ring0 + 2 * SLOT + 2720)
        xtok = take(3 * D, work0).rearrange("p (m c) -> p m c", m=3)
        Lh = take(H * 384, work0 + 3 * D).rearrange("p (h x) -> p h x", h=H)
        gT = take(22 * N, X_at).rearrange("p (f n) -> p f n", f=22)
        sil = take(2 * 2 * N, B_at).rearrange("p (i f n) -> p i f n", i=2, f=2)
        mpos = [work0]

        def mtake(n):
            mpos[0] += n
            assert mpos[0] <= Y_at
            return take(n, mpos[0] - n)

        h2 = mtake(3 * D).rearrange("p (m c) -> p m c", m=3)
        Xg = mtake(D).rearrange("p (k s) -> p k s", k=KD)
        yS = mtake(D)
        Sel = mtake(3 * P).rearrange("p (m s) -> p m s", m=3)
        SelG = mtake(3 * P).rearrange("p (m s) -> p m s", m=3)
        SelT = mtake(N)
        sl = mtake(512).rearrange("p (i x) -> p i x", i=2)
        gm = mtake(512).rearrange("p (i x) -> p i x", i=2)
        gTm = mtake(512).rearrange("p (i f x) -> p i f x", i=2, f=2)
        posT = mtake(N)
        gateT = mtake(N)
        gt = mtake(192).rearrange("p (m e j) -> p m e j", m=3, e=NE)
        eq = mtake(192).rearrange("p (m e j) -> p m e j", m=3, e=NE)
        lg, rank, sel, gate, gx, posm = (mtake(24).rearrange("p (m e) -> p m e", m=3) for _ in range(6))
        posI, gateI = (mtake(3 * NITEM).rearrange("p (m w) -> p m w", m=3) for _ in range(2))
        gmx, gsum = mtake(3), mtake(3)
        cnt, nblk, estart, eend, nb2 = (mtake(1) for _ in range(5))
        ge1, ge2, Mw, off = (mtake(NITEM) for _ in range(4))
        cvec = small[:, 0:2]
        nm = small[:, 2:6].rearrange("p (i r) -> p i r", i=2)
        sums = small[:, 6:10].rearrange("p (i r) -> p i r", i=2)
        gg = small[:, 10:14].rearrange("p (i r) -> p i r", i=2)
        cmx = small[:, 14:22]
        csm = small[:, 22:30]
        m0c = small[:, 30:38]
        snm = small[:, 38:41]
        ssm = small[:, 41:44]
        sgg = small[:, 44:47]
        dn = small[:, 48:51]
        dn2 = small[:, 52:55]
        dn3 = small[:, 56:59]
        mout = small[:, 60:69]
        fsig = take(4 * N, B_at + 512).rearrange("p (i x n) -> p i x n", i=2, x=2)
        ytok = take(3 * D, work0).rearrange("p (m c) -> p m c", m=3)
        gns = take(72).rearrange("p (m c) -> p m c", m=3)

        router = take(KD * NE).rearrange("p (k e) -> p k e", k=KD)
        ps = ctx.enter_context(nc.psum_tensor("ps", [P, 8, 512], F32))
        scr = nc.dram_tensor("bias_scratch", (H, WB), F32)
        gscr = nc.dram_tensor("gate_scratch", (2, NS, 24), F32)
        scr, gscr = scr.ap(), gscr.ap()

        def ev(name, per=1):
            return Event(ctx.enter_context(nc.semaphore(name)), per)

        wl = [ev(f"weights_in_{s}", 10) for s in range(3)]
        s_setup = ev("setup_in")
        s_xin = ev("x_in")
        y_pe, y_ev, y_st = ev("y_pe"), ev("y_ev"), ev("y_st")
        pt_in, st_cmp = ev("pages_in"), ev("st_cmp", 16)
        w8_pe, vt_pe0, bp1_pe, xt_pe, bp2_pe, bp3_pe = ev("setup_tensor", 13).steps(1, 1, 1, 8, 1, 1)
        w8_ev, bp_ev = ev("setup_vector", 4).steps(1, 3)
        vt_ev0, xt_ev = ev("setup_scalar", 9).steps(1, 8)
        w8_st, hank = ev("bias_row_out"), ev("hankel_in")
        x_done = ev("x_done")
        sq_ev, ss_pe0, var_ev, sd_ev, h_ev = ev("sq_done"), ev("sumsq_pe"), ev("var_done"), ev("std_done"), ev("h_done")
        cvp_in, cv_pe, cv_ev = ev("conv_in", 16), ev("conv_pe"), ev("conv_ev")
        q_pe, q_ev = ev("q_pe", 4), ev("q_ev", 4)
        kv_pe, kv_ev = ev("kv_pe", 6), ev("kv_ev", 6)
        u_pe, u_ev = ev("u_pe", 4), ev("u_ev", 4)
        o_pe, o_ev = ev("o_pe", 4), ev("o_ev", 4)
        if_pe, if_ev = ev("if_pe"), ev("if_ev")
        kt_pe, kt_ev = ev("kt_pe"), ev("kt_ev")
        gs_ev = ev("gate_sig")
        uc_d, uc_a = ev("conv_sum", 1), ev("conv_silu", 1)
        mqk_pe, mqk_ev = ev("mqk_pe", 8), ev("mqk_ev", 8)
        cmp_in = ev("cmp_in", 16 * 34)
        ct_pe, ct_a, ct_d = ev("ct_pe", 9), ev("ct_evA", 5), ev("ct_evD", 4)
        hid_pe, c_ev, hid_ev = ev("hid_pe", 2), ev("c_ev", 2), ev("hid_ev", 2)
        kc_pe, kc_a, kc_d = ev("kc_pe"), ev("kc_evA"), ev("kc_evD")
        cs_pe, cx_d, cx_a, cx_n, cx_t, pct_ev = (ev("cs_pe", 2), ev("cx_sub", 2), ev("cx_exp", 2), ev("cx_norm", 2),
                                                 ev("cx_tr", 2), ev("pct_ev", 2))
        s_pe, sa_ev, nm_ev, ex_ev, p_ev, t_pe, pt_ev, pv_pe, on_ev = (
            ev("scores_pe", 16), ev("scores_taken", 16), ev("rowmax", 16), ev("probs", 16), ev("probs_gated", 16),
            ev("probsT_pe", 16), ev("probsT_ev", 16), ev("pv_pe", 16), ev("on_ev", 2))
        qz_ev, hidr_ev, cst_ev = ev("qz_ev"), ev("hidr_ev"), ev("cst_ev")
        sw_in = ev("past_in", 2 * 9 * 16)
        skt_pe, skt_a, skt_d = ev("skt_pe", 8), ev("skt_evA", 4), ev("skt_evD", 4)
        ss_pe, sadd, snm_ev, sex_ev, sps_ev, st_pe, spt_ev, spv_pe, son_ev = (
            ev("s_scores_pe", 2), ev("s_taken", 2), ev("s_max", 2), ev("s_probs", 2), ev("s_gated", 2),
            ev("s_probsT", 2), ev("s_probsT_ev", 2), ev("s_pv_pe", 2), ev("s_on_ev", 2))
        gsS_st, gsS_in = ev("gates_st", 16), ev("gates_in", 16)
        m0_in, c0_in, n0_in = ev("m0_in", 16), ev("c0_in", 16), ev("n0_in", 16)
        lf_d, lf_d2, row_d = ev("gate_rows_vector", 3).steps(1, 1, 1)
        lf_a, lf_a2, row_a = ev("gate_rows_scalar", 3).steps(1, 1, 1)
        rt_pe, rt_ev, wcb_ev = ev("rt_pe"), ev("rt_ev"), ev("wcb_ev")
        vt_pe, vt_ev, ktk_ev = ev("vt_pe", 6), ev("vt_ev", 3), ev("ktok_ev", 3)
        mz_ev = ev("mqz_ev")
        mb_pe, md_ev, me_ev, ma_ev, num_pe, mh_ev = (ev("mb_pe", 4), ev("md_ev", 4), ev("me_ev", 4), ev("ma_ev", 4),
                                                    ev("num_pe", 4), ev("mh_ev", 4))
        var2_ev, sd2_ev, hn_ev, om_pe, om_ev = ev("mvar_ev"), ev("msd_ev"), ev("hn_ev"), ev("om_pe", 4), ev("om_ev", 4)
        cp_pe, cp_ev = ev("cp_pe"), ev("cp_ev")
        vz_ev, cn_pe, cn_ev, cs_ev = ev("vz_ev", 4), ev("cn_pe", 4), ev("cn_ev", 4), ev("c0_scaled")
        no_pe, no_ev = ev("no_pe"), ev("no_ev")
        f_pe, f_sig, f_ev = ev("up_pe", 8), ev("up_sig", 8), ev("up_ev", 8)
        wo_pe, wo_ev = ev("wo_pe", 8), ev("wo_ev", 8)
        st_kv, st_state = ev("st_kv", 16 * 12), ev("st_state", 16 * 8)
        st_win = ev("st_win", 16)
        ff_pe, ff_sil, ff_g = ev("ff_pe", 22), ev("ff_silu", 22), ev("ff_g", 22)
        fy_pe, fy_ev = ev("fy_pe", 8), ev("fy_ev", 8)
        lg_pe, pos_pe, nb_pe, tp_pe, it_pe = ev("route_tensor", 5).steps(1, 1, 1, 1, 1)
        lgx_d, sel_d, pos_d, nb_d, items = ev("route_vector", 5).steps(1, 1, 1, 1, 1)
        h2_ev, lgx_a, tp_ev = ev("route_scalar", 3).steps(1, 1, 1)
        g_sel, g_pe, g_ev, m_h, m_sil, m_g, m_t, m_gT, mo_pe, yS_ev, cmb_pe, cmb_ev = (ev(n) for n in (
            "m_select", "m_gather", "m_gather_ev", "m_hidden", "m_silu", "m_gated", "m_turned", "m_turned_ev", "m_out",
            "m_y_ev", "m_combine", "m_combined"))


        V_MIX, V_FFN, V_FIN, V_CW, V_CB, V_MN, V_PE = 0, 16, 32, 40, 72, 80, 88
        ident, ones, rev = c("ident"), c("ones"), c("rev")
        headsel = c("headsel").rearrange("p (h x) -> p h x", h=MH)
        hq = T // P

        def sview(t, h):
            return uext[:, h, T + 3:UE].rearrange("p (b x) -> p b x", b=NB)

        def pslot(s, k, n):
            return slot[s][:, 0:k * n].rearrange("p (k n) -> p k n", k=k)

        def loaded(s, u, l):
            return 48 * (u + 1) + (80 * (l + 1) if s == 0 else 0)

        def mixer_in(l, j):
            return loaded(j % 3, 10 * l + j // 3, l)

        block = ctx.enter_context(nc.Block())

        @block.sync
        def _(sp):
            sp.dma_start(cset, a["const"][:, NKEEP:NCOL]).then_inc(s_setup.sem, 16)
            sp.dma_start(cst, a["const"][:, 0:NKEEP]).then_inc(s_setup.sem, 16)
            sp.dma_start(tab[0:NBUCKET, :], a["table"]).then_inc(s_setup.sem, 16)
            sp.dma_start(vrow[:, 0:P], a["vecs"][0:P, :]).then_inc(s_setup.sem, 16)
            sp.dma_start(vrow[0:24, P:2 * P], a["vecs"][P:152, :]).then_inc(s_setup.sem, 16)
            sp.dma_start(xtok[:, 0:2, :], a["x_prompt"].rearrange("b (m p) c -> p (b m) c", p=P)).then_inc(s_xin.sem, 16)
            sp.dma_start(xtok[0:NS, 2, :], a["x_sample"].rearrange("b t c -> (b t) c")).then_inc(s_xin.sem, 16)
            sp.dma_start(router[:, :, :], a["router"][0].rearrange("(k p) e -> p k e", p=P)).then_inc(s_xin.sem, 16)
            sp.dma_start(gbias[0:MH, 0:4], a["gate_bias"].rearrange("l i h -> h (l i)")).then_inc(s_xin.sem, 16)
            sp.wait_ge(w8_ev.sem, w8_ev.at(0))
            sp.dma_start(scr, w8[0:H, :]).then_inc(w8_st.sem, 16)
            sp.wait_ge(w8_st.sem, 16)
            for h in range(H):
                src = scr[h:h + 1, 4:4 + 384]
                src = bass.AP(src.tensor, src.offset, [[1, P], [1, 384]])
                sp.dma_start(Lh[:, h, :], src).then_inc(hank.sem, 16)

            def put(s, pieces):
                for dst, src in pieces:
                    sp.dma_start(dst, src).then_inc(wl[s].sem, 16)

            def split(dst, src, cuts):
                return [(dst[:, i:j, :], src[:, i:j, :]) for i, j in zip(cuts[:-1], cuts[1:])]

            def mixer_chunk(l, j):
                s = j % 3
                w = a["w_in"][l].rearrange("(k p) c -> p k c", p=P)
                cols = {0: (0, 512), 1: (OFF_KV, KV_HALF), 2: (OFF_KV + KV_HALF, KV_HALF), 3: (OFF_U, 512),
                        4: (OFF_O, 520)}
                if j in cols:
                    o, n = cols[j]
                    if j == 0:
                        dst = slot[0][:, 0:4096].rearrange("p (k g v d) -> p k g v d", k=KD, g=G, v=KVH)
                        src = w[:, :, 0:n].rearrange("p k (v g d) -> p k g v d", v=KVH, g=G)
                        put(s, [(dst[:, :, g, v, :], src[:, :, g, v, :]) for g in range(G) for v in range(KVH)])
                    else:
                        put(s, split(pslot(s, KD, n), w[:, :, o:o + n], (0, 3, 6, 8)))
                elif j == 5:
                    put(s, split(pslot(s, 32, P), a["cmp_w1"][l].rearrange("v (j p) e -> p (v j) e", p=P), (0, 11, 22, 32)))
                elif j == 6:
                    m = pslot(s, 13, P)
                    put(s, split(m, a["m_qkv"][l].rearrange("t h d e -> d (t h) e"), (0, 6, 12)))
                    put(s, [(m[:, 12, :].rearrange("p (v d) -> p v d", v=2), a["cmp_w2"][l].rearrange("v e d -> e v d"))])
                elif j in (7, 10):
                    o = 0 if j == 7 else 512
                    m = pslot(s, 8, 512)
                    ua = a["w_up_a"][l].rearrange("(v g d) c -> v d g c", v=KVH, g=G)
                    ub = a["w_up_b"][l].rearrange("(k p) c -> p k c", p=P)
                    put(s, [(m[0:64, 0:4, :], ua[0][:, :, o:o + 512]), (m[64:128, 0:4, :], ua[1][:, :, o:o + 512]),
                            (m[:, 4:8, :], ub[:, :, o:o + 512])])
                elif j in (8, 9, 11, 12):
                    o = {8: 0, 9: 256, 11: 512, 12: 768}[j]
                    m = pslot(s, 16, 256)
                    put(s, split(m[:, 0:8, :], w[:, :, OFF_GA + o:OFF_GA + o + 256], (0, 4, 8)))
                    put(s, [(m[:, 8:16, :], w[:, :, OFF_GB + o:OFF_GB + o + 256])])
                else:
                    o = 512 * (j - 13)
                    put(s, split(pslot(s, KD, 512), a["w_out"][l].rearrange("(k p) c -> p k c", p=P)[:, :, o:o + 512],
                                 (0, 3, 6, 8)))

            mixer_chunk(0, 0)
            mixer_chunk(0, 1)
            sp.wait_ge(bp_ev.sem, bp_ev.at(0))
            sp.wait_ge(vt_ev0.sem, vt_ev0.at(0))
            sp.wait_ge(hank.sem, 16 * H)
            mixer_chunk(0, 2)
            for l in range(2):
                freed = {3: (q_pe, 4), 4: (kv_pe, 3), 5: (kv_pe, 6), 6: (u_pe, 4), 7: (if_pe, 1), 8: (hid_pe, 2),
                         9: (vt_pe, 6), 10: (f_pe, 4), 11: (f_pe, 2), 12: (f_pe, 4), 13: (f_pe, 8), 14: (f_pe, 6)}
                for j in range(3, 15):
                    sp.wait_ge(freed[j][0].sem, freed[j][0].at(l, freed[j][1]))
                    mixer_chunk(l, j)
                if l == 0:
                    w1 = a["ffn_w1"][0].rearrange("(k p) f -> p k f", p=P)
                    w3 = a["ffn_w3"][0].rearrange("(k p) f -> p k f", p=P)
                    w2 = a["ffn_w2"][0].rearrange("(f p) d -> p f d", p=P)
                    for ch in range(15):
                        s = ch % 3
                        if ch == 0:
                            sp.wait_ge(f_pe.sem, f_pe.at(0, 8))
                        elif ch == 1:
                            sp.wait_ge(wo_pe.sem, wo_pe.at(0, 4))
                        elif ch == 2:
                            sp.wait_ge(wo_pe.sem, wo_pe.at(0, 8))
                        elif ch < 14:
                            sp.wait_ge(ff_pe.sem, ff_pe.at(0, 2 * (ch - 2)))
                        else:
                            sp.wait_ge(fy_pe.sem, fy_pe.at(0, 2))
                        if ch < FCH:
                            m = pslot(s, 16, 256)
                            put(s, [(m[:, 0:8, :], w1[:, :, 256 * ch:256 * ch + 256])])
                            put(s, split(m[:, 8:16, :], w3[:, :, 256 * ch:256 * ch + 256], (0, 4, 8)))
                        else:
                            o = 256 * (ch - FCH)
                            put(s, split(pslot(s, 22, 256), w2[:, :, o:o + 256], (0, 8, 16, 22)))
                    for j in range(3):
                        sp.wait_ge(fy_pe.sem, fy_pe.at(0, 4 + 2 * j))
                        mixer_chunk(1, j)
                else:
                    sp.wait_ge(f_pe.sem, f_pe.at(1, 8))
                    sp.wait_ge(wo_pe.sem, wo_pe.at(1, 8))
                    sp.wait_ge(items.sem, items.at(0))
                    n_items = sp.value_load(itemi[0:1, NITEM:NITEM + 1], min_val=1, max_val=NITEM)
                    with sp.Fori(0, n_items) as w:
                        e = sp.value_load(itemi[0:1, bass.ds(w, 1)], min_val=0, max_val=NE - 1)
                        w1 = a["moe_w1"][0, e].rearrange("(k p) f -> p k f", p=P)
                        w3 = a["moe_w3"][0, e].rearrange("(k p) f -> p k f", p=P)
                        w2 = a["moe_w2"][0, e].rearrange("(f p) d -> p f d", p=P)
                        for ch in range(FCH):
                            sp.wait_ge(mo_pe.sem, FCH * w + (ch - 2 + FCH if ch >= 3 else (10, 11, 9)[ch]))
                            s = ch % 3
                            m = pslot(s, 16, 256)
                            put(s, [(m[:, 0:8, :], w1[:, :, 256 * ch:256 * ch + 256]),
                                    (m[:, 8:16, :], w3[:, :, 256 * ch:256 * ch + 256]),
                                    (slot[s][:, 4096:6144].rearrange("p (f d) -> p f d", f=2), w2[:, 2 * ch:2 * ch + 2, :])])

        @block.tensor
        def _(pe):
            def mm(out, lhsT, rhs, start=True, stop=True):
                return nc.tensor.matmul(out, lhsT, rhs, start=start, stop=stop)

            def tr(out, x):
                k = x.shape[0]
                return nc.tensor.transpose(out, x, ident[0:k, 0:k])

            def norm(idx):
                pe.wait_ge(sq_ev.sem, sq_ev.at(idx))
                for k in range(KD):
                    i = mm(ps[:, 0, 0:N], ones, hT[:, k, :], k == 0, k == KD - 1)
                i.then_inc(ss_pe0.sem, 1)

            pe.wait_ge(s_setup.sem, 16 * 5)
            for i in range(2):
                m = mm(ps[0:H, i, 0:272], tab[0:NBUCKET, :], c("bucket")[0:NBUCKET, 272 * i:272 * i + 272])
            m.then_inc(w8_pe.sem, 1)
            tr(ps[:, 2, 0:P], vrow[:, 0:P])
            tr(ps[:, 2, P:P + 24], vrow[0:24, P:2 * P]).then_inc(vt_pe0.sem, 1)
            pe.wait_ge(w8_ev.sem, w8_ev.at(0))
            rs = c("rowsel").rearrange("p (t r) -> p t r", t=TS)
            for t in range(TS):
                mm(ps[:, 3, 0:PAST], rs[0:H, t, :], w8[0:H, 3 - t:3 - t + PAST], t == 0, t == TS - 1)
            for t in range(TS):
                new = w8[0:H, DIM0 - t:DIM0 - t + TS]
                new = bass.AP(new.tensor, new.offset, [new.ap[0], [0, NB], [1, TS]])
                mm(ps[:, 3, PAST:N], rs[0:H, t, :], new, t == 0, t == TS - 1)
            for t in range(TS):
                m = mm(ps[:, 3, N:N + NC_BLK], rs[0:H, t, :], w8[0:H, 34 - t:34 - t + 16 * 14 + 1:16], t == 0, t == TS - 1)
            m.then_inc(bp1_pe.sem, 1)
            pe.wait_ge(s_xin.sem, s_xin.at(0, 64))
            for k in range(KD):
                if k >= 4:
                    pe.wait_ge(xt_ev.sem, xt_ev.at(0, k - 3))
                b = 4 + k % 4
                for m in range(3):
                    i = tr(ps[:, b, m * P:m * P + ROWS[m]], xtok[0:ROWS[m], m, k * P:k * P + P])
                i.then_inc(xt_pe.sem, 1)
            pe.wait_ge(hank.sem, 16 * H)
            pe.wait_ge(xt_ev.sem, xt_ev.at(0, 8))
            for i in range(4):
                m = mm(ps[:, 4 + i, :], rev, Lh[:, 2 * i:2 * i + 2, 0:T])
            m.then_inc(bp1_pe.sem, 1)
            pe.wait_ge(bp_ev.sem, bp_ev.at(0, 1))
            for q in range(hq):
                m = mm(ps[:, 3, 256 * q:256 * q + 120], rev, Lh[:, :, 159 - P * q:159 - P * q + 225:16])
            m.then_inc(bp1_pe.sem, 1)

            for l in range(2):
                pe.wait_ge(cvp_in.sem, cvp_in.at(l))
                if l == 0:
                    pe.wait_ge(bp_ev.sem, bp_ev.at(0))
                    pe.wait_ge(vt_ev0.sem, vt_ev0.at(0))
                else:
                    pe.wait_ge(fy_ev.sem, fy_ev.at(0))
                for h in range(MH):
                    m = tr(ps[:, 1, h * 24:h * 24 + 24], cvp[0:24, h * P:h * P + P])
                m.then_inc(cv_pe.sem, 1)
                norm(2 * l)
                pe.wait_ge(h_ev.sem, h_ev.at(2 * l))
                pe.wait_ge(wl[0].sem, mixer_in(l, 0))
                w = pslot(0, KD, 512)
                for g in range(G):
                    if g == 1:
                        pe.wait_ge(cv_ev.sem, cv_ev.at(l))
                    for k in range(KD):
                        m = mm(ps[:, g, 0:N], w[:, k, g * P:g * P + P], hT[:, k, :], k == 0, k == KD - 1)
                    m.then_inc(q_pe.sem, 1)
                for f in range(2):
                    pe.wait_ge(wl[(1 + f) % 3].sem, mixer_in(l, 1 + f))
                    w = pslot(1 + f, KD, KV_HALF)
                    for m in range(3):
                        b = (4 + 3 * f + m) % 8
                        if b < 2:
                            pe.wait_ge(q_ev.sem, q_ev.at(l, b + 1))
                        for k in range(KD):
                            i = mm(ps[0:ROWS[m], b, 0:KV_HALF], hT[:, k, m * P:m * P + ROWS[m]], w[:, k, :], k == 0, k == KD - 1)
                        i.then_inc(kv_pe.sem, 1)
                pe.wait_ge(wl[0].sem, mixer_in(l, 3))
                w = pslot(0, KD, 512)
                for h in range(MH):
                    if h < 2:
                        pe.wait_ge(q_ev.sem, q_ev.at(l, 3 + h))
                    else:
                        pe.wait_ge(kv_ev.sem, kv_ev.at(l, h - 1))
                    for k in range(KD):
                        m = mm(ps[:, 2 + h, 0:N], w[:, k, h * P:h * P + P], hT[:, k, :], k == 0, k == KD - 1)
                    m.then_inc(u_pe.sem, 1)
                pe.wait_ge(wl[1].sem, mixer_in(l, 4))
                w = pslot(1, KD, 520)
                for h in range(MH):
                    pe.wait_ge(kv_ev.sem, kv_ev.at(l, 3 + h))
                    for k in range(KD):
                        m = mm(ps[:, (6 + h) % 8, 0:N], w[:, k, h * P:h * P + P], hT[:, k, :], k == 0, k == KD - 1)
                    m.then_inc(o_pe.sem, 1)
                for i in range(2):
                    pe.wait_ge(u_ev.sem, u_ev.at(l, i + 1))
                    for k in range(KD):
                        m = mm(ps[0:MH, 2 + i, 0:N], w[:, k, 512 + 4 * i:516 + 4 * i], hT[:, k, :], k == 0, k == KD - 1)
                m.then_inc(if_pe.sem, 1)
                pe.wait_ge(o_ev.sem, o_ev.at(l, 4))
                pe.wait_ge(kv_ev.sem, kv_ev.at(l, 6))
                for r in range(2):
                    for m in range(hq):
                        tr(ps[:, 0, r * T + m * P:r * T + m * P + P], kv[:, m, 256 + 256 * r:384 + 256 * r])
                for r in range(2):
                    m = tr(ps[:, 1, r * NS:r * NS + NS], kv[0:NS, 2, 256 + 256 * r:384 + 256 * r])
                m.then_inc(kt_pe.sem, 1)
                pe.wait_ge(wl[0].sem, mixer_in(l, 6))
                qkv = slot[0][:, 0:1536].rearrange("p (t h e) -> p t h e", t=3, h=MH)
                cw2 = slot[0][:, 1536:1664].rearrange("p (v d) -> p v d", v=2)
                pe.wait_ge(uc_a.sem, uc_a.at(l))
                for i in range(8):
                    if i < 2:
                        pe.wait_ge(u_ev.sem, u_ev.at(l, 3 + i))
                    elif i >= 4:
                        pe.wait_ge(mqk_ev.sem, mqk_ev.at(l, i - 3))
                    m = mm(ps[:, 4 + i % 4, 0:N], qkv[:, i // 4, i % 4, :], ucT[:, i % 4, :])
                    m.then_inc(mqk_pe.sem, 1)
                pe.wait_ge(cmp_in.sem, cmp_in.at(l))
                for s in range(9):
                    if s < 2:
                        pe.wait_ge(mqk_ev.sem, mqk_ev.at(l, 5 + s))
                    else:
                        taken = ct_a if s % 2 == 0 else ct_d
                        pe.wait_ge(taken.sem, taken.at(l, s // 2))
                    x = cmpN[:, s, :].rearrange("p (u x) -> p u x", u=4)
                    for v in range(2):
                        for h in range(KVH):
                            o = (v * KVH + h) * P
                            m = tr(ps[:, 4 + s % 2, o:o + P], x[:, v * KVH + h, :])
                    m.then_inc(ct_pe.sem, 1)
                pe.wait_ge(wl[2].sem, mixer_in(l, 5))
                cw1 = slot[2][:, 0:4096].rearrange("p (v j e) -> p v j e", v=2, j=16)
                pe.wait_ge(ct_a.sem, ct_a.at(l))
                pe.wait_ge(ct_d.sem, ct_d.at(l))
                for v in range(2):
                    pe.wait_ge(mqk_ev.sem, mqk_ev.at(l, 7 + v))
                    for j in range(16):
                        mm(ps[:, 6 + v, 0:270], cw1[:, v, j, :], kvT2[:, v, :, j:j + 8 * 14 + 1:8], j == 0, j == 15)
                    for j in range(16):
                        o = V_PE + (l * 2 + v) * 16 + j
                        m = mm(ps[:, 6 + v, 300:301], cw1[:, v, j, :], vT[:, o:o + 1], j == 0, j == 15)
                    m.then_inc(hid_pe.sem, 1)
                pe.wait_ge(hidr_ev.sem, hidr_ev.at(l))
                for h in range(KVH):
                    mm(ps[64 * h:64 * h + 64, 4, 0:144], cw2[:, 0, :], hid[:, 0, 9 * h:9 * h + 9, :])
                for h in range(KVH):
                    mm(ps[64 * h:64 * h + 64, 7, 0:64], hidr[:, h, :], cw2[:, 1, :])
                for h in range(KVH):
                    for b in range(NB):
                        m = mm(ps[0:16, 5 + h, b * 64:b * 64 + 64], hid[:, 1, 9 * h + b, :], cw2[:, 1, :])
                m.then_inc(kc_pe.sem, 1)
                pe.wait_ge(if_ev.sem, if_ev.at(l))
                pe.wait_ge(kc_a.sem, kc_a.at(l))
                for v in range(KVH):
                    for q in range(hq):
                        for g in range(G):
                            h = v * G + g
                            m = mm(ps[:, 2 + q, h * 16:h * 16 + NC_BLK], qT[64 * v:64 * v + 64, g, q * P:q * P + P],
                                   KcT[64 * v:64 * v + 64, 8, 0:NC_BLK])
                        if v == 1:
                            m.then_inc(cs_pe.sem, 1)
                    if v == 0:
                        pe.drain()
                for q in range(hq):
                    pe.wait_ge(cx_n.sem, cx_n.at(l, q + 1))
                    tr(ps[:, 2 + q, 0:P], pc[:, q, :]).then_inc(cx_t.sem, 1)

                def scores(i):
                    q, h = i // H, i % H
                    v, g, ext = h // G, h % G, (q + 1) * P
                    if i >= 2:
                        pe.wait_ge(sa_ev.sem, sa_ev.at(l, i - 1))
                    for r in range(2):
                        m = mm(ps[:, 4 + i % 2, r * T:r * T + ext], qT[64 * v:64 * v + 64, g, q * P:q * P + P],
                               kTp[64 * v:64 * v + 64, r, 0:ext])
                    m.then_inc(s_pe.sem, 1)

                def turn(i):
                    q = i // H
                    pe.wait_ge(p_ev.sem, p_ev.at(l, i + 1))
                    if i >= 2:
                        pe.wait_ge(pt_ev.sem, pt_ev.at(l, i - 1))
                    for r in range(2):
                        for k in range(q + 1):
                            m = tr(ps[:, 6 + i % 2, (2 * r + k) * P:(2 * r + k + 1) * P], Pb[:, i % 2, r, k * P:k * P + P])
                    m.then_inc(t_pe.sem, 1)

                def values(i):
                    q, h = i // H, i % H
                    v, g = h // G, h % G
                    o = ps[64 * v:64 * v + 64, q, g * P:g * P + P]
                    if h == 0:
                        pe.wait_ge(pct_ev.sem, pct_ev.at(l, q + 1))
                    pe.wait_ge(pt_ev.sem, pt_ev.at(l, i + 1))
                    mm(o, VcZ[:, h, :], PcT[:, q, :], True, False)
                    for r in range(2):
                        for k in range(q + 1):
                            x = 384 + 256 * r + 64 * v
                            m = mm(o, kv[:, k, x:x + 64], PT[:, i % 2, r, k, :], False, r == 1 and k == q)
                    m.then_inc(pv_pe.sem, 1)

                pe.wait_ge(kt_ev.sem, kt_ev.at(l))
                pe.wait_ge(kc_d.sem, kc_d.at(l))
                for i in range(18):
                    if i < 16:
                        scores(i)
                    if 1 <= i < 17:
                        turn(i - 1)
                    if i >= 2:
                        values(i - 2)

                pe.wait_ge(qz_ev.sem, qz_ev.at(l))
                for t in range(2):
                    pe.wait_ge(sw_in.sem, sw_in.at(l, 144 * (t + 1)))
                    for i in range(16):
                        r, b, g = i // 8, (i // 2) % 4, i % 2
                        if i == 0:
                            pe.wait_ge(pct_ev.sem, pct_ev.at(l))
                            if t == 1:
                                pe.wait_ge(son_ev.sem, son_ev.at(l, 1))
                        if i == 8:
                            pe.wait_ge(sa_ev.sem, sa_ev.at(l))
                        m = tr(ps[:, 2 + i // 4, (i % 4) * P:(i % 4) * P + P], sw[:, r, b, g, 0:P])
                        if i % 4 == 3:
                            m.then_inc(skt_pe.sem, 1)
                    pe.wait_ge(skt_a.sem, skt_a.at(l, 2 * t + 2))
                    pe.wait_ge(skt_d.sem, skt_d.at(l, 2 * t + 2))
                    if t == 0:
                        pe.wait_ge(pt_ev.sem, pt_ev.at(l))
                    else:
                        pe.wait_ge(sadd.sem, sadd.at(l, 1))
                    for r in range(2):
                        for b in range(4):
                            qz = Qz[:, t, 32 * b:32 * b + 32]
                            mm(ps[32 * b:32 * b + 32, 6 + r, 0:PAST], qz, kTs[:, r, b, :])
                            if r == 1:
                                mm(ps[32 * b:32 * b + 32, 7, N:N + NC_BLK], qz, KcT[:, 4 * t + b, 0:NC_BLK])
                        m = mm(ps[:, 6 + r, PAST:N], Qz[:, t, :], kTn[:, r, :])
                    m.then_inc(ss_pe.sem, 1)
                    pe.wait_ge(sps_ev.sem, sps_ev.at(l, t + 1))
                    if t == 0:
                        pe.wait_ge(on_ev.sem, on_ev.at(l))
                    for r in range(2):
                        for g in range(2):
                            tr(ps[:, 0, (2 * r + g) * P:(2 * r + g + 1) * P], Ps[:, r, g * P:g * P + P])
                        tr(ps[0:NS, 1, r * P:r * P + P], Ps[:, r, PAST:N])
                    tr(ps[0:16, 1, 2 * P:3 * P], Psc[:, :]).then_inc(st_pe.sem, 1)
                    pe.wait_ge(spt_ev.sem, spt_ev.at(l, t + 1))
                    for b in range(4):
                        o, cc = ps[:, 2, 32 * b:32 * b + 32], slice(32 * b, 32 * b + 32)
                        mm(o, VcS[0:16, 4 * t + b, :], PTn[0:16, 2 * P + 32 * b:2 * P + 32 * b + 32], True, False)
                        for r in range(2):
                            for g in range(2):
                                mm(o, sw[:, r, b, g, P:2 * P], PT[:, 0, r, g, cc], False, False)
                            x = 384 + 256 * r
                            m = mm(o, kv[0:NS, 2, x:x + P], PTn[0:NS, r * P + 32 * b:r * P + 32 * b + 32], False, r == 1)
                    m.then_inc(spv_pe.sem, 1)

                pe.wait_ge(row_a.sem, row_a.at(l))
                for m in range(3):
                    i = tr(ps[0:ROWS[m], 6, m * P:m * P + P], R[:, m * P:m * P + ROWS[m]])
                for h in range(MH):
                    mm(ps[:, 7, h * NB:h * NB + NB], headsel[0:MH, h, :], R[0:MH, T + TS - 1:N:TS])
                pe.wait_ge(n0_in.sem, n0_in.at(l))
                tr(ps[:, 7, 64:96], nld[0:NS, :]).then_inc(rt_pe.sem, 1)
                pe.wait_ge(spt_ev.sem, spt_ev.at(l))
                pe.wait_ge(son_ev.sem, son_ev.at(l))
                for kind in range(2):
                    for m in range(3):
                        for h in range(MH):
                            if kind == 0:
                                x = uext[:, h, 3 + m * P:3 + m * P + P] if m < 2 else us[:, h, :]
                            else:
                                x = ucT[:, h, m * P:m * P + ROWS[m]]
                            i = mm(ps[0:ROWS[m], 3 * kind + m, h * P:h * P + P], x, qkv[:, 2 - kind, h, :])
                        i.then_inc(vt_pe.sem, 1)
                pe.wait_ge(rt_ev.sem, rt_ev.at(l))
                pe.wait_ge(wcb_ev.sem, wcb_ev.at(l))
                pe.wait_ge(vt_ev.sem, vt_ev.at(l))
                pe.wait_ge(ktk_ev.sem, ktk_ev.at(l))

                def gates(h):
                    if h >= 1:
                        pe.wait_ge(md_ev.sem, md_ev.at(l, h))
                        pe.wait_ge(ma_ev.sem, ma_ev.at(l, h))
                    mm(ps[:, 6, 0:N], headsel[0:MH, h, :], Mrow[0:MH, :])
                    mm(ps[:, 7, 0:T], mkT[:, h, 0:P], mqT[:, h, 0:T])
                    mm(ps[:, 7, T:T + P], mkT[:, h, P:T], mqT[:, h, P:T])
                    mm(ps[0:NS, 7, 384:416], mkT[:, h, T:N], mqT[:, h, T:N]).then_inc(mb_pe.sem, 1)

                gates(0)
                pe.wait_ge(c0_in.sem, c0_in.at(l))
                pe.wait_ge(mz_ev.sem, mz_ev.at(l))
                for h in range(MH):
                    pe.wait_ge(ma_ev.sem, ma_ev.at(l, h + 1))
                    if h >= 1:
                        pe.wait_ge(mh_ev.sem, mh_ev.at(l, h))
                    mm(ps[:, 0, 0:129], Ab[:, 0:P], mv[:, 0, h, :])
                    mm(ps[:, 0, 129:258], Ab[:, P:T], mv[:, 0, h, :], True, False)
                    mm(ps[:, 0, 129:258], Ab[:, T:T + P], mv[:, 1, h, :], False, True)
                    mm(ps[0:NS, 1, 0:129], Ab[0:NS, 384:416], mv[0:NS, 2, h, :])
                    for b in range(NB):
                        m = mm(ps[0:NS, 1, 129:258], mqz[:, h, b, :], C0[:, b, h, :], b == 0, b == NB - 1)
                    m.then_inc(num_pe.sem, 1)
                    if h + 1 < MH:
                        gates(h + 1)
                for h in range(MH):
                    o = ps[:, 3 + h // 3, (h % 3) * 129:(h % 3) * 129 + 129]
                    mm(o, mk[:, 0, h, :], mv[:, 0, h, :], True, False)
                    m = mm(o, mk[:, 1, h, :], mv[:, 1, h, :], False, True)
                m.then_inc(cp_pe.sem, 1)
                pe.wait_ge(ma_ev.sem, ma_ev.at(l))
                for h in range(MH):
                    pe.wait_ge(vz_ev.sem, vz_ev.at(l, h + 1))
                    if h >= 1:
                        pe.wait_ge(cn_ev.sem, cn_ev.at(l, h))
                    for i, (b0, b1) in enumerate(((0, 3), (3, 6), (6, 8))):
                        m = mm(ps[:, 5 + i, 0:129 * (b1 - b0)], mk[0:NS, 2, h, :], mvz[0:NS, b0:b1, :])
                    m.then_inc(cn_pe.sem, 1)
                pe.wait_ge(hn_ev.sem, hn_ev.at(l))
                pe.wait_ge(mh_ev.sem, mh_ev.at(l))
                pe.wait_ge(cp_ev.sem, cp_ev.at(l))
                for h in range(MH):
                    for m in range(3):
                        i = tr(ps[:, h, m * P:m * P + ROWS[m]], hm[0:ROWS[m], m, h, :])
                    i.then_inc(om_pe.sem, 1)
                pe.wait_ge(cn_ev.sem, cn_ev.at(l))
                tr(ps[0:NS, 4, 0:P], C0[:, :, :, 128:129].rearrange("p b h e -> p (b h e)"))
                tr(ps[0:MH, 4, P:2 * P], Cp[:, :, 128:129].rearrange("p h e -> p (h e)"))
                for h in range(MH):
                    m = tr(ps[0:27, 5, h * P:h * P + P], cstage[:, h, :])
                m.then_inc(no_pe.sem, 1)

                pe.wait_ge(wl[1].sem, mixer_in(l, 7))
                pe.wait_ge(om_ev.sem, om_ev.at(l))
                pe.wait_ge(son_ev.sem, son_ev.at(l))
                pe.wait_ge(no_ev.sem, no_ev.at(l))
                for d in range(8):
                    ju, jg = (7, 10)[d // 4], (8, 9, 11, 12)[d // 2]
                    pe.wait_ge(wl[ju % 3].sem, mixer_in(l, ju))
                    pe.wait_ge(wl[jg % 3].sem, mixer_in(l, jg))
                    up = pslot(ju % 3, 8, 512)[:, :, (d % 4) * P:(d % 4) * P + P]
                    wg = pslot(jg % 3, 16, 256)[:, :, (d % 2) * P:(d % 2) * P + P]
                    b = 4 * (d % 2)
                    if d >= 2:
                        pe.wait_ge(f_ev.sem, f_ev.at(l, d - 1))
                    for x in range(2):
                        for k in range(KD):
                            mm(ps[:, b + x, 0:N], wg[:, 8 * x + k, :], hT[:, k, :], k == 0, k == KD - 1)
                    for x in range(2):
                        src = (oNT, omT)[x]
                        for k in range(4):
                            m = mm(ps[:, b + 2 + x, 0:N], up[:, 4 * x + k, :], src[:, k, :], k == 0, k == 3)
                    m.then_inc(f_pe.sem, 1)
                pe.wait_ge(f_ev.sem, f_ev.at(l))
                for d in range(8):
                    pe.wait_ge(wl[(13 + d // 4) % 3].sem, mixer_in(l, 13 + d // 4))
                    w = pslot((13 + d // 4) % 3, KD, 512)
                    if d >= 4:
                        pe.wait_ge(wo_ev.sem, wo_ev.at(l, d - 3))
                    for k in range(KD):
                        m = mm(ps[:, d % 4, 0:N], w[:, k, (d % 4) * P:(d % 4) * P + P], merged[:, k, :], k == 0, k == KD - 1)
                    m.then_inc(wo_pe.sem, 1)

                if l == 0:
                    norm(1)
                    pe.wait_ge(h_ev.sem, h_ev.at(1))
                    for f in range(22):
                        if f % 2 == 0:
                            pe.wait_ge(wl[(f // 2) % 3].sem, loaded((f // 2) % 3, 5 + f // 6, 0))
                        w = pslot((f // 2) % 3, 16, 256)[:, :, (f % 2) * P:(f % 2) * P + P]
                        b = 1 + 2 * (f % 3)
                        if f >= 3:
                            pe.wait_ge(ff_g.sem, ff_g.at(0, f - 2))
                        for x in range(2):
                            for k in range(KD):
                                m = mm(ps[:, b + x, 0:N], w[:, 8 * x + k, :], hT[:, k, :], k == 0, k == KD - 1)
                        m.then_inc(ff_pe.sem, 1)
                    pe.wait_ge(ff_g.sem, ff_g.at(0))
                    for d in range(8):
                        ch = FCH + d // 2
                        if d % 2 == 0:
                            pe.wait_ge(wl[ch % 3].sem, loaded(ch % 3, 5 + ch // 3, 0))
                        w = pslot(ch % 3, 22, 256)[:, :, (d % 2) * P:(d % 2) * P + P]
                        if d >= 4:
                            pe.wait_ge(fy_ev.sem, fy_ev.at(0, d - 3))
                        for f in range(22):
                            m = mm(ps[:, d % 4, 0:N], w[:, f, :], gT[:, f, :], f == 0, f == 21)
                        m.then_inc(fy_pe.sem, 1)
                elif MOE:
                    norm(3)
                    pe.wait_ge(h_ev.sem, h_ev.at(3))
                    for m in range(3):
                        n = ROWS[m]
                        for k in range(KD):
                            tr(ps[0:n, 2 + 2 * m + k // 4, (k % 4) * P:(k % 4) * P + P], hT[:, k, m * P:m * P + n])
                        for k in range(KD):
                            i = mm(ps[0:n, 1, 8 * m:8 * m + NE], hT[:, k, m * P:m * P + n], router[:, k, :], k == 0, k == KD - 1)
                    i.then_inc(lg_pe.sem, 1)
                    pe.wait_ge(sel_d.sem, sel_d.at(0))
                    for m in range(3):
                        n = ROWS[m]
                        for j in range(m):
                            mm(ps[0:n, 1, 64 + 8 * m:72 + 8 * m], ones[:, 0:n], sel[:, j, :], j == 0, False)
                        mm(ps[0:n, 1, 64 + 8 * m:72 + 8 * m], c("tri")[0:n, 0:n], sel[0:n, m, :], m == 0, True)
                    for m in range(3):
                        i = mm(ps[0:NE, 1, 96:97], sel[0:ROWS[m], m, :], ones[0:ROWS[m], 0:1], m == 0, m == 2)
                    i.then_inc(pos_pe.sem, 1)
                    pe.wait_ge(pos_d.sem, pos_d.at(0))
                    mm(ps[0:NE, 1, 100:101], c("etri")[0:NE, :], nblk[0:NE, :]).then_inc(nb_pe.sem, 1)
                    pe.wait_ge(h2_ev.sem, h2_ev.at(0))
                    for m in range(3):
                        n = ROWS[m]
                        tr(ps[0:NE, 2, m * P:m * P + n], posm[0:n, m, :])
                        i = tr(ps[0:NE, 3, m * P:m * P + n], gate[0:n, m, :])
                    i.then_inc(tp_pe.sem, 1)
                    pe.wait_ge(tp_ev.sem, tp_ev.at(0))
                    pe.wait_ge(nb_d.sem, nb_d.at(0))
                    for m in range(3):
                        n = ROWS[m]
                        mm(ps[0:n, 4, 16 * m:16 * m + NITEM], posT[0:NE, m * P:m * P + n], Mw[0:NE, :], True, False)
                        mm(ps[0:n, 4, 16 * m:16 * m + NITEM], ones[0:NE, 0:n], off[0:NE, :], False, True)
                        mm(ps[0:n, 4, 64 + 16 * m:64 + 16 * m + NITEM], gateT[0:NE, m * P:m * P + n], Mw[0:NE, :])
                    mm(ps[0:1, 4, 128:128 + NITEM], c("eidx")[0:NE, :], Mw[0:NE, :])
                    mm(ps[0:1, 4, 128 + NITEM:129 + NITEM], nblk[0:NE, :], ones[0:NE, 0:1]).then_inc(it_pe.sem, 1)
                    pe.wait_ge(items.sem, items.at(0))
                    pe.sem_inc(mo_pe.sem, FCH)
                    n_items = pe.value_load(itemi[0:1, NITEM:NITEM + 1], min_val=1, max_val=NITEM)
                    with pe.Fori(0, n_items) as w:
                        pe.wait_ge(g_sel.sem, w + 1)
                        pe.wait_ge(cmb_ev.sem, 8 * w + 8)
                        for k in range(KD):
                            for m in range(3):
                                n = ROWS[m]
                                mm(ps[:, k // 4, (k % 4) * P:(k % 4) * P + P], h2[0:n, m, k * P:k * P + P], Sel[0:n, m, :],
                                   m == 0, m == 2)
                        for m in range(3):
                            n = ROWS[m]
                            i = tr(ps[:, 5, m * P:m * P + n], SelG[0:n, m, :])
                        i.then_inc(g_pe.sem, 1)
                        pe.wait_ge(g_ev.sem, w + 1)

                        def out_products(ch):
                            w2 = slot[ch % 3][:, 4096:6144].rearrange("p (f d) -> p f d", f=2)
                            pe.wait_ge(m_gT.sem, FCH * w + ch + 1)
                            for f in range(2):
                                for x in range(2):
                                    i = mm(ps[:, 6 + x, :], gTm[:, ch % 2, f, :], w2[:, f, 512 * x:512 * x + 512],
                                           ch == 0 and f == 0, ch == FCH - 1 and f == 1)
                            i.then_inc(mo_pe.sem, 1)

                        for ch in range(FCH):
                            s = ch % 3
                            before = 48 * 15 + (160 if s == 0 else 0)
                            pe.wait_ge(wl[s].sem, w * (48 * (4, 4, 3)[s]) + before + 48 * (ch // 3 + 1))
                            m = pslot(s, 16, 256)
                            if ch >= 2:
                                pe.wait_ge(m_g.sem, FCH * w + ch - 1)
                            for x in range(2):
                                for k in range(KD):
                                    i = mm(ps[:, 2 + ch % 2, 256 * x:256 * x + 256], Xg[:, k, :], m[:, 8 * x + k, :],
                                           k == 0, k == KD - 1)
                            i.then_inc(m_h.sem, 1)
                            if ch >= 1:
                                out_products(ch - 1)
                            pe.wait_ge(m_g.sem, FCH * w + ch + 1)
                            for f in range(2):
                                i = tr(ps[:, 4 + ch % 2, f * P:f * P + P], gm[:, ch % 2, f * P:f * P + P])
                            i.then_inc(m_t.sem, 1)
                        out_products(FCH - 1)
                        pe.wait_ge(yS_ev.sem, w + 1)
                        for d in range(KD):
                            if d >= 4:
                                pe.wait_ge(cmb_ev.sem, 8 * w + 8 + d - 3)
                            mm(ps[:, d % 4, 0:N], yS[:, d * P:d * P + P], SelT[:, :]).then_inc(cmb_pe.sem, 1)
                    pe.wait_ge(cmb_ev.sem, 8 * n_items + 8)
            norm(3 + MOE)
            pe.wait_ge(h_ev.sem, h_ev.at(3 + MOE))
            for k in range(KD):
                b = 2 + 2 * (k // 4)
                for m in range(3):
                    i = tr(ps[0:ROWS[m], 1 + 2 * m + k // 4, (k % 4) * P:(k % 4) * P + P], hT[:, k, m * P:m * P + ROWS[m]])
            i.then_inc(y_pe.sem, 1)

        @block.scalar
        def _(act):
            def fn(out, x, f, **kw):
                return nc.scalar.activation(out, x, f, **kw)

            def copy(out, x, scale=1.0):
                return nc.scalar.activation(out, x, ACT.Copy, scale=scale)

            def norm(idx):
                act.wait_ge(x_done.sem, x_done.at(idx))
                fn(hT[:, :, :], xT[:, :, :], ACT.Square).then_inc(sq_ev.sem, 1)
                act.wait_ge(var_ev.sem, var_ev.at(idx))
                fn(srow, srow, ACT.Sqrt).then_inc(sd_ev.sem, 1)

            act.wait_ge(vt_pe0.sem, vt_pe0.at(0))
            copy(vT, ps[:, 2, 0:152]).then_inc(vt_ev0.sem, 1)
            for k in range(KD):
                act.wait_ge(xt_pe.sem, xt_pe.at(0, k + 1))
                copy(xT[:, k, :], ps[:, 4 + k % 4, 0:N]).then_inc(xt_ev.sem, 1)

            for l in range(2):
                act.wait_ge(cv_pe.sem, cv_pe.at(l))
                copy(uext[:, :, T + 3:UE].rearrange("p h (b x) -> p h b x", b=NB)[:, :, :, 0:3],
                     ps[:, 1, 0:96].rearrange("p (h b x) -> p h b x", h=MH, b=NB)).then_inc(cv_ev.sem, 1)
                norm(2 * l)
                for g in range(G):
                    act.wait_ge(q_pe.sem, q_pe.at(l, g + 1))
                    copy(qT[:, g, :], ps[:, g, 0:N], HD ** -0.5).then_inc(q_ev.sem, 1)
                act.wait_ge(kv_ev.sem, kv_ev.at(l))
                fn(gns[:, 0:2, :], kv[:, 0:2, 768:792], ACT.Sigmoid)
                fn(gns[0:NS, 2, :], kv[0:NS, 2, 768:792], ACT.Sigmoid).then_inc(gs_ev.sem, 1)
                for h in range(MH):
                    act.wait_ge(o_pe.sem, o_pe.at(l, h + 1))
                    fn(oT[:, h, :], ps[:, (6 + h) % 8, 0:N], ACT.Sigmoid).then_inc(o_ev.sem, 1)
                act.wait_ge(kt_pe.sem, kt_pe.at(l))
                copy(kTp[:, :, :], ps[:, 0, :].rearrange("p (r x) -> p r x", r=2))
                copy(kTn[:, :, :], ps[:, 1, 0:64].rearrange("p (r x) -> p r x", r=2)).then_inc(kt_ev.sem, 1)
                act.wait_ge(uc_d.sem, uc_d.at(l))
                fn(ucT[:, :, :], ucT[:, :, :], ACT.Silu).then_inc(uc_a.sem, 1)
                for i in range(8):
                    act.wait_ge(mqk_pe.sem, mqk_pe.at(l, i + 1))
                    dst = (mqT, mkT)[i // 4][:, i % 4, :]
                    copy(dst, ps[:, 4 + i % 4, 0:N], (MD ** -0.5, 1.0)[i // 4]).then_inc(mqk_ev.sem, 1)
                kvu = take(4 * 9 * P, Y_at).rearrange("p (u s x) -> p u s x", u=4, s=9)
                for s in range(0, 9, 2):
                    act.wait_ge(ct_pe.sem, ct_pe.at(l, s + 1))
                    copy(kvu[:, :, s, :], ps[:, 4, :].rearrange("p (u x) -> p u x", u=4)).then_inc(ct_a.sem, 1)
                for v in range(2):
                    act.wait_ge(c_ev.sem, c_ev.at(l, v + 1))
                    fn(hid[:, v, :, 0:NC_BLK], ps[:, 6 + v, 0:270].rearrange("p (s x) -> p s x", s=18),
                       ACT.Gelu_apprx_tanh, bias=cvec[:, v:v + 1]).then_inc(hid_ev.sem, 1)
                act.wait_ge(kc_pe.sem, kc_pe.at(l))
                copy(KcT[:, :, :], ps[:, 4, 0:144].rearrange("p (s x) -> p s x", s=9))
                for h in range(KVH):
                    i = copy(VcS[0:16, :, 64 * h:64 * h + 64], ps[0:16, 5 + h, :].rearrange("p (b d) -> p b d", b=NB))
                i.then_inc(kc_a.sem, 1)
                for q in range(hq):
                    act.wait_ge(cx_d.sem, cx_d.at(l, q + 1))
                    x = pc[:, q, :].rearrange("p (h n) -> p h n", h=H)[:, :, 0:NC_BLK]
                    fn(x, x, ACT.Exp).then_inc(cx_a.sem, 1)
                for q in range(hq):
                    act.wait_ge(cx_t.sem, cx_t.at(l, q + 1))
                    copy(PcT[:, q, :], ps[:, 2 + q, 0:P]).then_inc(pct_ev.sem, 1)
                for i in range(17):
                    if i < 16:
                        ext = (i // H + 1) * P
                        act.wait_ge(nm_ev.sem, nm_ev.at(l, i + 1))
                        for r in range(2):
                            x = Pb[:, i % 2, r, 0:ext]
                            e = fn(x, x, ACT.Exp, bias=nm[:, i % 2, r:r + 1], accum_out=sums[:, i % 2, r:r + 1])
                        e.then_inc(ex_ev.sem, 1)
                    if i >= 1:
                        j = i - 1
                        w = (j // H + 1) * P
                        act.wait_ge(t_pe.sem, t_pe.at(l, j + 1))
                        if j >= 2:
                            act.wait_ge(pv_pe.sem, pv_pe.at(l, j - 1))
                        copy(PT[:, j % 2, :, 0:j // H + 1, :],
                             ps[:, 6 + j % 2, :].rearrange("p (r k x) -> p r k x", r=2, k=2)[:, :, 0:j // H + 1, :]
                             ).then_inc(pt_ev.sem, 1)
                for q in range(hq):
                    act.wait_ge(pv_pe.sem, pv_pe.at(l, H * (q + 1)))
                    copy(oNT[:, :, q * P:q * P + P], ps[:, q, :].rearrange("p (g x) -> p g x", g=G)).then_inc(on_ev.sem, 1)
                for t in range(2):
                    for i in range(2):
                        act.wait_ge(skt_pe.sem, skt_pe.at(l, 4 * t + i + 1))
                        copy(kTs[:, 0, 2 * i:2 * i + 2, :], ps[:, 2 + i, :].rearrange("p (b x) -> p b x", b=2)
                             ).then_inc(skt_a.sem, 1)
                    act.wait_ge(snm_ev.sem, snm_ev.at(l, t + 1))
                    fn(Psc[:, 0:NC_BLK], Psc[:, 0:NC_BLK], ACT.Exp, bias=snm[:, 0:1], accum_out=ssm[:, 0:1])
                    for r in range(2):
                        e = fn(Ps[:, r, :], Ps[:, r, :], ACT.Exp, bias=snm[:, 1 + r:2 + r], accum_out=ssm[:, 1 + r:2 + r])
                    e.then_inc(sex_ev.sem, 1)
                    act.wait_ge(st_pe.sem, st_pe.at(l, t + 1))
                    copy(PT[:, 0, :, :, :], ps[:, 0, :].rearrange("p (r k x) -> p r k x", r=2, k=2))
                    copy(PTn[0:NS, 0:2 * P], ps[0:NS, 1, 0:2 * P])
                    copy(PTn[0:16, 2 * P:3 * P], ps[0:16, 1, 2 * P:3 * P]).then_inc(spt_ev.sem, 1)
                act.wait_ge(lf_d.sem, lf_d.at(l))
                fn(rows[0:MH, 1, :], rows[0:MH, 1, :], ACT.Exp, scale=-1.0).then_inc(lf_a.sem, 1)
                act.wait_ge(lf_d2.sem, lf_d2.at(l))
                fn(rows[0:MH, 1, :], rows[0:MH, 1, :], ACT.Ln).then_inc(lf_a2.sem, 1)
                act.wait_ge(row_d.sem, row_d.at(l))
                fn(R[0:MH, :], rows[0:MH, 7, :], ACT.Exp)
                copy(R[32:32 + MH, :], rows[0:MH, 3, :])
                fn(R[64:64 + MH, :], rows[0:MH, 6, :], ACT.Exp, scale=-1.0)
                copy(mout[0:MH, :], rows[0:MH, 6, T - 1:N:TS])
                fn(R[96:96 + MH, :], rows[0:MH, 8, :], ACT.Exp).then_inc(row_a.sem, 1)
                act.wait_ge(rt_pe.sem, rt_pe.at(l))
                copy(RT[:, 0:2, :], ps[:, 6, 0:2 * P].rearrange("p (m x) -> p m x", m=2))
                copy(RT[0:NS, 2, :], ps[0:NS, 6, 2 * P:3 * P]).then_inc(rt_ev.sem, 1)
                copy(wcb[:, :, :], ps[:, 7, 0:NS].rearrange("p (h b) -> p h b", h=MH))
                copy(C0[:, :, :, 128], ps[:, 7, 64:96].rearrange("p (b h) -> p b h", b=NB)).then_inc(wcb_ev.sem, 1)
                for m in range(3):
                    act.wait_ge(vt_pe.sem, vt_pe.at(l, m + 1))
                    n = ROWS[m]
                    copy(mv[0:n, m, :, 0:MD], ps[0:n, m, :].rearrange("p (h e) -> p h e", h=MH)).then_inc(vt_ev.sem, 1)
                for h in range(MH):
                    act.wait_ge(md_ev.sem, md_ev.at(l, h + 1))
                    fn(Db[:, 0:T], Db[:, 0:T], ACT.Exp, scale=-1.0, bias=RT[:, 0, 32 + h:33 + h])
                    fn(Db[:, T:T + P], Db[:, T:T + P], ACT.Exp, scale=-1.0, bias=RT[:, 1, 32 + h:33 + h])
                    fn(Db[0:NS, 384:416], Db[0:NS, 384:416], ACT.Exp, scale=-1.0, bias=RT[0:NS, 2, 32 + h:33 + h]
                       ).then_inc(me_ev.sem, 1)
                act.wait_ge(cp_pe.sem, cp_pe.at(l))
                copy(Cp[:, 0:3, :], ps[:, 3, 0:387].rearrange("p (h e) -> p h e", h=3))
                copy(Cp[:, 3, :], ps[:, 4, 0:129]).then_inc(cp_ev.sem, 1)
                act.wait_ge(var2_ev.sem, var2_ev.at(l))
                fn(ssr[:, :, :], ssr[:, :, :], ACT.Sqrt).then_inc(sd2_ev.sem, 1)
                act.wait_ge(no_pe.sem, no_pe.at(l))
                copy(nout[0:NS, 0:P], ps[0:NS, 4, 0:P])
                copy(nout[0:MH, P:2 * P], ps[0:MH, 4, P:2 * P])
                copy(cvo[0:27, :], ps[0:27, 5, :]).then_inc(no_ev.sem, 1)
                for d in range(8):
                    act.wait_ge(f_pe.sem, f_pe.at(l, d + 1))
                    b = 4 * (d % 2)
                    fn(fsig[:, d % 2, 0, :], ps[:, b, 0:N], ACT.Sigmoid)
                    fn(fsig[:, d % 2, 1, :], ps[:, b + 1, 0:N], ACT.Sigmoid).then_inc(f_sig.sem, 1)
                if l == 0:
                    norm(1)
                    act.wait_ge(st_state.sem, st_state.at(0))
                    for f in range(22):
                        act.wait_ge(ff_pe.sem, ff_pe.at(0, f + 1))
                        if f >= 2:
                            act.wait_ge(ff_g.sem, ff_g.at(0, f - 1))
                        fn(sil[:, f % 2, 0, :], ps[:, 1 + 2 * (f % 3), 0:N], ACT.Silu).then_inc(ff_sil.sem, 1)
                elif MOE:
                    norm(3)
                    act.wait_ge(lg_pe.sem, lg_pe.at(0))
                    act.wait_ge(st_kv.sem, st_kv.at(1))
                    for m in range(3):
                        n = ROWS[m]
                        i = copy(h2[0:n, m, :].rearrange("p (b x) -> p b x", b=2), ps[0:n, 2 + 2 * m:4 + 2 * m, :])
                    i.then_inc(h2_ev.sem, 1)
                    act.wait_ge(lgx_d.sem, lgx_d.at(0))
                    fn(gx[:, :, :], gx[:, :, :], ACT.Exp).then_inc(lgx_a.sem, 1)
                    act.wait_ge(tp_pe.sem, tp_pe.at(0))
                    copy(posT[0:NE, :], ps[0:NE, 2, 0:N])
                    copy(gateT[0:NE, :], ps[0:NE, 3, 0:N]).then_inc(tp_ev.sem, 1)
                    act.wait_ge(items.sem, items.at(0))
                    n_items = act.value_load(itemi[0:1, NITEM:NITEM + 1], min_val=1, max_val=NITEM)
                    with act.Fori(0, n_items) as w:
                        act.wait_ge(g_pe.sem, w + 1)
                        copy(Xg[:, :, :].rearrange("p (b k) s -> p b (k s)", b=2), ps[:, 0:2, :])
                        copy(SelT[:, :], ps[:, 5, 0:N]).then_inc(g_ev.sem, 1)
                        for ch in range(FCH):
                            act.wait_ge(m_h.sem, FCH * w + ch + 1)
                            if ch >= 2:
                                act.wait_ge(m_g.sem, FCH * w + ch - 1)
                            fn(sl[:, ch % 2, :], ps[:, 2 + ch % 2, 0:256], ACT.Silu).then_inc(m_sil.sem, 1)
                            act.wait_ge(m_t.sem, FCH * w + ch + 1)
                            if ch >= 2:
                                act.wait_ge(mo_pe.sem, FCH * w + FCH + ch - 1)
                            copy(gTm[:, ch % 2, :, :], ps[:, 4 + ch % 2, 0:256].rearrange("p (f x) -> p f x", f=2)
                                 ).then_inc(m_gT.sem, 1)
                        act.wait_ge(mo_pe.sem, FCH * w + 2 * FCH)
                        copy(yS[:, :].rearrange("p (b x) -> p b x", b=2), ps[:, 6:8, :]).then_inc(yS_ev.sem, 1)
            norm(3 + MOE)
            act.wait_ge(y_pe.sem, y_pe.at(0))
            for m in range(3):
                n = ROWS[m]
                e = copy(ytok[0:n, m, :].rearrange("p (b x) -> p b x", b=2), ps[0:n, 1 + 2 * m:3 + 2 * m, :])
            e.then_inc(y_ev.sem, 1)

        @block.vector
        def _(dve):
            V = nc.vector

            def tt(out, x, y, op):
                return V.tensor_tensor(out, x, y, op)

            def bc(x, n):
                return bass.AP(x.tensor, x.offset, list(x.ap[:-1]) + [[0, n]]) if x.ap[-1][1] == 1 else x

            def rep(x, n):
                return bass.AP(x.tensor, x.offset, list(x.ap) + [[0, n]])

            def norm(idx, col):
                dve.wait_ge(ss_pe0.sem, ss_pe0.at(idx))
                V.tensor_scalar(srow, ps[:, 0, 0:N], 1.0 / D, EPS, ALU.mult, ALU.add).then_inc(var_ev.sem, 1)
                dve.wait_ge(sd_ev.sem, sd_ev.at(idx))
                V.reciprocal(srow, srow)
                dve.drain()
                for k in range(KD):
                    i = V.scalar_tensor_tensor(out=hT[:, k, :], in0=xT[:, k, :], scalar=vT[:, col + k:col + k + 1],
                                               in1=srow, op0=ALU.mult, op1=ALU.mult)
                i.then_inc(h_ev.sem, 1)

            def x_is_done():
                dve.drain()
                dve.sem_inc(x_done.sem, 1)

            dve.wait_ge(w8_pe.sem, w8_pe.at(0))
            for i in range(2):
                m = tt(w8[0:H, 272 * i:272 * i + 272], ps[0:H, i, 0:272], c("future")[0:H, 272 * i:272 * i + 272], ALU.add)
            m.then_inc(w8_ev.sem, 1)
            V.memset(ssum[:, :, :], 1.0)
            V.memset(R, 0.0)
            V.memset(Qz[:, :, :], 0.0)
            dve.wait_ge(bp1_pe.sem, bp1_pe.at(0))
            own = c("own").rearrange("p (m x) -> p m x", m=2)
            for t in range(2):
                V.tensor_copy(biasS[:, t, 0:PAST], ps[:, 3, 0:PAST])
                tt(biasS[:, t, PAST:N], ps[:, 3, PAST:N], own[:, t, :], ALU.add)
            V.tensor_copy(biasSc, ps[:, 3, N:N + NC_BLK]).then_inc(bp_ev.sem, 1)
            dve.wait_ge(xt_ev.sem, xt_ev.at(0, 8))
            dve.sem_inc(x_done.sem, 1)
            dve.wait_ge(bp2_pe.sem, bp2_pe.at(0))
            V.tensor_copy(biasP[:, :, :].rearrange("p (i h) x -> p i (h x)", i=4), ps[:, 4:8, :]).then_inc(bp_ev.sem, 1)
            dve.wait_ge(bp3_pe.sem, bp3_pe.at(0))
            for q in range(2):
                m = V.tensor_copy(biasC[:, q, :, :], ps[:, 3, 256 * q:256 * q + 120].rearrange("p (h n) -> p h n", h=H))
            m.then_inc(bp_ev.sem, 1)
            V.memset(uext[:, :, 0:3], 0.0)

            for l in range(2):
                dve.wait_ge(vt_ev0.sem, vt_ev0.at(0))
                norm(2 * l, V_MIX + 8 * l)
                if l == 1:
                    dve.wait_ge(st_kv.sem, st_kv.at(0))
                for f in range(2):
                    for m in range(3):
                        dve.wait_ge(kv_pe.sem, kv_pe.at(l, 3 * f + m + 1))
                        n = ROWS[m]
                        V.tensor_copy(kv[0:n, m, KV_HALF * f:KV_HALF * f + KV_HALF],
                                      ps[0:n, (4 + 3 * f + m) % 8, 0:KV_HALF]).then_inc(kv_ev.sem, 1)
                for h in range(MH):
                    dve.wait_ge(u_pe.sem, u_pe.at(l, h + 1))
                    V.tensor_copy(uext[:, h, 3:3 + T], ps[:, 2 + h, 0:T])
                    V.tensor_copy(sview(None, h)[:, :, 3:7], ps[:, 2 + h, T:N].rearrange("p (b t) -> p b t", b=NB)
                                  ).then_inc(u_ev.sem, 1)
                dve.wait_ge(cv_ev.sem, cv_ev.at(l))
                dve.drain()
                for h in range(MH):
                    V.tensor_copy(us[:, h, :].rearrange("p (b t) -> p b t", b=NB), sview(None, h)[:, :, 3:7])
                    x = uext[:, h, T:T + 3]
                    i = V.tensor_copy(cstage[:, h, :].rearrange("p (s x) -> p s x", x=3),
                                      bass.AP(x.tensor, x.offset, [x.ap[0], [7, NB + 1], [1, 3]]))
                i.then_inc(cst_ev.sem, 1)
                for j in range(4):
                    for h in range(MH):
                        w = vT[:, V_CW + (4 * l + j) * 4 + h:V_CW + (4 * l + j) * 4 + h + 1]
                        uq = ucT[:, h, T:N].rearrange("p (b t) -> p b t", b=NB)
                        if j == 0:
                            b = vT[:, V_CB + 4 * l + h:V_CB + 4 * l + h + 1]
                            V.tensor_scalar(ucT[:, h, 0:T], uext[:, h, 0:T], w, b, ALU.mult, ALU.add)
                            i = V.tensor_scalar(uq, sview(None, h)[:, :, 0:4], w, b, ALU.mult, ALU.add)
                        else:
                            V.scalar_tensor_tensor(out=ucT[:, h, 0:T], in0=uext[:, h, j:j + T], scalar=w,
                                                   in1=ucT[:, h, 0:T], op0=ALU.mult, op1=ALU.add)
                            i = V.scalar_tensor_tensor(out=uq, in0=sview(None, h)[:, :, j:j + 4], scalar=w,
                                                       in1=uq, op0=ALU.mult, op1=ALU.add)
                    if j < 3:
                        dve.drain()
                i.then_inc(uc_d.sem, 1)
                dve.wait_ge(if_pe.sem, if_pe.at(l))
                V.tensor_scalar(srow[0:MH, :], ps[0:MH, 2, 0:N], gbias[0:MH, 2 * l:2 * l + 1], None, ALU.add)
                V.tensor_scalar(Mrow[0:MH, :], ps[0:MH, 3, 0:N], gbias[0:MH, 2 * l + 1:2 * l + 2], None, ALU.add
                                ).then_inc(if_ev.sem, 1)
                dve.wait_ge(q_ev.sem, q_ev.at(l))
                for t in range(2):
                    for v in range(KVH):
                        rr = slice(64 * v, 64 * v + 64)
                        i = V.tensor_copy(Qz[rr, t, :].rearrange("p (b v g) -> p b v g", v=KVH, g=G)[:, :, v, :],
                                          qT[rr, :, T + 16 * t:T + 16 * t + 16].rearrange("p g b -> p b g"))
                i.then_inc(qz_ev.sem, 1)
                V.memset(pc[:, :, :], 0.0)
                V.memset(hid[:, :, :, 15:16], 0.0)
                kvu = take(4 * 9 * P, Y_at).rearrange("p (u s x) -> p u s x", u=4, s=9)
                for s in range(1, 9, 2):
                    dve.wait_ge(ct_pe.sem, ct_pe.at(l, s + 1))
                    V.tensor_copy(kvu[:, :, s, :], ps[:, 5, :].rearrange("p (u x) -> p u x", u=4)).then_inc(ct_d.sem, 1)
                for v in range(2):
                    dve.wait_ge(hid_pe.sem, hid_pe.at(l, v + 1))
                    V.tensor_copy(cvec[:, v:v + 1], ps[:, 6 + v, 300:301]).then_inc(c_ev.sem, 1)
                dve.wait_ge(hid_ev.sem, hid_ev.at(l))
                x = hid[:, 1, 8:18:9, :]
                V.tensor_copy(hidr[:, :, :].rearrange("p h (g n) -> p h g n", g=G),
                              bass.AP(x.tensor, x.offset, [x.ap[0], x.ap[1], [0, G], x.ap[2]])).then_inc(hidr_ev.sem, 1)
                dve.wait_ge(kc_pe.sem, kc_pe.at(l))
                x, y = ps[:, 7, 0:64], c("hrow")
                tt(VcZ[:, :, :], bass.AP(x.tensor, x.offset, [x.ap[0], [0, H], x.ap[1]]), rep(y, 64), ALU.mult
                   ).then_inc(kc_d.sem, 1)
                dve.drain()
                dve.wait_ge(gs_ev.sem, gs_ev.at(l))
                for q in range(hq):
                    x = pc[:, q, :].rearrange("p (h n) -> p h n", h=H)[:, :, 0:NC_BLK]
                    dve.wait_ge(cs_pe.sem, cs_pe.at(l, q + 1))
                    tt(x, ps[:, 2 + q, 0:P].rearrange("p (h n) -> p h n", h=H)[:, :, 0:NC_BLK], biasC[:, q, :, :], ALU.add)
                    dve.drain()
                    V.tensor_reduce(cmx, x, AX.X, ALU.max)
                    dve.drain()
                    tt(x, x, rep(cmx, NC_BLK), ALU.subtract).then_inc(cx_d.sem, 1)
                    dve.wait_ge(cx_a.sem, cx_a.at(l, q + 1))
                    V.tensor_reduce(csm, x, AX.X, ALU.add)
                    dve.drain()
                    V.reciprocal(csm, csm)
                    dve.drain()
                    V.scalar_tensor_tensor(out=csm, in0=csm, scalar=c("cvalid")[:, q:q + 1], in1=gns[:, q, 0:24:3],
                                           op0=ALU.mult, op1=ALU.mult)
                    dve.drain()
                    tt(x, x, rep(csm, NC_BLK), ALU.mult).then_inc(cx_n.sem, 1)
                    dve.drain()

                def add(i):
                    q, h = i // H, i % H
                    ext = (q + 1) * P
                    dve.wait_ge(s_pe.sem, s_pe.at(l, i + 1))
                    if i >= 2:
                        dve.wait_ge(t_pe.sem, t_pe.at(l, i - 1))
                    x = Pb[:, i % 2, :, 0:ext]
                    b = biasP[:, h, T - ext:T]
                    tt(x, ps[:, 4 + i % 2, :].rearrange("p (r x) -> p r x", r=2)[:, :, 0:ext],
                       bass.AP(b.tensor, b.offset, [b.ap[0], [0, 2], b.ap[1]]), ALU.add).then_inc(sa_ev.sem, 1)
                    dve.drain()
                    V.tensor_reduce(nm[:, i % 2, :], x, AX.X, ALU.max, negate=True).then_inc(nm_ev.sem, 1)

                def scale(i):
                    q, h = i // H, i % H
                    g = gg[:, i % 2, :]
                    x = Pb[:, i % 2, :, 0:(q + 1) * P]
                    dve.wait_ge(ex_ev.sem, ex_ev.at(l, i + 1))
                    V.reciprocal(g, sums[:, i % 2, :])
                    dve.drain()
                    tt(g, g, gns[:, q, 3 * h + 1:3 * h + 3], ALU.mult)
                    dve.drain()
                    tt(x, x, rep(g, (q + 1) * P), ALU.mult).then_inc(p_ev.sem, 1)

                add(0)
                for i in range(16):
                    if i < 15:
                        add(i + 1)
                    scale(i)
                dve.wait_ge(gsS_in.sem, gsS_in.at(l))
                for t in range(2):
                    for i in range(2):
                        dve.wait_ge(skt_pe.sem, skt_pe.at(l, 4 * t + i + 3))
                        V.tensor_copy(kTs[:, 1, 2 * i:2 * i + 2, :], ps[:, 4 + i, :].rearrange("p (b x) -> p b x", b=2)
                                      ).then_inc(skt_d.sem, 1)
                    dve.wait_ge(ss_pe.sem, ss_pe.at(l, t + 1))
                    dve.drain()
                    V.memset(Psc[:, 15:16], 0.0)
                    b = biasS[:, t, :]
                    tt(Ps[:, :, :], ps[:, 6:8, 0:N], bass.AP(b.tensor, b.offset, [b.ap[0], [0, 2], b.ap[1]]), ALU.add)
                    tt(Psc[:, 0:NC_BLK], ps[:, 7, N:N + NC_BLK], biasSc, ALU.add).then_inc(sadd.sem, 1)
                    dve.drain()
                    V.tensor_reduce(snm[:, 1:3], Ps[:, :, :], AX.X, ALU.max, negate=True)
                    V.tensor_reduce(snm[:, 0:1], Psc[:, 0:NC_BLK], AX.X, ALU.max, negate=True).then_inc(snm_ev.sem, 1)
                    dve.wait_ge(sex_ev.sem, sex_ev.at(l, t + 1))
                    V.reciprocal(sgg, ssm)
                    dve.drain()
                    tt(sgg, sgg, gS[:, t, :], ALU.mult)
                    dve.drain()
                    tt(Ps[:, :, :], Ps[:, :, :], rep(sgg[:, 1:3], N), ALU.mult)
                    V.tensor_scalar(Psc[:, 0:NC_BLK], Psc[:, 0:NC_BLK], sgg[:, 0:1], None, ALU.mult).then_inc(sps_ev.sem, 1)
                    dve.wait_ge(spv_pe.sem, spv_pe.at(l, t + 1))
                    for v in range(KVH):
                        rr = slice(64 * v, 64 * v + 64)
                        i = V.tensor_copy(oNT[rr, :, T + 16 * t:T + 16 * t + 16].rearrange("p g b -> p b g"),
                                          ps[rr, 2, 0:P].rearrange("p (b v g) -> p b v g", v=KVH, g=G)[:, :, v, :])
                    i.then_inc(son_ev.sem, 1)
                li, f = srow[0:MH, :], Mrow[0:MH, :]
                r = [rows[0:MH, i, :] for i in range(10)]
                dve.drain()
                V.tensor_scalar(r[0], f, 0.0, None, ALU.min)
                V.scalar_tensor_tensor(out=r[1], in0=f, scalar=-1.0, in1=f, op0=ALU.mult, op1=ALU.max).then_inc(lf_d.sem, 1)
                dve.wait_ge(lf_a.sem, lf_a.at(l))
                V.tensor_scalar(r[1], r[1], 1.0, None, ALU.add).then_inc(lf_d2.sem, 1)
                dve.wait_ge(m0_in.sem, m0_in.at(l))
                V.memset(r[4][:, 0:T], 0.0)
                V.tensor_copy(r[4][:, T:N].rearrange("p (b t) -> p b t", b=NB), rep(m0c[0:MH, :], TS))
                dve.wait_ge(lf_a2.sem, lf_a2.at(l))
                tt(r[0], r[0], r[1], ALU.subtract)
                dve.drain()
                V.tensor_tensor_scan(r[2], c("keep")[0:MH, :], r[0], 0.0, ALU.mult, ALU.add)
                dve.drain()
                tt(r[3], li, r[2], ALU.subtract)
                dve.drain()
                tt(r[5], r[3], r[4], ALU.max)
                dve.drain()
                V.tensor_tensor_scan(f, c("reset")[0:MH, :], r[5], 0.0, ALU.add, ALU.max)
                dve.drain()
                tt(r[6], r[2], f, ALU.add)
                tt(r[7], r[4], f, ALU.subtract)
                V.tensor_scalar(r[8][:, 0:T], r[3][:, 0:T], f[:, T - 1:T], None, ALU.subtract)
                last = f[:, T + TS - 1:N:TS]
                tt(r[8][:, T:N].rearrange("p (b t) -> p b t", b=NB), r[3][:, T:N].rearrange("p (b t) -> p b t", b=NB),
                   rep(last, TS), ALU.subtract).then_inc(row_d.sem, 1)
                dve.wait_ge(rt_ev.sem, rt_ev.at(l))
                for m in range(3):
                    n = ROWS[m]
                    dve.wait_ge(vt_pe.sem, vt_pe.at(l, 4 + m))
                    if m == 0:
                        V.memset(mv[:, :, :, 128:129], 1.0)
                    tt(mk[0:n, m, :, :], ps[0:n, 3 + m, :].rearrange("p (h e) -> p h e", h=MH),
                       rep(RT[0:n, m, 96:96 + MH], MD), ALU.mult).then_inc(ktk_ev.sem, 1)
                cau, caus = c("causal"), c("causal_s")[0:NS, :]

                def decay(h):
                    dve.wait_ge(mb_pe.sem, mb_pe.at(l, h + 1))
                    dve.drain()
                    tt(Db[:, 0:P], ps[:, 6, 0:P], cau, ALU.add)
                    V.tensor_copy(Db[:, P:T], ps[:, 6, P:T])
                    tt(Db[:, T:T + P], ps[:, 6, P:T], cau, ALU.add)
                    tt(Db[0:NS, 384:416], ps[0:NS, 6, T:N], caus, ALU.add).then_inc(md_ev.sem, 1)
                    dve.wait_ge(me_ev.sem, me_ev.at(l, h + 1))
                    if h >= 1:
                        dve.wait_ge(num_pe.sem, num_pe.at(l, h))
                    tt(Ab[:, 0:384], ps[:, 7, 0:384], Db[:, 0:384], ALU.mult)
                    tt(Ab[0:NS, 384:416], ps[0:NS, 7, 384:416], Db[0:NS, 384:416], ALU.mult).then_inc(ma_ev.sem, 1)

                decay(0)
                for h in range(MH):
                    dve.wait_ge(num_pe.sem, num_pe.at(l, h + 1))
                    nd = ps[:, 0, 0:258].rearrange("p (m e) -> p m e", m=2)
                    dve.drain()
                    V.tensor_copy(stmp[0:NS, 0:129], ps[0:NS, 1, 0:129])
                    V.scalar_tensor_tensor(out=dn[:, 0:2], in0=nd[:, :, 128], scalar=-1.0, in1=RT[:, 0:2, 64 + h],
                                           op0=ALU.mult, op1=ALU.max)
                    dve.drain()
                    V.scalar_tensor_tensor(out=stmp[0:NS, 0:129], in0=ps[0:NS, 1, 129:258], scalar=RT[0:NS, 2, h:h + 1],
                                           in1=stmp[0:NS, 0:129], op0=ALU.mult, op1=ALU.add)
                    dve.drain()
                    V.scalar_tensor_tensor(out=dn[0:NS, 2:3], in0=stmp[0:NS, 128:129], scalar=-1.0,
                                           in1=RT[0:NS, 2, 64 + h:65 + h], op0=ALU.mult, op1=ALU.max)
                    tt(dn2[:, 0:2], dn[:, 0:2], nd[:, :, 128], ALU.max)
                    dve.drain()
                    tt(dn2[0:NS, 2:3], dn[0:NS, 2:3], stmp[0:NS, 128:129], ALU.max)
                    dve.drain()
                    V.reciprocal(dn3[:, 0:2], dn2[:, 0:2])
                    V.reciprocal(dn3[0:NS, 2:3], dn2[0:NS, 2:3])
                    dve.drain()
                    V.tensor_scalar(hm[0:NS, 2, h, :], stmp[0:NS, 0:128], dn3[0:NS, 2:3], None, ALU.mult)
                    tt(hm[:, 0:2, h, :], nd[:, :, 0:128], rep(dn3[:, 0:2], MD), ALU.mult).then_inc(mh_ev.sem, 1)
                    if h + 1 < MH:
                        decay(h + 1)
                dve.drain()
                tt(hsq[:, 0:2, :, :], hm[:, 0:2, :, :], hm[:, 0:2, :, :], ALU.mult)
                tt(hsq[0:NS, 2, :, :], hm[0:NS, 2, :, :], hm[0:NS, 2, :, :], ALU.mult)
                dve.drain()
                V.tensor_reduce(ssum[:, 0:2, :], hsq[:, 0:2, :, :], AX.X, ALU.add)
                V.tensor_reduce(ssum[0:NS, 2, :], hsq[0:NS, 2, :, :], AX.X, ALU.add)
                dve.drain()
                V.tensor_scalar(ssr[:, :, :], ssum[:, :, :], 1.0 / MD, EPS, ALU.mult, ALU.add).then_inc(var2_ev.sem, 1)
                dve.wait_ge(wcb_ev.sem, wcb_ev.at(l))
                for h in range(MH):
                    dve.wait_ge(cn_pe.sem, cn_pe.at(l, h + 1))
                    dve.wait_ge(cs_ev.sem, cs_ev.at(l))
                    for i, (b0, b1) in enumerate(((0, 3), (3, 6), (6, 8))):
                        x = C0[:, b0:b1, h, :]
                        m = tt(x, x, ps[:, 5 + i, 0:129 * (b1 - b0)].rearrange("p (b e) -> p b e", e=129), ALU.add)
                    m.then_inc(cn_ev.sem, 1)
                dve.wait_ge(sd2_ev.sem, sd2_ev.at(l))
                V.reciprocal(ssi[:, :, :], ssr[:, :, :])
                dve.drain()
                tt(hm[:, 0:2, :, :], hm[:, 0:2, :, :], rep(ssi[:, 0:2, :], MD), ALU.mult)
                tt(hm[0:NS, 2, :, :], hm[0:NS, 2, :, :], rep(ssi[0:NS, 2, :], MD), ALU.mult).then_inc(hn_ev.sem, 1)
                dve.wait_ge(o_ev.sem, o_ev.at(l))
                for h in range(MH):
                    dve.wait_ge(om_pe.sem, om_pe.at(l, h + 1))
                    V.scalar_tensor_tensor(out=omT[:, h, :], in0=ps[:, h, 0:N], scalar=vT[:, V_MN + 4 * l + h:V_MN + 4 * l + h + 1],
                                           in1=oT[:, h, :], op0=ALU.mult, op1=ALU.mult).then_inc(om_ev.sem, 1)
                for d in range(8):
                    dve.wait_ge(f_sig.sem, f_sig.at(l, d + 1))
                    b = 4 * (d % 2)
                    x = fsig[:, d % 2, :, :]
                    tt(x, x, ps[:, b + 2:b + 4, 0:N], ALU.mult)
                    dve.drain()
                    tt(merged[:, d, :], x[:, 0, :], x[:, 1, :], ALU.add).then_inc(f_ev.sem, 1)
                for d in range(8):
                    dve.wait_ge(wo_pe.sem, wo_pe.at(l, d + 1))
                    tt(xT[:, d, :], xT[:, d, :], ps[:, d % 4, 0:N], ALU.add).then_inc(wo_ev.sem, 1)
                x_is_done()
                if l == 0:
                    norm(1, V_FFN)
                    dve.wait_ge(st_state.sem, st_state.at(0))
                    for f in range(22):
                        dve.wait_ge(ff_sil.sem, ff_sil.at(0, f + 1))
                        tt(gT[:, f, :], sil[:, f % 2, 0, :], ps[:, 2 + 2 * (f % 3), 0:N], ALU.mult).then_inc(ff_g.sem, 1)
                    for d in range(8):
                        dve.wait_ge(fy_pe.sem, fy_pe.at(0, d + 1))
                        tt(xT[:, d, :], xT[:, d, :], ps[:, d % 4, 0:N], ALU.add).then_inc(fy_ev.sem, 1)
                    x_is_done()
                elif MOE:
                    norm(3, V_FFN + 8)
                    dve.wait_ge(st_state.sem, st_state.at(1))
                    dve.wait_ge(st_kv.sem, st_kv.at(1))

                    def mid(x, n):
                        return bass.AP(x.tensor, x.offset, [x.ap[0], x.ap[1], [0, n], x.ap[2]])

                    V.memset(lg[:, :, :], 0.0)
                    dve.drain()
                    dve.wait_ge(lg_pe.sem, lg_pe.at(0))
                    V.tensor_copy(lg[:, 0:2, :], ps[:, 1, 0:16].rearrange("p (m e) -> p m e", m=2))
                    V.tensor_copy(lg[0:NS, 2, :], ps[0:NS, 1, 16:24])
                    dve.drain()
                    low = c("elow").rearrange("p (e j) -> p e j", e=NE)
                    tt(gt[:, :, :, :], mid(lg[:, :, :], NE), rep(lg[:, :, :], NE), ALU.is_gt)
                    tt(eq[:, :, :, :], mid(lg[:, :, :], NE), rep(lg[:, :, :], NE), ALU.is_equal)
                    V.tensor_reduce(gmx, lg[:, :, :], AX.X, ALU.max)
                    dve.drain()
                    for m in range(3):
                        tt(eq[:, m, :, :], eq[:, m, :, :], low, ALU.mult)
                    tt(gx[:, :, :], lg[:, :, :], rep(gmx, NE), ALU.subtract).then_inc(lgx_d.sem, 1)
                    dve.drain()
                    tt(gt[:, :, :, :], gt[:, :, :, :], eq[:, :, :, :], ALU.add)
                    dve.drain()
                    V.tensor_reduce(rank[:, :, :], gt[:, :, :, :], AX.X, ALU.add)
                    dve.drain()
                    V.tensor_scalar(sel[:, :, :], rank[:, :, :], 1.5, None, ALU.is_lt)
                    dve.drain()
                    tt(sel[:, :, :], sel[:, :, :], rep(c("valid"), NE), ALU.mult).then_inc(sel_d.sem, 1)
                    dve.wait_ge(lgx_a.sem, lgx_a.at(0))
                    dve.drain()
                    tt(gate[:, :, :], gx[:, :, :], sel[:, :, :], ALU.mult)
                    dve.drain()
                    V.tensor_reduce(gsum, gate[:, :, :], AX.X, ALU.add)
                    dve.drain()
                    V.tensor_scalar(gsum, gsum, 0.5, None, ALU.max)
                    dve.drain()
                    V.reciprocal(gsum, gsum)
                    dve.drain()
                    tt(gate[:, :, :], gate[:, :, :], rep(gsum, NE), ALU.mult)
                    dve.wait_ge(pos_pe.sem, pos_pe.at(0))
                    V.tensor_scalar(posm[:, :, :], sel[:, :, :], 1e6, -1e6, ALU.mult, ALU.add)
                    dve.drain()
                    tt(posm[:, 0:2, :], posm[:, 0:2, :], ps[:, 1, 64:80].rearrange("p (m e) -> p m e", m=2), ALU.add)
                    tt(posm[0:NS, 2, :], posm[0:NS, 2, :], ps[0:NS, 1, 80:88], ALU.add)
                    cn = cnt[0:NE, :]
                    V.tensor_copy(cn, ps[0:NE, 1, 96:97])
                    dve.drain()
                    V.tensor_scalar(nblk[0:NE, :], cn, 0.5, None, ALU.is_gt)
                    V.tensor_scalar(nb2[0:NE, :], cn, P + 0.5, None, ALU.is_gt)
                    V.tensor_scalar(eend[0:NE, :], cn, 2 * P + 0.5, None, ALU.is_gt)
                    dve.drain()
                    tt(nb2[0:NE, :], nb2[0:NE, :], eend[0:NE, :], ALU.add)
                    dve.drain()
                    tt(nblk[0:NE, :], nblk[0:NE, :], nb2[0:NE, :], ALU.add).then_inc(pos_d.sem, 1)
                    dve.wait_ge(nb_pe.sem, nb_pe.at(0))
                    V.tensor_copy(estart[0:NE, :], ps[0:NE, 1, 100:101])
                    dve.drain()
                    tt(eend[0:NE, :], estart[0:NE, :], nblk[0:NE, :], ALU.add)
                    V.tensor_scalar(ge1[0:NE, :], c("item")[0:NE, :], estart[0:NE, :], None, ALU.is_ge)
                    V.tensor_scalar(off[0:NE, :], c("item")[0:NE, :], estart[0:NE, :], -float(P), ALU.subtract, ALU.mult)
                    dve.drain()
                    V.tensor_scalar(ge2[0:NE, :], c("item")[0:NE, :], eend[0:NE, :], None, ALU.is_ge)
                    dve.drain()
                    tt(Mw[0:NE, :], ge1[0:NE, :], ge2[0:NE, :], ALU.subtract)
                    dve.drain()
                    tt(off[0:NE, :], off[0:NE, :], Mw[0:NE, :], ALU.mult).then_inc(nb_d.sem, 1)
                    dve.wait_ge(it_pe.sem, it_pe.at(0))
                    for m in range(3):
                        n = ROWS[m]
                        V.tensor_copy(posI[0:n, m, :], ps[0:n, 4, 16 * m:16 * m + NITEM])
                        V.tensor_copy(gateI[0:n, m, :], ps[0:n, 4, 64 + 16 * m:64 + 16 * m + NITEM])
                    V.tensor_copy(itemi[0:1, 0:NITEM + 1], ps[0:1, 4, 128:129 + NITEM]).then_inc(items.sem, 1)
                    dve.drain()
                    dve.sem_inc(cmb_ev.sem, 8)
                    dve.wait_ge(items.sem, items.at(0))
                    n_items = dve.value_load(itemi[0:1, NITEM:NITEM + 1], min_val=1, max_val=NITEM)
                    with dve.Fori(0, n_items) as w:
                        for m in range(3):
                            n = ROWS[m]
                            V.tensor_scalar(Sel[0:n, m, :], c("iota")[0:n, :], posI[0:n, m, bass.ds(w, 1)], None, ALU.is_equal)
                            i = V.tensor_scalar(SelG[0:n, m, :], c("iota")[0:n, :], posI[0:n, m, bass.ds(w, 1)],
                                                gateI[0:n, m, bass.ds(w, 1)], ALU.is_equal, ALU.mult)
                        i.then_inc(g_sel.sem, 1)
                        for ch in range(FCH):
                            dve.wait_ge(m_sil.sem, FCH * w + ch + 1)
                            if ch >= 2:
                                dve.wait_ge(m_t.sem, FCH * w + ch - 1)
                            tt(gm[:, ch % 2, :], sl[:, ch % 2, :], ps[:, 2 + ch % 2, 256:512], ALU.mult).then_inc(m_g.sem, 1)
                        for d in range(KD):
                            dve.wait_ge(cmb_pe.sem, 8 * w + d + 1)
                            tt(xT[:, d, :], xT[:, d, :], ps[:, d % 4, 0:N], ALU.add).then_inc(cmb_ev.sem, 1)
                        dve.drain()
                    x_is_done()
            norm(3 + MOE, V_FIN)

        @block.gpsimd
        def _(pool):
            pool.dma_start(pti[:, :], a["pages"]).then_inc(pt_in.sem, 16)
            pool.wait_ge(pt_in.sem, 16)

            cmpQ = cmpN.rearrange("p s (u q d) -> p s u q d", u=4, q=2)

            def pairs(x):
                return x.rearrange("(r q) (u d) -> r q u d", q=2, u=4)

            def page(l, cache, b, g):
                v = pool.value_load(pti[0:1, 2 * b + g:2 * b + g + 1], min_val=0, max_val=a[cache].shape[1] - 1)
                return a[cache][l, v]

            for l in range(2):
                if l == 1:
                    pool.wait_ge(st_state.sem, st_state.at(0))
                    pool.wait_ge(fy_pe.sem, fy_pe.at(0))
                pool.dma_start(cvp[0:24, :], a["state_conv"][l].rearrange("b j c -> (b j) c")).then_inc(cvp_in.sem, 16)
                if l == 0:
                    pool.wait_ge(xt_pe.sem, xt_pe.at(0, 8))
                    pool.wait_ge(bp3_pe.sem, bp3_pe.at(0))
                for b in range(NB):
                    for g in range(2):
                        src = pairs(page(l, "cache_cmp", b, g))
                        for q in range(2):
                            pool.dma_start(cmpQ[64 * g:64 * g + 64, b, :, q, :], src[:, q]).then_inc(cmp_in.sem, 16)
                pool.dma_start(m0c[0:MH, :], a["state_m"][l].rearrange("b h -> h b")).then_inc(m0_in.sem, 16)
                pool.dma_start(nld[0:NS, :], a["state_n"][l].rearrange("b h d -> (b h) d")).then_inc(n0_in.sem, 16)
                pool.wait_ge(kv_ev.sem, kv_ev.at(l))
                for k, name in enumerate(("p_cmp", "p_slc", "p_win")):
                    s = (st_cmp if k == 0 else st_kv).sem
                    pool.dma_start(outs[name][l].rearrange("(m p) c -> p m c", p=P), kv[:, 0:2, 256 * k:256 * k + 256]
                                   ).then_inc(s, 16)
                for k, name in enumerate(("s_cmp", "s_slc")):
                    pool.dma_start(outs[name][l].rearrange("b t c -> (b t) c"), kv[0:NS, 2, 256 * k:256 * k + 256]
                                   ).then_inc(st_kv.sem, 16)
                for b in range(NB):
                    pool.dma_start(outs["s_win"][l, b, PAST - TS:PAST, :], kv[TS * b:TS * b + TS, 2, 512:768]
                                   ).then_inc(st_kv.sem, 16)
                pool.dma_start(outs["s_win"][l, :, 0:PAST - TS, :], a["cache_win"][l, :, TS:PAST, :]).then_inc(st_win.sem, 16)
                pool.wait_ge(st_cmp.sem, st_cmp.at(l))
                src = pairs(outs["p_cmp"][l])
                for q in range(2):
                    pool.dma_start(cmpQ[:, 8, :, q, :], src[:, q]).then_inc(cmp_in.sem, 16)
                pool.wait_ge(gs_ev.sem, gs_ev.at(l))
                pool.dma_start(gscr[l], gns[0:NS, 2, :]).then_inc(gsS_st.sem, 16)
                pool.wait_ge(gsS_st.sem, gsS_st.at(l))
                pool.dma_start(gS[:, :, :], gscr[l].rearrange("n (h c) -> (n h) c", c=3).rearrange("(m p) c -> p m c", p=P)
                               ).then_inc(gsS_in.sem, 16)
                for t in range(2):
                    if t == 0:
                        pool.wait_ge(ct_pe.sem, ct_pe.at(l))
                    else:
                        pool.wait_ge(spv_pe.sem, spv_pe.at(l, 1))
                    for b in range(4):
                        for g in range(2):
                            pool.dma_start(sw[:, 0, b, g, :], page(l, "cache_slc", 4 * t + b, g)).then_inc(sw_in.sem, 16)
                    pool.dma_start(sw[:, 1, :, :, :].rearrange("p b g c -> p (b g) c"),
                                   a["cache_win"][l, 4 * t:4 * t + 4].rearrange("b (g p) c -> p (b g) c", p=P)
                                   ).then_inc(sw_in.sem, 16)
                    if t == 0:
                        pool.wait_ge(hid_pe.sem, hid_pe.at(l))
                        pool.dma_start(C0[:, :, :, 0:MD].rearrange("p b h e -> p (b h) e"),
                                       a["state_C"][l].rearrange("b h d e -> d (b h) e")).then_inc(c0_in.sem, 16)
                pool.wait_ge(spv_pe.sem, spv_pe.at(l))
                pool.wait_ge(mqk_ev.sem, mqk_ev.at(l))
                nc.gpsimd.memset(mqz[:, :, :, :], 0.0)
                pool.drain()
                for h in range(MH):
                    x = mqz[:, h, 0, 0:TS]
                    i = nc.gpsimd.tensor_copy(bass.AP(x.tensor, x.offset, [x.ap[0], [NS + TS, NB], [1, TS]]),
                                              mqT[:, h, T:N].rearrange("p (b t) -> p b t", b=NB))
                i.then_inc(mz_ev.sem, 1)
                pool.wait_ge(row_a.sem, row_a.at(l))
                pool.wait_ge(vt_ev.sem, vt_ev.at(l))
                pool.wait_ge(ktk_ev.sem, ktk_ev.at(l))

                def own_values(h):
                    if h >= 1:
                        pool.wait_ge(cn_pe.sem, cn_pe.at(l, h))
                    y, z = mv[0:NS, 2, h, :], c("bsel")[0:NS, :]
                    nc.gpsimd.tensor_tensor(mvz[0:NS, :, :], bass.AP(y.tensor, y.offset, [y.ap[0], [0, NB], y.ap[1]]),
                                            bass.AP(z.tensor, z.offset, [z.ap[0], z.ap[1], [0, 129]]), ALU.mult
                                            ).then_inc(vz_ev.sem, 1)

                own_values(0)
                pool.wait_ge(num_pe.sem, num_pe.at(l))
                pool.wait_ge(wcb_ev.sem, wcb_ev.at(l))
                for h in range(MH):
                    x, y = C0[:, :, h, :], wcb[:, h, :]
                    i = nc.gpsimd.tensor_tensor(x, x, bass.AP(y.tensor, y.offset, [y.ap[0], y.ap[1], [0, 129]]), ALU.mult)
                i.then_inc(cs_ev.sem, 1)
                for h in range(1, MH):
                    own_values(h)
                pool.wait_ge(cp_ev.sem, cp_ev.at(l))
                pool.dma_start(outs["p_C"][l, 0].rearrange("h d e -> d h e"), Cp[:, :, 0:MD]).then_inc(st_state.sem, 16)
                pool.wait_ge(cn_ev.sem, cn_ev.at(l))
                pool.dma_start(outs["s_C"][l].rearrange("b h d e -> d (b h) e"),
                               C0[:, :, :, 0:MD].rearrange("p b h e -> p (b h) e")).then_inc(st_state.sem, 16)
                pool.dma_start(outs["p_m"][l].rearrange("b h -> h b"), mout[0:MH, 0:1]).then_inc(st_state.sem, 16)
                pool.dma_start(outs["s_m"][l].rearrange("b h -> h b"), mout[0:MH, 1:9]).then_inc(st_state.sem, 16)
                pool.wait_ge(no_ev.sem, no_ev.at(l))
                pool.dma_start(outs["s_n"][l].rearrange("b h d -> (b h) d"), nout[0:NS, 0:P]).then_inc(st_state.sem, 16)
                pool.dma_start(outs["p_n"][l, 0], nout[0:MH, P:2 * P]).then_inc(st_state.sem, 16)
                pool.dma_start(outs["p_conv"][l, 0], cvo[0:3, :]).then_inc(st_state.sem, 16)
                pool.dma_start(outs["s_conv"][l].rearrange("b j c -> (b j) c"), cvo[3:27, :]).then_inc(st_state.sem, 16)
            pool.wait_ge(y_ev.sem, y_ev.at(0))
            pool.dma_start(outs["y_p"][0].rearrange("(m p) c -> p m c", p=P), ytok[:, 0:2, :]).then_inc(y_st.sem, 16)
            pool.dma_start(outs["y_s"].rearrange("b t c -> (b t) c"), ytok[0:NS, 2, :]).then_inc(y_st.sem, 16)
            pool.wait_ge(st_state.sem, st_state.at(1))
            pool.wait_ge(st_kv.sem, st_kv.at(1))
            pool.wait_ge(st_win.sem, st_win.at(1))
            pool.wait_ge(y_st.sem, 32)


OUTS = [("y_p", (1, T, D)), ("y_s", (NB, TS, D)),
        ("p_cmp", (2, T, 256)), ("p_slc", (2, T, 256)), ("p_win", (2, T, 256)),
        ("p_C", (2, 1, MH, MD, MD)), ("p_n", (2, 1, MH, MD)), ("p_m", (2, 1, MH)), ("p_conv", (2, 1, 3, 512)),
        ("s_cmp", (2, NB, TS, 256)), ("s_slc", (2, NB, TS, 256)), ("s_win", (2, NB, PAST, 256)),
        ("s_C", (2, NB, MH, MD, MD)), ("s_n", (2, NB, MH, MD)), ("s_m", (2, NB, MH)), ("s_conv", (2, NB, 3, 512))]
RETURN_SHAPES = [(1, T, D), (NB, TS, D), (2, 1, T, 2, 2, 64), (2, 1, T, 2, 2, 64), (2, 1, T, 2, 2, 64),
                 (2, 1, MH, MD, MD), (2, 1, MH, MD), (2, 1, MH), (2, 1, 3, 512),
                 (2, NB, TS, 2, 2, 64), (2, NB, TS, 2, 2, 64), (2, NB, PAST, 2, 2, 64),
                 (2, NB, MH, MD, MD), (2, NB, MH, MD), (2, NB, MH), (2, NB, 3, 512)]


def kernel(**inputs):
    import concourse.bacc as bacc
    from concourse.bass_utils import run_bass_kernel_spmd

    x = {k: np.asarray(v) for k, v in inputs.items()}
    n_phys = x["cache_cmp_kv"].shape[1]
    vecs = np.concatenate([x[k].reshape(-1, P) for k in
                           ("norm_mix", "norm_ffn", "norm_final", "m_conv_w", "m_conv_b", "m_norm", "cmp_pe")])
    arrays = {
        "const": CONST, "table": x["rel_bias_table"], "vecs": vecs, "x_prompt": x["x_prompt"],
        "x_sample": x["x_sample"], "gate_bias": x["m_gate_bias"],
        "cache_cmp": x["cache_cmp_kv"].reshape(2, n_phys, P, 256), "cache_slc": x["cache_slc_kv"].reshape(2, n_phys, P, 256),
        "cache_win": x["cache_win_kv"].reshape(2, NB, PAST, 256), "state_C": x["state_mlstm_C"],
        "state_n": x["state_mlstm_n"], "state_m": x["state_mlstm_m"], "state_conv": x["state_mlstm_conv"],
        "pages": x["page_table"].reshape(1, -1), "w_in": x["w_in"], "cmp_w1": x["cmp_w1"].reshape(2, 2, 2048, P),
        "cmp_w2": x["cmp_w2"], "m_qkv": x["m_qkv"], "w_up_a": x["w_up_a"], "w_up_b": x["w_up_b"], "w_out": x["w_out"],
        "ffn_w1": x["ffn_w1"], "ffn_w3": x["ffn_w3"], "ffn_w2": x["ffn_w2"], "router": x["moe_router"],
        "moe_w1": x["moe_w1"], "moe_w3": x["moe_w3"], "moe_w2": x["moe_w2"],
    }
    nc = bacc.Bacc("TRN2", target_bir_lowering=False, num_devices=1)
    feeds, a = {}, {}
    for name, v in arrays.items():
        v = np.ascontiguousarray(v)
        feeds["in_" + name] = v
        a[name] = nc.dram_tensor("in_" + name, v.shape, mybir.dt.from_np(v.dtype), kind="ExternalInput").ap()
    outs = {n: nc.dram_tensor("out_" + n, s, F32, kind="ExternalOutput").ap() for n, s in OUTS}
    build(nc, a, outs)
    r = run_bass_kernel_spmd(nc, [feeds], core_ids=[0])
    return tuple(r.results[0]["out_" + n].reshape(s) for (n, _), s in zip(OUTS, RETURN_SHAPES))
```

```python
from contextlib import ExitStack

import numpy as np

import concourse.bass as bass
from concourse import mybir

ALU = mybir.AluOpType
ACT = mybir.ActivationFunctionType
F32 = mybir.dt.float32
I32 = mybir.dt.int32
F32R = mybir.dt.float32r
AX = mybir.AxisListType

P = 128
D = 1024
KD = D // P
T = 256
NB, TS = 8, 4
NS = NB * TS
N = T + NS
ROWS = (P, P, NS)
PAST = 256
H, KVH, HD = 8, 2, 64
G = H // KVH
MH, MD = 4, 128
EPS = 1e-6
NBUCKET, MAX_DIST = 32, 128
NC_BLK = 15
FF = 2816
NE = 8
NEG = -1e30
DIM0 = 259
WB = 544

OFF_KV = 512
OFF_G = OFF_KV + 768
OFF_U = OFF_G + 24
OFF_O = OFF_U + 512
OFF_IF = OFF_O + 512
OFF_GA = OFF_IF + 8
OFF_GB = OFF_GA + D
KV_HALF = 396
UE = T + 3 + NB * 7

NITEM = 12
NRAW = 6
NU = 33
FCH = FF // 256


def constants():
    cols = {}
    parts = []

    def put(name, a):
        a = np.asarray(a, np.float32)
        full = np.zeros((P, a.shape[1]), np.float32)
        full[:a.shape[0]] = a
        cols[name] = (sum(p.shape[1] for p in parts), a.shape[1])
        parts.append(full)

    r = np.arange(P)
    put("ident", np.eye(P))
    put("rev", np.eye(P)[::-1])
    put("ones", np.ones((P, P)))
    put("causal", np.where(r[:, None] > r[None, :], -NEG, 0.0))
    q = np.arange(NS)
    same = q[:, None] // TS == q[None, :] // TS
    put("causal_s", np.where(same & (q[:, None] <= q[None, :]), 0.0, -NEG))
    put("headsel", np.repeat(np.eye(MH), P, axis=1))
    start = np.ones(N)
    first = np.concatenate([[0], T + TS * np.arange(NB)])
    start[first] = 0.0
    put("keep", np.tile(start, (MH, 1)))
    put("reset", np.tile(np.where(start == 0.0, NEG, 0.0), (MH, 1)))
    put("hrow", np.repeat(np.eye(H), 16, axis=0))
    put("cvalid", np.stack([r >= 31, np.ones(P)], axis=1))
    put("bsel", np.repeat(np.eye(NB), TS, axis=0))
    put("iota", np.tile(r, (P, 1)))
    put("tri", np.where(r[:, None] < r[None, :], 1.0, 0.0))
    e = np.arange(NE)
    put("elow", np.tile((e[None, :] < e[:, None]).astype(np.float32).reshape(1, 64), (P, 1)))
    put("etri", (e[:, None] < e[None, :]).astype(np.float32))
    put("valid", np.stack([np.ones(P), np.ones(P), r < NS], axis=1))
    put("item", np.tile(np.arange(NITEM), (NE, 1)))
    put("eidx", e[:, None])
    keep_cols = sum(p.shape[1] for p in parts)
    sel = np.zeros((H, TS, P))
    for row in range(P):
        sel[row % H, (row // H) % TS, row] = 1.0
    put("rowsel", sel.reshape(H, TS * P))
    dist = DIM0 - np.arange(WB)
    d = np.maximum(dist, 0)
    exact = NBUCKET // 2
    logp = exact + (np.log(np.maximum(d, 1).astype(np.float32) / exact)
                    / np.float32(np.log(MAX_DIST / exact)) * (NBUCKET - exact)).astype(np.int32)
    bucket = np.where(d < exact, d, np.minimum(logp, NBUCKET - 1))
    put("bucket", (bucket[None, :] == np.arange(NBUCKET)[:, None]).astype(np.float32))
    put("future", np.tile(np.where(dist < 0, NEG, 0.0), (H, 1)))
    own = np.zeros((P, 2, NS))
    for tile in range(2):
        for row in range(P):
            own[row, tile] = np.where(np.arange(NS) // TS == tile * 4 + row // 32, 0.0, NEG)
    put("own", own.reshape(P, 2 * NS))
    return np.ascontiguousarray(np.concatenate(parts, axis=1)), cols, keep_cols


CONST, CC, NKEEP = constants()


UNITS = [("A", 0), ("B", 0)] + [u for c in range(1, FCH) for u in (("A", c), ("B", c), ("C", c - 1))] + [("C", FCH - 1)]
UNIT_AT = {u: i for i, u in enumerate(UNITS)}


class Event:

    def __init__(self, sem, per, first=0, n=None):
        self.sem, self.per, self.first, self.n = sem, per, first, per if n is None else n

    def at(self, l, k=None):
        return l * self.per + self.first + (self.n if k is None else k)

    def steps(self, *counts):
        firsts = [sum(counts[:i]) for i in range(len(counts))]
        return [Event(self.sem, self.per, f, n) for f, n in zip(firsts, counts)]


def build(nc, a, outs):
    with ExitStack() as ctx:
        ctx.enter_context(nc.allow_non_contiguous_dma(reason="small state vectors"))
        NCOL = CONST.shape[1]
        SLOT = 6144
        MIX = 4352
        HALF = 2048
        XN, YN = 4620, 4608
        TOT = 53104
        BASE = 16640
        arena = nc.alloc_sbuf_tensor_at("arena", [P, TOT], F32, offset=BASE)
        pos = [0]

        def take(n, at=None):
            if at is None:
                at = pos[0]
                pos[0] += n
                assert pos[0] <= TOT, pos[0]
            return arena[:, at:at + n]

        cst = take(NKEEP)

        def c(name):
            o, n = CC[name]
            if o + n <= NKEEP:
                return cst[:, o:o + n]
            return cset[:, o - NKEEP:o - NKEEP + n]

        xT = take(KD * N).rearrange("p (k n) -> p k n", k=KD)
        hT = take(KD * N).rearrange("p (k n) -> p k n", k=KD)
        vT = take(152)
        gbias = take(4)
        biasP = take(H * T).rearrange("p (h x) -> p h x", h=H)
        biasC = take(2 * H * NC_BLK).rearrange("p (m h n) -> p m h n", m=2, h=H)
        biasS = take(2 * N).rearrange("p (m x) -> p m x", m=2)
        biasSc = take(NC_BLK)
        small = take(160)
        pti = nc.alloc_sbuf_tensor_at("pages", [1, 16], I32, offset=BASE + 4 * TOT)
        itemi = nc.alloc_sbuf_tensor_at("items", [1, 16], I32, offset=BASE + 4 * TOT + 64)
        ring0 = pos[0]
        take(3 * SLOT)
        slot = [take(SLOT, ring0 + s * SLOT) for s in range(3)]
        gap = [ring0 + s * SLOT + MIX for s in range(3)]
        work0 = pos[0]
        qT_at = pos[0]
        qT = take(G * N).rearrange("p (g n) -> p g n", g=G)
        omT = take(G * N, qT_at).rearrange("p (g n) -> p g n", g=G)
        kv = take(3 * 792).rearrange("p (m c) -> p m c", m=3)
        oT = take(MH * N).rearrange("p (h n) -> p h n", h=MH)
        uext = take(MH * UE).rearrange("p (h n) -> p h n", h=MH)
        X_at = pos[0]
        take(XN)
        cmpN = take(9 * 512, X_at).rearrange("p (s c) -> p s c", s=9)
        sw = take(4096, X_at).rearrange("p (r b g c) -> p r b g c", r=2, b=4, g=2)
        mk = take(3 * 512, X_at).rearrange("p (m h e) -> p m h e", m=3, h=MH)
        mv = take(3 * 516, X_at + 1536).rearrange("p (m h e) -> p m h e", m=3, h=MH)
        hm = take(3 * 512, X_at + 3084).rearrange("p (m h e) -> p m h e", m=3, h=MH)
        Y_at = pos[0]
        take(YN)
        kvT2 = take(4 * 9 * P, Y_at).rearrange("p (v s x) -> p v s x", v=2, s=18)
        C0 = take(NB * MH * 129, Y_at).rearrange("p (b h e) -> p b h e", b=NB, h=MH)
        cvp_at = Y_at + 4096
        cvp = take(512, cvp_at)
        Z_at = pos[0]
        take(KD * N)
        kTs = take(2048, Z_at).rearrange("p (r b x) -> p r b x", r=2, b=4)
        hsq = take(1536, Z_at).rearrange("p (m h e) -> p m h e", m=3, h=MH)
        merged = take(KD * N, Z_at).rearrange("p (k n) -> p k n", k=KD)
        B_at = pos[0]
        take(2960)
        Pb = take(1024, B_at).rearrange("p (i r x) -> p i r x", i=2, r=2)
        PT = take(1024, B_at + 1024).rearrange("p (i r k x) -> p i r k x", i=2, r=2, k=2)
        PTn = take(384, B_at + 2048)
        pc = take(256, B_at + 2432).rearrange("p (i x) -> p i x", i=2)
        PcT = take(256, B_at + 2688).rearrange("p (i x) -> p i x", i=2)
        Ps = take(2 * N, B_at).rearrange("p (r x) -> p r x", r=2)
        Psc = take(16, B_at + 2 * N)
        rows = take(7 * N, B_at).rearrange("p (i n) -> p i n", i=7)
        Db = take(416, B_at)
        Ab = take(416, B_at + 416)
        mvz = [take(NB * 129, at).rearrange("p (b e) -> p b e", b=NB) for at in (B_at + 832, gap[0])]
        Cp = take(516, B_at + 1864).rearrange("p (h e) -> p h e", h=MH)
        nout = take(256, B_at + 2380)
        stmp = take(132, B_at + 2636)
        cvo = take(512, B_at)
        VcS_at = pos[0]
        VcS = take(NB * P).rearrange("p (b c) -> p b c", b=NB)
        mqz = take(MH * NB * NS, VcS_at).rearrange("p (h b t) -> p h b t", h=MH, b=NB)
        oNT = take(G * N).rearrange("p (g n) -> p g n", g=G)
        Qz = take(2 * P).rearrange("p (m r) -> p m r", m=2)
        RT = take(3 * P).rearrange("p (m r) -> p m r", m=3)
        R = take(N)
        Mrow = take(N)
        wcb = take(MH * NB).rearrange("p (h b) -> p h b", h=MH)
        gS = take(6).rearrange("p (m c) -> p m c", m=2)
        nld = take(P)
        ssum = take(12).rearrange("p (m h) -> p m h", m=3)
        ssr = take(12).rearrange("p (m h) -> p m h", m=3)
        ssi = take(12).rearrange("p (m h) -> p m h", m=3)
        srow = take(N)
        hidr = take(KVH * G * 16).rearrange("p (h x) -> p h x", h=KVH)
        us = take(MH * NS).rearrange("p (h t) -> p h t", h=MH)
        cstage = take(MH * 27).rearrange("p (h t) -> p h t", h=MH)
        ucT = take(MH * N, gap[0]).rearrange("p (h n) -> p h n", h=MH)
        hid = take(2 * KVH * 9 * 16, gap[0] + 1152).rearrange("p (v s x) -> p v s x", v=2, s=18)
        mqT = take(MH * N, gap[1]).rearrange("p (h n) -> p h n", h=MH)
        kTp = take(512, gap[1] + 1152).rearrange("p (r x) -> p r x", r=2)
        kTn = take(64, gap[1] + 1664).rearrange("p (r x) -> p r x", r=2)
        mkT = take(MH * N, gap[2]).rearrange("p (h n) -> p h n", h=MH)
        VcZ = take(512, gap[2] + 1152).rearrange("p (h d) -> p h d", h=H)
        KcT = take(144, ring0 + 1664).rearrange("p (s x) -> p s x", s=9)
        cset = take(NCOL - NKEEP, ring0 + 2 * SLOT)
        w8 = take(WB, ring0 + 2 * SLOT + 2100)
        tab = take(8, ring0 + 2 * SLOT + 2700)
        vrow = take(2 * P, ring0 + 2 * SLOT + 2720)
        xtok = take(3 * D, work0).rearrange("p (m c) -> p m c", m=3)
        Lh = take(H * 384, work0 + 3 * D).rearrange("p (h x) -> p h x", h=H)
        gT = take(22 * N, X_at).rearrange("p (f n) -> p f n", f=22)
        sil = take(2 * 2 * N, B_at).rearrange("p (i f n) -> p i f n", i=2, f=2)
        RAW_AT = -(-ring0 // 8) * 8
        at = [RAW_AT]

        def tensor(name, n, dtype=F32R):
            at[0] += n
            return nc.alloc_sbuf_tensor_at(name, [P, n], dtype, offset=BASE + 4 * (at[0] - n))

        raws = tensor("weights_in", NRAW * 2048, F32)
        whs, wls = tensor("weights_high", 3 * 2048), tensor("weights_low", 3 * 2048)
        h2h, h2l = (tensor(n, 3 * D)[:, :].rearrange("p (m c) -> p m c", m=3) for n in ("tokens_high", "tokens_low"))
        Sel = tensor("chosen", 3 * P)[:, :].rearrange("p (m s) -> p m s", m=3)
        Xh, Xl = (tensor(n, D)[:, :].rearrange("p (k s) -> p k s", k=KD) for n in ("item_high", "item_low"))
        gTh, gTl = (tensor(n, 512)[:, :].rearrange("p (i f x) -> p i f x", i=2, f=2) for n in ("gated_high", "gated_low"))
        raw = [raws[:, i * 2048:i * 2048 + 2048] for i in range(NRAW)]
        Wh, Wl = ([t[:, i * 2048:i * 2048 + 2048].rearrange("p (k n) -> p k n", k=4) for i in range(3)] for t in (whs, wls))
        mpos = [at[0]]

        def mtake(n):
            mpos[0] += n
            assert mpos[0] <= pos[0]
            return take(n, mpos[0] - n)

        yS = mtake(D)
        SelG = mtake(3 * P).rearrange("p (m s) -> p m s", m=3)
        SelT = mtake(N)
        sl = mtake(512).rearrange("p (i x) -> p i x", i=2)
        gm = mtake(512).rearrange("p (i x) -> p i x", i=2)
        posT = mtake(N)
        gateT = mtake(N)
        gt = mtake(192).rearrange("p (m e j) -> p m e j", m=3, e=NE)
        eq = mtake(192).rearrange("p (m e j) -> p m e j", m=3, e=NE)
        lg, rank, sel, gate, gx, posm = (mtake(24).rearrange("p (m e) -> p m e", m=3) for _ in range(6))
        posI, gateI = (mtake(3 * (NITEM + 1)).rearrange("p (m w) -> p m w", m=3) for _ in range(2))
        gmx, gsum = mtake(3), mtake(3)
        cnt, nblk, estart, eend, nb2 = (mtake(1) for _ in range(5))
        ge1, ge2, Mw, off = (mtake(NITEM) for _ in range(4))
        cvec = small[:, 0:2]
        nm = small[:, 2:6].rearrange("p (i r) -> p i r", i=2)
        sums = small[:, 6:10].rearrange("p (i r) -> p i r", i=2)
        gg = small[:, 10:14].rearrange("p (i r) -> p i r", i=2)
        cmx = small[:, 14:22]
        csm = small[:, 22:30]
        m0c = small[:, 30:38]
        snm = small[:, 38:41]
        ssm = small[:, 41:44]
        sgg = small[:, 44:47]
        dn = small[:, 48:51]
        dn2 = small[:, 52:55]
        dn3 = small[:, 56:59]
        mout = small[:, 60:69]
        ytok = take(3 * D, work0).rearrange("p (m c) -> p m c", m=3)
        gns = take(72).rearrange("p (m c) -> p m c", m=3)

        router = take(KD * NE).rearrange("p (k e) -> p k e", k=KD)
        ps = ctx.enter_context(nc.psum_tensor("ps", [P, 8, 512], F32))
        scr = nc.dram_tensor("bias_scratch", (H, WB), F32)
        gscr = nc.dram_tensor("gate_scratch", (2, NS, 24), F32)
        scr, gscr = scr.ap(), gscr.ap()

        def ev(name, per=1):
            return Event(ctx.enter_context(nc.semaphore(name)), per)

        wl = [ev(f"weights_in_{s}", 10) for s in range(3)]
        s_setup = ev("setup_in")
        s_xin = ev("x_in")
        y_pe, y_ev, y_st = ev("y_pe"), ev("y_ev"), ev("y_st")
        pt_in, st_cmp = ev("pages_in"), ev("st_cmp", 16)
        w8_pe, vt_pe0, bp1_pe, xt_pe, bp2_pe, bp3_pe = ev("setup_tensor", 13).steps(1, 1, 1, 8, 1, 1)
        w8_ev, bp_ev = ev("setup_vector", 4).steps(1, 3)
        vt_ev0, xt_ev = ev("setup_scalar", 9).steps(1, 8)
        w8_st, hank = ev("bias_row_out"), ev("hankel_in")
        x_done = ev("x_done")
        sq_ev, ss_pe0, var_ev, sd_ev, h_ev = ev("sq_done", KD), ev("sumsq_pe"), ev("var_done"), ev("std_done"), ev("h_done", KD)
        cvp_in, cv_pe, cv_ev = ev("conv_in", 16), ev("conv_pe"), ev("conv_ev")
        q_pe, q_ev = ev("q_pe", 4), ev("q_ev", 4)
        kv_pe, kv_ev = ev("kv_pe", 6), ev("kv_ev", 6)
        u_pe, u_ev = ev("u_pe", 4), ev("u_ev", 4)
        o_pe, o_ev = ev("o_pe", 4), ev("o_ev", 4)
        if_pe, if_ev = ev("if_pe"), ev("if_ev")
        kt_pe, kt_ev = ev("kt_pe"), ev("kt_ev")
        gs_ev = ev("gate_sig")
        uc_d, uc_a = ev("conv_sum", 1), ev("conv_silu", 1)
        mqk_pe, mqk_ev = ev("mqk_pe", 8), ev("mqk_ev", 8)
        cmp_in = ev("cmp_in", 16 * 34)
        ct_pe, ct_a, ct_d = ev("ct_pe", 9), ev("ct_evA", 5), ev("ct_evD", 4)
        hid_pe, c_ev, hid_ev = ev("hid_pe", 2), ev("c_ev", 2), ev("hid_ev", 2)
        kc_pe, kc_a, kc_d = ev("kc_pe"), ev("kc_evA"), ev("kc_evD")
        cs_pe, cx_d, cx_a, cx_n, cx_t, pct_ev = (ev("cs_pe", 2), ev("cx_sub", 2), ev("cx_exp", 2), ev("cx_norm", 2),
                                                 ev("cx_tr", 2), ev("pct_ev", 2))
        s_pe, sa_ev, nm_ev, ex_ev, p_ev, t_pe, pt_ev, pv_pe, on_ev = (
            ev("scores_pe", 16), ev("scores_taken", 16), ev("rowmax", 16), ev("probs", 16), ev("probs_gated", 16),
            ev("probsT_pe", 16), ev("probsT_ev", 16), ev("pv_pe", 16), ev("on_ev", 2))
        qz_ev, hidr_ev, cst_ev = ev("qz_ev"), ev("hidr_ev"), ev("cst_ev")
        sw_in = ev("past_in", 2 * 9 * 16)
        skt_pe, skt_a, skt_d = ev("skt_pe", 8), ev("skt_evA", 4), ev("skt_evD", 4)
        ss_pe, sadd, snm_ev, sex_ev, sps_ev, st_pe, spt_ev, spv_pe, son_ev = (
            ev("s_scores_pe", 2), ev("s_taken", 2), ev("s_max", 2), ev("s_probs", 2), ev("s_gated", 2),
            ev("s_probsT", 2), ev("s_probsT_ev", 2), ev("s_pv_pe", 2), ev("s_on_ev", 2))
        gsS_st, gsS_in = ev("gates_st", 16), ev("gates_in", 16)
        m0_in, c0_in, n0_in = ev("m0_in", 16), ev("c0_in", 16), ev("n0_in", 16)
        lf_d, lf_d2, row_d = ev("gate_rows_vector", 3).steps(1, 1, 1)
        lf_a, lf_a2, row_a = ev("gate_rows_scalar", 3).steps(1, 1, 1)
        rt_pe, rt_ev, wcb_ev = ev("rt_pe"), ev("rt_ev"), ev("wcb_ev")
        vt_pe, vt_ev, ktk_ev = ev("vt_pe", 6), ev("vt_ev", 3), ev("ktok_ev", 3)
        mz_ev = ev("mqz_ev")
        mb_pe, md_ev, me_ev, ma_ev, num_pe, mh_ev = (ev("mb_pe", 4), ev("md_ev", 4), ev("me_ev", 4), ev("ma_ev", 4),
                                                    ev("num_pe", 4), ev("mh_ev", 4))
        var2_ev, sd2_ev, hn_ev, om_pe, om_ev = ev("mvar_ev"), ev("msd_ev"), ev("hn_ev"), ev("om_pe", 4), ev("om_ev", 4)
        cp_pe, cp_ev = ev("cp_pe"), ev("cp_ev")
        vz_ev, cn_pe, cn_ev, cs_ev = ev("vz_ev", 4), ev("cn_pe", 4), ev("cn_ev", 4), ev("c0_scaled")
        no_pe, no_ev = ev("no_pe"), ev("no_ev")
        gt_pe, gt_ev = ev("channel_gate_pe", 16), ev("channel_gate_ev", 16)
        f_pe, f_ev = ev("up_pe", 8), ev("up_ev", 8)
        wo_pe, wo_ev = ev("wo_pe", 8), ev("wo_ev", 8)
        st_kv, st_state = ev("st_kv", 16 * 12), ev("st_state", 16 * 8)
        st_win = ev("st_win", 16)
        ff_pe, ff_sil, ff_g = ev("ff_pe", 22), ev("ff_silu", 22), ev("ff_g", 22)
        fy_pe, fy_ev = ev("fy_pe", 8), ev("fy_ev", 8)
        lg_pe, pos_pe, nb_pe, tp_pe, it_pe = ev("route_tensor", 5).steps(1, 1, 1, 1, 1)
        lgx_d, sel_d, pos_d, nb_d, items = ev("route_vector", 5).steps(1, 1, 1, 1, 1)
        h2_ev, lgx_a, tp_ev = ev("route_scalar", 3).steps(1, 1, 1)
        h2l_ev = ev("route_low")
        raw_in = [ev(f"unit_in_{i}") for i in range(NRAW)]
        g_sel, g_pe, g_ev, hi, lo, used, m_sil, m_g, m_t, m_gh, m_gl, yS_ev, cmb_pe, cmb_ev = (ev(n) for n in (
            "m_select", "m_gather", "m_gather_ev", "unit_high", "unit_low", "unit_used", "m_silu", "m_gated", "m_turned",
            "m_turned_high", "m_turned_low", "m_y_ev", "m_combine", "m_combined"))

        CMB_BANK = (0, 1, 6, 7)
        CN_BANK = ((5, 6, 7), (2, 3, 0))
        V_MIX, V_FFN, V_FIN, V_CW, V_CB, V_MN, V_PE = 0, 16, 32, 40, 72, 80, 88
        ident, ones, rev = c("ident"), c("ones"), c("rev")
        headsel = c("headsel").rearrange("p (h x) -> p h x", h=MH)
        hq = T // P

        def sview(t, h):
            return uext[:, h, T + 3:UE].rearrange("p (b x) -> p b x", b=NB)

        def pslot(s, k, n):
            return slot[s][:, 0:k * n].rearrange("p (k n) -> p k n", k=k)

        def loaded(s, u, l):
            return 48 * (u + 1) + (80 * (l + 1) if s == 0 else 0)

        FIRST = (3, 2, 2)

        def mixer_in(l, j):
            return loaded(j % 3, (FIRST[j % 3] + 5) * l + j // 3, l)

        half = [slot[1][:, 0:HALF], slot[2][:, 0:HALF], slot[2][:, HALF:2 * HALF], slot[0][:, 0:HALF],
                slot[1][:, HALF:2 * HALF]]
        half_in = [ev("half_in_0", 48 * 5), ev("half_in_1", 48 * 5), ev("half_in_2", 48 * 4)]
        half_in += ev("half_in_3", 48 * 2).steps(48, 48)
        HALVES = {f"G{j}": (j % 3, j // 3) for j in range(8)}
        HALVES |= {"U0": (2, 2), "U1": (0, 3), "U2": (1, 3), "U3": (3, 0)}
        HALVES |= {"W0": (2, 3), "W1": (0, 4), "W2": (1, 4), "W3": (4, 0)}

        def in_of(name, l):
            b, u = HALVES[name]
            return half_in[b].sem, half_in[b].at(l, 48 * (u + 1)), half[b].rearrange("p (k n) -> p k n", k=8)

        gsig = [slot[i][:, HALF:HALF + 8 * N].rearrange("p (x d n) -> p x d n", x=2, d=4) for i in range(2)]
        GATE_TILES = [(x, 2 * pair + i) for pair in range(4) for x in range(2) for i in range(2)]

        block = ctx.enter_context(nc.Block())

        @block.sync
        def _(sp):
            sp.dma_start(cset, a["const"][:, NKEEP:NCOL]).then_inc(s_setup.sem, 16)
            sp.dma_start(cst, a["const"][:, 0:NKEEP]).then_inc(s_setup.sem, 16)
            sp.dma_start(tab[0:NBUCKET, :], a["table"]).then_inc(s_setup.sem, 16)
            sp.dma_start(vrow[:, 0:P], a["vecs"][0:P, :]).then_inc(s_setup.sem, 16)
            sp.dma_start(vrow[0:24, P:2 * P], a["vecs"][P:152, :]).then_inc(s_setup.sem, 16)
            sp.dma_start(xtok[:, 0:2, :], a["x_prompt"].rearrange("b (m p) c -> p (b m) c", p=P)).then_inc(s_xin.sem, 16)
            sp.dma_start(xtok[0:NS, 2, :], a["x_sample"].rearrange("b t c -> (b t) c")).then_inc(s_xin.sem, 16)
            sp.dma_start(router[:, :, :], a["router"][0].rearrange("(k p) e -> p k e", p=P)).then_inc(s_xin.sem, 16)
            sp.dma_start(gbias[0:MH, 0:4], a["gate_bias"].rearrange("l i h -> h (l i)")).then_inc(s_xin.sem, 16)
            sp.wait_ge(w8_ev.sem, w8_ev.at(0))
            sp.dma_start(scr, w8[0:H, :]).then_inc(w8_st.sem, 16)
            sp.wait_ge(w8_st.sem, 16)
            for h in range(H):
                src = scr[h:h + 1, 4:4 + 384]
                src = bass.AP(src.tensor, src.offset, [[1, P], [1, 384]])
                sp.dma_start(Lh[:, h, :], src).then_inc(hank.sem, 16)

            def put(s, pieces):
                for dst, src in pieces:
                    sp.dma_start(dst, src).then_inc(wl[s].sem, 16)

            def split(dst, src, cuts):
                return [(dst[:, i:j, :], src[:, i:j, :]) for i, j in zip(cuts[:-1], cuts[1:])]

            def mixer_chunk(l, j):
                s = j % 3
                w = a["w_in"][l].rearrange("(k p) c -> p k c", p=P)
                cols = {0: (0, 512), 1: (OFF_KV, KV_HALF), 2: (OFF_KV + KV_HALF, KV_HALF), 3: (OFF_U, 512),
                        4: (OFF_O, 520)}
                if j in cols:
                    o, n = cols[j]
                    if j == 0:
                        dst = slot[0][:, 0:4096].rearrange("p (k g v d) -> p k g v d", k=KD, g=G, v=KVH)
                        src = w[:, :, 0:n].rearrange("p k (v g d) -> p k g v d", v=KVH, g=G)
                        put(s, [(dst[:, :, g, v, :], src[:, :, g, v, :]) for g in range(G) for v in range(KVH)])
                    else:
                        put(s, split(pslot(s, KD, n), w[:, :, o:o + n], (0, 3, 6, 8)))
                elif j == 5:
                    put(s, split(pslot(s, 32, P), a["cmp_w1"][l].rearrange("v (j p) e -> p (v j) e", p=P), (0, 11, 22, 32)))
                elif j == 6:
                    m = pslot(s, 13, P)
                    put(s, split(m, a["m_qkv"][l].rearrange("t h d e -> d (t h) e"), (0, 6, 12)))
                    put(s, [(m[:, 12, :].rearrange("p (v d) -> p v d", v=2), a["cmp_w2"][l].rearrange("v e d -> e v d"))])

            def half_chunk(l, name):
                b, _ = HALVES[name]
                m = half[b].rearrange("p (k n) -> p k n", k=8)
                kind, j = name[0], int(name[1])
                if kind == "U":
                    cc = slice(256 * j, 256 * j + 256)
                    ua = a["w_up_a"][l].rearrange("(v g d) c -> v d g c", v=KVH, g=G)
                    ub = a["w_up_b"][l].rearrange("(k p) c -> p k c", p=P)
                    pieces = [(m[0:64, 0:4, :], ua[0][:, :, cc]), (m[64:128, 0:4, :], ua[1][:, :, cc]),
                              (m[:, 4:8, :], ub[:, :, cc])]
                elif kind == "G":
                    o = (OFF_GA, OFF_GB)[j % 2] + 256 * (j // 2)
                    pieces = split(m, a["w_in"][l].rearrange("(k p) c -> p k c", p=P)[:, :, o:o + 256], (0, 3, 6, 8))
                else:
                    w = a["w_out"][l].rearrange("(k p) c -> p k c", p=P)
                    pieces = split(m, w[:, :, 256 * j:256 * j + 256], (0, 3, 6, 8))
                for dst, src in pieces:
                    sp.dma_start(dst, src).then_inc(half_in[b].sem, 16)

            mixer_chunk(0, 0)
            mixer_chunk(0, 1)
            sp.wait_ge(bp_ev.sem, bp_ev.at(0))
            sp.wait_ge(vt_ev0.sem, vt_ev0.at(0))
            sp.wait_ge(hank.sem, 16 * H)
            mixer_chunk(0, 2)
            for l in range(2):
                freed = {3: (q_pe, 4), 4: (kv_pe, 3), 5: (kv_pe, 6), 6: (u_pe, 4)}
                for j in range(3, 7):
                    sp.wait_ge(freed[j][0].sem, freed[j][0].at(l, freed[j][1]))
                    mixer_chunk(l, j)
                freed = {"G0": (if_pe, 1), "G1": (hid_pe, 2), "G2": (hid_pe, 2)}
                freed |= {f"G{j}": (gt_pe, 2 * j - 4) for j in range(3, 8)}
                freed |= {"U0": (gt_pe, 12), "U1": (gt_pe, 14), "U2": (gt_pe, 16), "U3": (vt_pe, 6)}
                freed |= {"W0": (f_pe, 2), "W1": (f_pe, 4), "W2": (f_pe, 6), "W3": (f_ev, 8)}
                for name, (event, k) in freed.items():
                    sp.wait_ge(event.sem, event.at(l, k))
                    half_chunk(l, name)
                if l == 0:
                    w1 = a["ffn_w1"][0].rearrange("(k p) f -> p k f", p=P)
                    w3 = a["ffn_w3"][0].rearrange("(k p) f -> p k f", p=P)
                    w2 = a["ffn_w2"][0].rearrange("(f p) d -> p f d", p=P)
                    for ch in range(15):
                        s = ch % 3
                        if ch == 0:
                            sp.wait_ge(f_ev.sem, f_ev.at(0, 8))
                        elif ch == 1:
                            sp.wait_ge(wo_pe.sem, wo_pe.at(0, 8))
                        elif ch == 2:
                            sp.wait_ge(wo_pe.sem, wo_pe.at(0, 8))
                        elif ch < 14:
                            sp.wait_ge(ff_pe.sem, ff_pe.at(0, 2 * (ch - 2)))
                        else:
                            sp.wait_ge(fy_pe.sem, fy_pe.at(0, 2))
                        if ch < FCH:
                            m = pslot(s, 16, 256)
                            put(s, [(m[:, 0:8, :], w1[:, :, 256 * ch:256 * ch + 256])])
                            put(s, split(m[:, 8:16, :], w3[:, :, 256 * ch:256 * ch + 256], (0, 4, 8)))
                        else:
                            o = 256 * (ch - FCH)
                            put(s, split(pslot(s, 22, 256), w2[:, :, o:o + 256], (0, 8, 16, 22)))
                    for j in range(3):
                        sp.wait_ge(fy_pe.sem, fy_pe.at(0, 4 + 2 * j))
                        mixer_chunk(1, j)
                else:
                    sp.wait_ge(f_pe.sem, f_pe.at(1, 8))
                    sp.wait_ge(wo_pe.sem, wo_pe.at(1, 8))
                    sp.wait_ge(items.sem, items.at(0))
                    n_items = sp.value_load(itemi[0:1, NITEM:NITEM + 1], min_val=1, max_val=NITEM)
                    with sp.Fori(0, n_items) as w:
                        e = sp.value_load(itemi[0:1, bass.ds(w, 1)], min_val=0, max_val=NE - 1)
                        w1 = a["moe_w1"][0, e].rearrange("(k p) f -> p k f", p=P)
                        w3 = a["moe_w3"][0, e].rearrange("(k p) f -> p k f", p=P)
                        w2 = a["moe_w2"][0, e].rearrange("(f p) d -> p f d", p=P)
                        for i, (kind, ch) in enumerate(UNITS):
                            s = i % NRAW
                            before = i - NRAW if i >= NRAW else (30 + s if s < 3 else 24 + s) - NU
                            sp.wait_ge(lo.sem, NU * w + NU + before + 1)
                            if kind == "C":
                                m = raw[s].rearrange("p (f d) -> p f d", f=2)
                                for f in range(2):
                                    sp.dma_start(m[:, f, :], w2[:, 2 * ch + f, :]).then_inc(raw_in[s].sem, 16)
                            else:
                                k0 = 0 if kind == "A" else 4
                                m = raw[s].rearrange("p (k x n) -> p k x n", k=4, x=2)
                                cc = slice(256 * ch, 256 * ch + 256)
                                sp.dma_start(m[:, :, 0, :], w1[:, k0:k0 + 4, cc]).then_inc(raw_in[s].sem, 16)
                                sp.dma_start(m[:, :, 1, :], w3[:, k0:k0 + 4, cc]).then_inc(raw_in[s].sem, 16)

        @block.tensor
        def _(pe):
            def mm(out, lhsT, rhs, start=True, stop=True):
                return nc.tensor.matmul(out, lhsT, rhs, start=start, stop=stop)

            def tr(out, x):
                k = x.shape[0]
                return nc.tensor.transpose(out, x, ident[0:k, 0:k])

            def norm(idx, k0, k1):
                for k in range(k0, k1):
                    pe.wait_ge(sq_ev.sem, sq_ev.at(idx, k + 1))
                    i = mm(ps[:, 4, 0:N], ones, hT[:, k, :], k == 0, k == KD - 1)
                if k1 == KD:
                    i.then_inc(ss_pe0.sem, 1)

            pe.wait_ge(s_setup.sem, 16 * 5)
            for i in range(2):
                m = mm(ps[0:H, i, 0:272], tab[0:NBUCKET, :], c("bucket")[0:NBUCKET, 272 * i:272 * i + 272])
            m.then_inc(w8_pe.sem, 1)
            tr(ps[:, 2, 0:P], vrow[:, 0:P])
            tr(ps[:, 2, P:P + 24], vrow[0:24, P:2 * P]).then_inc(vt_pe0.sem, 1)
            pe.wait_ge(w8_ev.sem, w8_ev.at(0))
            rs = c("rowsel").rearrange("p (t r) -> p t r", t=TS)
            for t in range(TS):
                mm(ps[:, 3, 0:PAST], rs[0:H, t, :], w8[0:H, 3 - t:3 - t + PAST], t == 0, t == TS - 1)
            for t in range(TS):
                new = w8[0:H, DIM0 - t:DIM0 - t + TS]
                new = bass.AP(new.tensor, new.offset, [new.ap[0], [0, NB], [1, TS]])
                mm(ps[:, 3, PAST:N], rs[0:H, t, :], new, t == 0, t == TS - 1)
            for t in range(TS):
                m = mm(ps[:, 3, N:N + NC_BLK], rs[0:H, t, :], w8[0:H, 34 - t:34 - t + 16 * 14 + 1:16], t == 0, t == TS - 1)
            m.then_inc(bp1_pe.sem, 1)
            pe.wait_ge(s_xin.sem, s_xin.at(0, 64))
            for k in range(KD):
                if k >= 4:
                    pe.wait_ge(xt_ev.sem, xt_ev.at(0, k - 3))
                b = 4 + k % 4
                for m in range(3):
                    i = tr(ps[:, b, m * P:m * P + ROWS[m]], xtok[0:ROWS[m], m, k * P:k * P + P])
                i.then_inc(xt_pe.sem, 1)
            pe.wait_ge(hank.sem, 16 * H)
            pe.wait_ge(xt_ev.sem, xt_ev.at(0, 8))
            for i in range(4):
                m = mm(ps[:, 4 + i, :], rev, Lh[:, 2 * i:2 * i + 2, 0:T])
            m.then_inc(bp1_pe.sem, 1)
            pe.wait_ge(bp_ev.sem, bp_ev.at(0, 1))
            for q in range(hq):
                m = mm(ps[:, 3, 256 * q:256 * q + 120], rev, Lh[:, :, 159 - P * q:159 - P * q + 225:16])
            m.then_inc(bp1_pe.sem, 1)

            for l in range(2):
                pe.wait_ge(cvp_in.sem, cvp_in.at(l))
                if l == 0:
                    pe.wait_ge(bp_ev.sem, bp_ev.at(0))
                    pe.wait_ge(vt_ev0.sem, vt_ev0.at(0))
                else:
                    pe.wait_ge(fy_ev.sem, fy_ev.at(0))
                for h in range(MH):
                    m = tr(ps[:, 1, h * 24:h * 24 + 24], cvp[0:24, h * P:h * P + P])
                m.then_inc(cv_pe.sem, 1)
                norm(2 * l, 0 if l == 0 else KD - 2, KD)
                pe.wait_ge(wl[0].sem, mixer_in(l, 0))
                w = pslot(0, KD, 512)
                for g in range(G):
                    if g == 1:
                        pe.wait_ge(cv_ev.sem, cv_ev.at(l))
                    for k in range(KD):
                        if g == 0:
                            pe.wait_ge(h_ev.sem, h_ev.at(2 * l, k + 1))
                        m = mm(ps[:, g, 0:N], w[:, k, g * P:g * P + P], hT[:, k, :], k == 0, k == KD - 1)
                    m.then_inc(q_pe.sem, 1)
                for f in range(2):
                    pe.wait_ge(wl[(1 + f) % 3].sem, mixer_in(l, 1 + f))
                    w = pslot(1 + f, KD, KV_HALF)
                    for m in range(3):
                        b = (4 + 3 * f + m) % 8
                        if b < 2:
                            pe.wait_ge(q_ev.sem, q_ev.at(l, b + 1))
                        for k in range(KD):
                            i = mm(ps[0:ROWS[m], b, 0:KV_HALF], hT[:, k, m * P:m * P + ROWS[m]], w[:, k, :], k == 0, k == KD - 1)
                        i.then_inc(kv_pe.sem, 1)
                pe.wait_ge(wl[0].sem, mixer_in(l, 3))
                w = pslot(0, KD, 512)
                for h in range(MH):
                    if h < 2:
                        pe.wait_ge(q_ev.sem, q_ev.at(l, 3 + h))
                    else:
                        pe.wait_ge(kv_ev.sem, kv_ev.at(l, h - 1))
                    for k in range(KD):
                        m = mm(ps[:, 2 + h, 0:N], w[:, k, h * P:h * P + P], hT[:, k, :], k == 0, k == KD - 1)
                    m.then_inc(u_pe.sem, 1)
                pe.wait_ge(wl[1].sem, mixer_in(l, 4))
                w = pslot(1, KD, 520)
                for h in range(MH):
                    pe.wait_ge(kv_ev.sem, kv_ev.at(l, 3 + h))
                    for k in range(KD):
                        m = mm(ps[:, (6 + h) % 8, 0:N], w[:, k, h * P:h * P + P], hT[:, k, :], k == 0, k == KD - 1)
                    m.then_inc(o_pe.sem, 1)
                for i in range(2):
                    pe.wait_ge(u_ev.sem, u_ev.at(l, i + 1))
                    for k in range(KD):
                        m = mm(ps[0:MH, 2 + i, 0:N], w[:, k, 512 + 4 * i:516 + 4 * i], hT[:, k, :], k == 0, k == KD - 1)
                m.then_inc(if_pe.sem, 1)
                pe.wait_ge(o_ev.sem, o_ev.at(l, 4))
                pe.wait_ge(kv_ev.sem, kv_ev.at(l, 6))
                for r in range(2):
                    for m in range(hq):
                        tr(ps[:, 0, r * T + m * P:r * T + m * P + P], kv[:, m, 256 + 256 * r:384 + 256 * r])
                for r in range(2):
                    m = tr(ps[:, 1, r * NS:r * NS + NS], kv[0:NS, 2, 256 + 256 * r:384 + 256 * r])
                m.then_inc(kt_pe.sem, 1)
                pe.wait_ge(wl[0].sem, mixer_in(l, 6))
                qkv = slot[0][:, 0:1536].rearrange("p (t h e) -> p t h e", t=3, h=MH)
                cw2 = slot[0][:, 1536:1664].rearrange("p (v d) -> p v d", v=2)
                pe.wait_ge(uc_a.sem, uc_a.at(l))
                for i in range(8):
                    if i < 2:
                        pe.wait_ge(u_ev.sem, u_ev.at(l, 3 + i))
                    elif i >= 4:
                        pe.wait_ge(mqk_ev.sem, mqk_ev.at(l, i - 3))
                    m = mm(ps[:, 4 + i % 4, 0:N], qkv[:, i // 4, i % 4, :], ucT[:, i % 4, :])
                    m.then_inc(mqk_pe.sem, 1)
                pe.wait_ge(cmp_in.sem, cmp_in.at(l))
                for s in range(9):
                    if s < 2:
                        pe.wait_ge(mqk_ev.sem, mqk_ev.at(l, 5 + s))
                    else:
                        taken = ct_a if s % 2 == 0 else ct_d
                        pe.wait_ge(taken.sem, taken.at(l, s // 2))
                    x = cmpN[:, s, :].rearrange("p (u x) -> p u x", u=4)
                    for v in range(2):
                        for h in range(KVH):
                            o = (v * KVH + h) * P
                            m = tr(ps[:, 4 + s % 2, o:o + P], x[:, v * KVH + h, :])
                    m.then_inc(ct_pe.sem, 1)
                pe.wait_ge(wl[2].sem, mixer_in(l, 5))
                cw1 = slot[2][:, 0:4096].rearrange("p (v j e) -> p v j e", v=2, j=16)
                pe.wait_ge(ct_a.sem, ct_a.at(l))
                pe.wait_ge(ct_d.sem, ct_d.at(l))
                for v in range(2):
                    pe.wait_ge(mqk_ev.sem, mqk_ev.at(l, 7 + v))
                    for j in range(16):
                        mm(ps[:, 6 + v, 0:270], cw1[:, v, j, :], kvT2[:, v, :, j:j + 8 * 14 + 1:8], j == 0, j == 15)
                    for j in range(16):
                        o = V_PE + (l * 2 + v) * 16 + j
                        m = mm(ps[:, 6 + v, 300:301], cw1[:, v, j, :], vT[:, o:o + 1], j == 0, j == 15)
                    m.then_inc(hid_pe.sem, 1)
                pe.wait_ge(hidr_ev.sem, hidr_ev.at(l))
                for h in range(KVH):
                    mm(ps[64 * h:64 * h + 64, 4, 0:144], cw2[:, 0, :], hid[:, 0, 9 * h:9 * h + 9, :])
                for h in range(KVH):
                    mm(ps[64 * h:64 * h + 64, 7, 0:64], hidr[:, h, :], cw2[:, 1, :])
                for h in range(KVH):
                    for b in range(NB):
                        m = mm(ps[0:16, 5 + h, b * 64:b * 64 + 64], hid[:, 1, 9 * h + b, :], cw2[:, 1, :])
                m.then_inc(kc_pe.sem, 1)
                def gate_tile(n, bank, part=None):
                    x, d = GATE_TILES[n]
                    sem, at, w = in_of(f"G{n // 2}", l)
                    pe.wait_ge(sem, at)
                    if n >= 2 and part != 1:
                        pe.wait_ge(gt_ev.sem, gt_ev.at(l, n - 1))
                    for k in range(KD) if part is None else range(4 * part, 4 * part + 4):
                        m = mm(ps[:, bank, 0:N], w[:, k, (d % 2) * P:(d % 2) * P + P], hT[:, k, :], k == 0, k == KD - 1)
                    if part != 0:
                        m.then_inc(gt_pe.sem, 1)

                gate_tile(0, 0)
                pe.wait_ge(if_ev.sem, if_ev.at(l))
                pe.wait_ge(kc_a.sem, kc_a.at(l))
                for v in range(KVH):
                    for q in range(hq):
                        for g in range(G):
                            h = v * G + g
                            m = mm(ps[:, 2 + q, h * 16:h * 16 + NC_BLK], qT[64 * v:64 * v + 64, g, q * P:q * P + P],
                                   KcT[64 * v:64 * v + 64, 8, 0:NC_BLK])
                        if v == 1:
                            m.then_inc(cs_pe.sem, 1)
                    if v == 0:
                        pe.drain()
                gate_tile(1, 1)
                for q in range(hq):
                    pe.wait_ge(cx_n.sem, cx_n.at(l, q + 1))
                    tr(ps[:, 2 + q, 0:P], pc[:, q, :]).then_inc(cx_t.sem, 1)

                def scores(i):
                    q, h = i // H, i % H
                    v, g, ext = h // G, h % G, (q + 1) * P
                    if i >= 2:
                        pe.wait_ge(sa_ev.sem, sa_ev.at(l, i - 1))
                    for r in range(2):
                        m = mm(ps[:, 4 + i % 2, r * T:r * T + ext], qT[64 * v:64 * v + 64, g, q * P:q * P + P],
                               kTp[64 * v:64 * v + 64, r, 0:ext])
                    m.then_inc(s_pe.sem, 1)

                def turn(i):
                    q = i // H
                    pe.wait_ge(p_ev.sem, p_ev.at(l, i + 1))
                    if i >= 2:
                        pe.wait_ge(pt_ev.sem, pt_ev.at(l, i - 1))
                    for r in range(2):
                        for k in range(q + 1):
                            m = tr(ps[:, 6 + i % 2, (2 * r + k) * P:(2 * r + k + 1) * P], Pb[:, i % 2, r, k * P:k * P + P])
                    m.then_inc(t_pe.sem, 1)

                def values(i):
                    q, h = i // H, i % H
                    v, g = h // G, h % G
                    o = ps[64 * v:64 * v + 64, q, g * P:g * P + P]
                    if h == 0:
                        pe.wait_ge(pct_ev.sem, pct_ev.at(l, q + 1))
                    pe.wait_ge(pt_ev.sem, pt_ev.at(l, i + 1))
                    mm(o, VcZ[:, h, :], PcT[:, q, :], True, False)
                    for r in range(2):
                        for k in range(q + 1):
                            x = 384 + 256 * r + 64 * v
                            m = mm(o, kv[:, k, x:x + 64], PT[:, i % 2, r, k, :], False, r == 1 and k == q)
                    m.then_inc(pv_pe.sem, 1)

                pe.wait_ge(kt_ev.sem, kt_ev.at(l))
                pe.wait_ge(kc_d.sem, kc_d.at(l))
                pe.wait_ge(pct_ev.sem, pct_ev.at(l))
                for i in range(18):
                    if i < 16:
                        scores(i)
                        gate_tile(2 + i // 2, 2 + i // 2 % 2, i % 2)
                    if 1 <= i < 17:
                        turn(i - 1)
                    if i >= 2:
                        values(i - 2)

                pe.wait_ge(qz_ev.sem, qz_ev.at(l))
                for t in range(2):
                    pe.wait_ge(sw_in.sem, sw_in.at(l, 144 * (t + 1)))
                    for i in range(16):
                        r, b, g = i // 8, (i // 2) % 4, i % 2
                        if i == 0:
                            pe.wait_ge(gt_ev.sem, gt_ev.at(l, (10, 14)[t]))
                            if t == 1:
                                pe.wait_ge(son_ev.sem, son_ev.at(l, 1))
                        if i == 8:
                            pe.wait_ge(sa_ev.sem, sa_ev.at(l))
                        m = tr(ps[:, 2 + i // 4, (i % 4) * P:(i % 4) * P + P], sw[:, r, b, g, 0:P])
                        if i % 4 == 3:
                            m.then_inc(skt_pe.sem, 1)
                    pe.wait_ge(skt_a.sem, skt_a.at(l, 2 * t + 2))
                    pe.wait_ge(skt_d.sem, skt_d.at(l, 2 * t + 2))
                    if t == 0:
                        pe.wait_ge(pt_ev.sem, pt_ev.at(l))
                    else:
                        pe.wait_ge(sadd.sem, sadd.at(l, 1))
                    for r in range(2):
                        for b in range(4):
                            qz = Qz[:, t, 32 * b:32 * b + 32]
                            mm(ps[32 * b:32 * b + 32, 6 + r, 0:PAST], qz, kTs[:, r, b, :])
                            if r == 1:
                                mm(ps[32 * b:32 * b + 32, 7, N:N + NC_BLK], qz, KcT[:, 4 * t + b, 0:NC_BLK])
                        m = mm(ps[:, 6 + r, PAST:N], Qz[:, t, :], kTn[:, r, :])
                    m.then_inc(ss_pe.sem, 1)
                    gate_tile((10, 14)[t], 3)
                    pe.wait_ge(sps_ev.sem, sps_ev.at(l, t + 1))
                    if t == 0:
                        pe.wait_ge(on_ev.sem, on_ev.at(l))
                    for r in range(2):
                        for g in range(2):
                            tr(ps[:, 0, (2 * r + g) * P:(2 * r + g + 1) * P], Ps[:, r, g * P:g * P + P])
                        tr(ps[0:NS, 1, r * P:r * P + P], Ps[:, r, PAST:N])
                    tr(ps[0:16, 1, 2 * P:3 * P], Psc[:, :]).then_inc(st_pe.sem, 1)
                    gate_tile((11, 15)[t], 4)
                    pe.wait_ge(spt_ev.sem, spt_ev.at(l, t + 1))
                    for b in range(4):
                        o, cc = ps[:, 2, 32 * b:32 * b + 32], slice(32 * b, 32 * b + 32)
                        mm(o, VcS[0:16, 4 * t + b, :], PTn[0:16, 2 * P + 32 * b:2 * P + 32 * b + 32], True, False)
                        for r in range(2):
                            for g in range(2):
                                mm(o, sw[:, r, b, g, P:2 * P], PT[:, 0, r, g, cc], False, False)
                            x = 384 + 256 * r
                            m = mm(o, kv[0:NS, 2, x:x + P], PTn[0:NS, r * P + 32 * b:r * P + 32 * b + 32], False, r == 1)
                    m.then_inc(spv_pe.sem, 1)
                    if t == 0:
                        gate_tile(12, 3)
                        gate_tile(13, 5)

                pe.wait_ge(row_a.sem, row_a.at(l))
                for m in range(3):
                    i = tr(ps[0:ROWS[m], 6, m * P:m * P + P], R[:, m * P:m * P + ROWS[m]])
                for h in range(MH):
                    mm(ps[:, 7, h * NB:h * NB + NB], headsel[0:MH, h, :], R[0:MH, T + TS - 1:N:TS])
                pe.wait_ge(n0_in.sem, n0_in.at(l))
                tr(ps[:, 7, 64:96], nld[0:NS, :]).then_inc(rt_pe.sem, 1)
                pe.wait_ge(spt_ev.sem, spt_ev.at(l))
                pe.wait_ge(son_ev.sem, son_ev.at(l))
                pe.wait_ge(gt_ev.sem, gt_ev.at(l))
                for kind in range(2):
                    for m in range(3):
                        for h in range(MH):
                            if kind == 0:
                                x = uext[:, h, 3 + m * P:3 + m * P + P] if m < 2 else us[:, h, :]
                            else:
                                x = ucT[:, h, m * P:m * P + ROWS[m]]
                            i = mm(ps[0:ROWS[m], 3 * kind + m, h * P:h * P + P], x, qkv[:, 2 - kind, h, :])
                        i.then_inc(vt_pe.sem, 1)
                pe.wait_ge(rt_ev.sem, rt_ev.at(l))
                pe.wait_ge(wcb_ev.sem, wcb_ev.at(l))
                pe.wait_ge(vt_ev.sem, vt_ev.at(l))
                pe.wait_ge(ktk_ev.sem, ktk_ev.at(l))

                def gates(h):
                    if h >= 1:
                        pe.wait_ge(md_ev.sem, md_ev.at(l, h))
                        pe.wait_ge(ma_ev.sem, ma_ev.at(l, h))
                    mm(ps[:, 6, 0:N], headsel[0:MH, h, :], Mrow[0:MH, :])
                    mm(ps[:, 7, 0:T], mkT[:, h, 0:P], mqT[:, h, 0:T])
                    mm(ps[:, 7, T:T + P], mkT[:, h, P:T], mqT[:, h, P:T])
                    mm(ps[0:NS, 7, 384:416], mkT[:, h, T:N], mqT[:, h, T:N]).then_inc(mb_pe.sem, 1)

                gates(0)
                pe.wait_ge(c0_in.sem, c0_in.at(l))
                pe.wait_ge(mz_ev.sem, mz_ev.at(l))
                for h in range(MH):
                    pe.wait_ge(ma_ev.sem, ma_ev.at(l, h + 1))
                    if h + 1 < MH:
                        gates(h + 1)
                    if h >= 2:
                        pe.wait_ge(mh_ev.sem, mh_ev.at(l, h - 1))
                    n = 2 * (h % 2)
                    mm(ps[:, n, 0:129], Ab[:, 0:P], mv[:, 0, h, :])
                    mm(ps[:, n, 129:258], Ab[:, P:T], mv[:, 0, h, :], True, False)
                    mm(ps[:, n, 129:258], Ab[:, T:T + P], mv[:, 1, h, :], False, True)
                    mm(ps[0:NS, n + 1, 0:129], Ab[0:NS, 384:416], mv[0:NS, 2, h, :])
                    for b in range(NB):
                        m = mm(ps[0:NS, n + 1, 129:258], mqz[:, h, b, :], C0[:, b, h, :], b == 0, b == NB - 1)
                    m.then_inc(num_pe.sem, 1)
                pe.wait_ge(mh_ev.sem, mh_ev.at(l, 3))
                for h in range(MH):
                    o = ps[:, (4, 1)[h // 3], (h % 3) * 129:(h % 3) * 129 + 129]
                    mm(o, mk[:, 0, h, :], mv[:, 0, h, :], True, False)
                    m = mm(o, mk[:, 1, h, :], mv[:, 1, h, :], False, True)
                m.then_inc(cp_pe.sem, 1)
                pe.wait_ge(ma_ev.sem, ma_ev.at(l))
                for h in range(MH):
                    pe.wait_ge(vz_ev.sem, vz_ev.at(l, h + 1))
                    if h == 1:
                        pe.wait_ge(mh_ev.sem, mh_ev.at(l))
                    if h >= 2:
                        pe.wait_ge(cn_ev.sem, cn_ev.at(l, h - 1))
                    for i, (b0, b1) in enumerate(((0, 3), (3, 6), (6, 8))):
                        m = mm(ps[:, CN_BANK[h % 2][i], 0:129 * (b1 - b0)], mk[0:NS, 2, h, :], mvz[h % 2][0:NS, b0:b1, :])
                    m.then_inc(cn_pe.sem, 1)
                pe.wait_ge(hn_ev.sem, hn_ev.at(l))
                pe.wait_ge(mh_ev.sem, mh_ev.at(l))
                pe.wait_ge(cp_ev.sem, cp_ev.at(l))
                for h in range(MH):
                    for m in range(3):
                        i = tr(ps[:, h, m * P:m * P + ROWS[m]], hm[0:ROWS[m], m, h, :])
                    i.then_inc(om_pe.sem, 1)
                pe.wait_ge(cn_ev.sem, cn_ev.at(l))
                tr(ps[0:NS, 4, 0:P], C0[:, :, :, 128:129].rearrange("p b h e -> p (b h e)"))
                tr(ps[0:MH, 4, P:2 * P], Cp[:, :, 128:129].rearrange("p h e -> p (h e)"))
                for h in range(MH):
                    m = tr(ps[0:27, 5, h * P:h * P + P], cstage[:, h, :])
                m.then_inc(no_pe.sem, 1)

                pe.wait_ge(om_ev.sem, om_ev.at(l))
                pe.wait_ge(son_ev.sem, son_ev.at(l))
                pe.wait_ge(no_ev.sem, no_ev.at(l))
                for d in range(8):
                    sem, at, w = in_of(f"U{d // 2}", l)
                    pe.wait_ge(sem, at)
                    b = 2 * (d % 4)
                    if d >= 4:
                        pe.wait_ge(f_ev.sem, f_ev.at(l, d - 3))
                    for x in range(2):
                        src = (oNT, omT)[x]
                        for k in range(4):
                            m = mm(ps[:, b + x, 0:N], w[:, 4 * x + k, (d % 2) * P:(d % 2) * P + P], src[:, k, :], k == 0, k == 3)
                    m.then_inc(f_pe.sem, 1)
                pe.wait_ge(f_ev.sem, f_ev.at(l))
                for d in range(8):
                    sem, at, w = in_of(f"W{d // 2}", l)
                    pe.wait_ge(sem, at)
                    if d >= 4:
                        pe.wait_ge(wo_ev.sem, wo_ev.at(l, d - 3))
                    for k in range(KD):
                        m = mm(ps[:, d % 4, 0:N], w[:, k, (d % 2) * P:(d % 2) * P + P], merged[:, k, :], k == 0, k == KD - 1)
                    m.then_inc(wo_pe.sem, 1)
                    if d >= 2:
                        norm(2 * l + 1, d - 2, d - 1)

                if l == 0:
                    norm(1, KD - 2, KD)
                    for f in range(22):
                        if f % 2 == 0:
                            pe.wait_ge(wl[(f // 2) % 3].sem, loaded((f // 2) % 3, FIRST[(f // 2) % 3] + f // 6, 0))
                        w = pslot((f // 2) % 3, 16, 256)[:, :, (f % 2) * P:(f % 2) * P + P]
                        b = 1 + 2 * (f % 3)
                        if f >= 3:
                            pe.wait_ge(ff_g.sem, ff_g.at(0, f - 2))
                        for x in range(2):
                            for k in range(KD):
                                if f == 0 and x == 0:
                                    pe.wait_ge(h_ev.sem, h_ev.at(1, k + 1))
                                m = mm(ps[:, b + x, 0:N], w[:, 8 * x + k, :], hT[:, k, :], k == 0, k == KD - 1)
                        m.then_inc(ff_pe.sem, 1)
                    pe.wait_ge(ff_g.sem, ff_g.at(0))
                    for d in range(8):
                        ch = FCH + d // 2
                        if d % 2 == 0:
                            pe.wait_ge(wl[ch % 3].sem, loaded(ch % 3, FIRST[ch % 3] + ch // 3, 0))
                        w = pslot(ch % 3, 22, 256)[:, :, (d % 2) * P:(d % 2) * P + P]
                        if d >= 4:
                            pe.wait_ge(fy_ev.sem, fy_ev.at(0, d - 3))
                        for f in range(22):
                            m = mm(ps[:, d % 4, 0:N], w[:, f, :], gT[:, f, :], f == 0, f == 21)
                        m.then_inc(fy_pe.sem, 1)
                        if d >= 2:
                            norm(2, d - 2, d - 1)
                else:
                    norm(3, KD - 2, KD)
                    pe.wait_ge(h_ev.sem, h_ev.at(3))
                    for m in range(3):
                        n = ROWS[m]
                        for k in range(KD):
                            tr(ps[0:n, 2 + 2 * m + k // 4, (k % 4) * P:(k % 4) * P + P], hT[:, k, m * P:m * P + n])
                        for k in range(KD):
                            i = mm(ps[0:n, 1, 8 * m:8 * m + NE], hT[:, k, m * P:m * P + n], router[:, k, :], k == 0, k == KD - 1)
                    i.then_inc(lg_pe.sem, 1)
                    pe.wait_ge(sel_d.sem, sel_d.at(0))
                    for m in range(3):
                        n = ROWS[m]
                        for j in range(m):
                            mm(ps[0:n, 1, 64 + 8 * m:72 + 8 * m], ones[:, 0:n], sel[:, j, :], j == 0, False)
                        mm(ps[0:n, 1, 64 + 8 * m:72 + 8 * m], c("tri")[0:n, 0:n], sel[0:n, m, :], m == 0, True)
                    for m in range(3):
                        i = mm(ps[0:NE, 1, 96:97], sel[0:ROWS[m], m, :], ones[0:ROWS[m], 0:1], m == 0, m == 2)
                    i.then_inc(pos_pe.sem, 1)
                    pe.wait_ge(pos_d.sem, pos_d.at(0))
                    mm(ps[0:NE, 1, 100:101], c("etri")[0:NE, :], nblk[0:NE, :]).then_inc(nb_pe.sem, 1)
                    pe.wait_ge(h2_ev.sem, h2_ev.at(0))
                    for m in range(3):
                        n = ROWS[m]
                        tr(ps[0:NE, 2, m * P:m * P + n], posm[0:n, m, :])
                        i = tr(ps[0:NE, 3, m * P:m * P + n], gate[0:n, m, :])
                    i.then_inc(tp_pe.sem, 1)
                    pe.wait_ge(tp_ev.sem, tp_ev.at(0))
                    pe.wait_ge(nb_d.sem, nb_d.at(0))
                    for m in range(3):
                        n = ROWS[m]
                        mm(ps[0:n, 4, 16 * m:16 * m + NITEM], posT[0:NE, m * P:m * P + n], Mw[0:NE, :], True, False)
                        mm(ps[0:n, 4, 16 * m:16 * m + NITEM], ones[0:NE, 0:n], off[0:NE, :], False, True)
                        mm(ps[0:n, 4, 64 + 16 * m:64 + 16 * m + NITEM], gateT[0:NE, m * P:m * P + n], Mw[0:NE, :])
                    mm(ps[0:1, 4, 128:128 + NITEM], c("eidx")[0:NE, :], Mw[0:NE, :])
                    mm(ps[0:1, 4, 128 + NITEM:129 + NITEM], nblk[0:NE, :], ones[0:NE, 0:1]).then_inc(it_pe.sem, 1)
                    pe.wait_ge(items.sem, items.at(0))
                    pe.sem_inc(used.sem, NU)
                    pe.wait_ge(h2l_ev.sem, 1)
                    n_items = pe.value_load(itemi[0:1, NITEM:NITEM + 1], min_val=1, max_val=NITEM)

                    def gather(w):
                        pe.wait_ge(g_sel.sem, w + 1)
                        for x, part in enumerate((h2h, h2l)):
                            for k in range(KD):
                                for m in range(3):
                                    n = ROWS[m]
                                    i = mm(ps[:, 2 + 2 * x + k // 4, (k % 4) * P:(k % 4) * P + P],
                                           part[0:n, m, k * P:k * P + P], Sel[0:n, m, :], m == 0, m == 2)
                        i.then_inc(g_pe.sem, 1)

                    def combine(w):
                        pe.wait_ge(yS_ev.sem, w + 1)
                        for d in range(KD):
                            if d >= 4:
                                pe.wait_ge(cmb_ev.sem, 8 * w + d - 3)
                            mm(ps[:, CMB_BANK[d % 4], 0:N], yS[:, d * P:d * P + P], SelT[:, :]).then_inc(cmb_pe.sem, 1)

                    gather(0)
                    with pe.Fori(0, n_items) as w:
                        combine(w)
                        pe.wait_ge(g_ev.sem, w + 1)
                        for i, (kind, ch) in enumerate(UNITS):
                            if kind == "A" and ch >= 2:
                                pe.wait_ge(m_g.sem, FCH * w + ch - 1)
                            if kind == "C":
                                pe.wait_ge(m_gl.sem, FCH * w + ch + 1)
                            pe.wait_ge(lo.sem, NU * w + NU + i + 1)
                            wh, wlo = Wh[i % 3], Wl[i % 3]
                            for j in range(4):
                                if kind == "C":
                                    o, xh, xl = ps[:, 6 + j % 2, :], gTh[:, ch % 2, j // 2, :], gTl[:, ch % 2, j // 2, :]
                                    first, last = ch == 0 and j < 2, ch == FCH - 1 and j >= 2
                                else:
                                    k = j + (4 if kind == "B" else 0)
                                    o, xh, xl = ps[:, 2 + ch % 2, :], Xh[:, k, :], Xl[:, k, :]
                                    first, last = k == 0, k == KD - 1
                                mm(o, xh, wh[:, j, :], first, False)
                                mm(o, xh, wlo[:, j, :], False, False)
                                m = mm(o, xl, wh[:, j, :], False, last)
                            m.then_inc(used.sem, 1)
                            if (kind, ch) == ("A", 1):
                                pe.wait_ge(cmb_ev.sem, 8 * w + 8)
                                for m in range(3):
                                    n = ROWS[m]
                                    m = tr(ps[:, 1, m * P:m * P + n], SelG[0:n, m, :])
                                m.then_inc(g_pe.sem, 1)
                            if kind == "C" and ch < FCH - 1 or (kind, ch) == ("A", 1):
                                nx = ch + 1 if kind == "C" else 0
                                pe.wait_ge(m_g.sem, FCH * w + nx + 1)
                                for f in range(2):
                                    m = tr(ps[:, 4 + nx % 2, f * P:f * P + P], gm[:, nx % 2, f * P:f * P + P])
                                m.then_inc(m_t.sem, 1)
                        gather(w + 1)
                    combine(n_items)
            norm(4, 0, KD)
            for k in range(KD):
                pe.wait_ge(h_ev.sem, h_ev.at(4, k + 1))
                for m in range(3):
                    i = tr(ps[0:ROWS[m], 1 + 2 * m + k // 4, (k % 4) * P:(k % 4) * P + P], hT[:, k, m * P:m * P + ROWS[m]])
            i.then_inc(y_pe.sem, 1)

        @block.scalar
        def _(act):
            def fn(out, x, f, **kw):
                return nc.scalar.activation(out, x, f, **kw)

            def copy(out, x, scale=1.0):
                return nc.scalar.activation(out, x, ACT.Copy, scale=scale)

            def norm(idx, done=None):
                if done is None:
                    act.wait_ge(x_done.sem, x_done.at(idx // 4))
                for k in range(KD):
                    if done is not None:
                        act.wait_ge(done.sem, done.at(idx // 2 if idx % 2 else 0, k + 1))
                    fn(hT[:, k, :], xT[:, k, :], ACT.Square).then_inc(sq_ev.sem, 1)
                act.wait_ge(var_ev.sem, var_ev.at(idx))
                fn(srow, srow, ACT.Sqrt).then_inc(sd_ev.sem, 1)

            act.wait_ge(vt_pe0.sem, vt_pe0.at(0))
            copy(vT, ps[:, 2, 0:152]).then_inc(vt_ev0.sem, 1)
            for k in range(KD):
                act.wait_ge(xt_pe.sem, xt_pe.at(0, k + 1))
                copy(xT[:, k, :], ps[:, 4 + k % 4, 0:N]).then_inc(xt_ev.sem, 1)

            for l in range(2):
                norm(2 * l, fy_ev if l == 1 else None)
                act.wait_ge(cv_pe.sem, cv_pe.at(l))
                copy(uext[:, :, T + 3:UE].rearrange("p h (b x) -> p h b x", b=NB)[:, :, :, 0:3],
                     ps[:, 1, 0:96].rearrange("p (h b x) -> p h b x", h=MH, b=NB)).then_inc(cv_ev.sem, 1)
                for g in range(G):
                    act.wait_ge(q_pe.sem, q_pe.at(l, g + 1))
                    copy(qT[:, g, :], ps[:, g, 0:N], HD ** -0.5).then_inc(q_ev.sem, 1)
                act.wait_ge(kv_ev.sem, kv_ev.at(l))
                fn(gns[:, 0:2, :], kv[:, 0:2, 768:792], ACT.Sigmoid)
                fn(gns[0:NS, 2, :], kv[0:NS, 2, 768:792], ACT.Sigmoid).then_inc(gs_ev.sem, 1)
                for h in range(MH):
                    act.wait_ge(o_pe.sem, o_pe.at(l, h + 1))
                    fn(oT[:, h, :], ps[:, (6 + h) % 8, 0:N], ACT.Sigmoid).then_inc(o_ev.sem, 1)
                act.wait_ge(kt_pe.sem, kt_pe.at(l))
                copy(kTp[:, :, :], ps[:, 0, :].rearrange("p (r x) -> p r x", r=2))
                copy(kTn[:, :, :], ps[:, 1, 0:64].rearrange("p (r x) -> p r x", r=2)).then_inc(kt_ev.sem, 1)
                act.wait_ge(uc_d.sem, uc_d.at(l))
                fn(ucT[:, :, :], ucT[:, :, :], ACT.Silu).then_inc(uc_a.sem, 1)
                for i in range(8):
                    act.wait_ge(mqk_pe.sem, mqk_pe.at(l, i + 1))
                    dst = (mqT, mkT)[i // 4][:, i % 4, :]
                    copy(dst, ps[:, 4 + i % 4, 0:N], (MD ** -0.5, 1.0)[i // 4]).then_inc(mqk_ev.sem, 1)
                act.wait_ge(lf_d.sem, lf_d.at(l))
                fn(rows[0:MH, 1, :], rows[0:MH, 1, :], ACT.Exp, scale=-1.0).then_inc(lf_a.sem, 1)
                act.wait_ge(lf_d2.sem, lf_d2.at(l))
                fn(rows[0:MH, 1, :], rows[0:MH, 1, :], ACT.Ln).then_inc(lf_a2.sem, 1)
                kvu = take(4 * 9 * P, Y_at).rearrange("p (u s x) -> p u s x", u=4, s=9)
                for s in range(0, 9, 2):
                    act.wait_ge(ct_pe.sem, ct_pe.at(l, s + 1))
                    copy(kvu[:, :, s, :], ps[:, 4, :].rearrange("p (u x) -> p u x", u=4)).then_inc(ct_a.sem, 1)
                act.wait_ge(row_d.sem, row_d.at(l))
                fn(R[0:MH, :], rows[0:MH, 1, :], ACT.Exp)
                copy(R[32:32 + MH, :], rows[0:MH, 3, :])
                fn(R[64:64 + MH, :], rows[0:MH, 6, :], ACT.Exp, scale=-1.0)
                copy(mout[0:MH, :], rows[0:MH, 6, T - 1:N:TS])
                fn(R[96:96 + MH, :], rows[0:MH, 5, :], ACT.Exp).then_inc(row_a.sem, 1)
                for v in range(2):
                    act.wait_ge(c_ev.sem, c_ev.at(l, v + 1))
                    fn(hid[:, v, :, 0:NC_BLK], ps[:, 6 + v, 0:270].rearrange("p (s x) -> p s x", s=18),
                       ACT.Gelu_apprx_tanh, bias=cvec[:, v:v + 1]).then_inc(hid_ev.sem, 1)
                act.wait_ge(kc_pe.sem, kc_pe.at(l))
                copy(KcT[:, :, :], ps[:, 4, 0:144].rearrange("p (s x) -> p s x", s=9))
                for h in range(KVH):
                    i = copy(VcS[0:16, :, 64 * h:64 * h + 64], ps[0:16, 5 + h, :].rearrange("p (b d) -> p b d", b=NB))
                i.then_inc(kc_a.sem, 1)

                def gate_sigmoid(n, bank):
                    x, d = GATE_TILES[n]
                    act.wait_ge(gt_pe.sem, gt_pe.at(l, n + 1))
                    fn(gsig[d // 4][:, x, d % 4, :], ps[:, bank, 0:N], ACT.Sigmoid).then_inc(gt_ev.sem, 1)

                gate_sigmoid(0, 0)
                for q in range(hq):
                    act.wait_ge(cx_d.sem, cx_d.at(l, q + 1))
                    x = pc[:, q, :].rearrange("p (h n) -> p h n", h=H)[:, :, 0:NC_BLK]
                    fn(x, x, ACT.Exp).then_inc(cx_a.sem, 1)
                gate_sigmoid(1, 1)
                for q in range(hq):
                    act.wait_ge(cx_t.sem, cx_t.at(l, q + 1))
                    copy(PcT[:, q, :], ps[:, 2 + q, 0:P]).then_inc(pct_ev.sem, 1)

                for i in range(17):
                    if i < 16:
                        ext = (i // H + 1) * P
                        act.wait_ge(nm_ev.sem, nm_ev.at(l, i + 1))
                        for r in range(2):
                            x = Pb[:, i % 2, r, 0:ext]
                            e = fn(x, x, ACT.Exp, bias=nm[:, i % 2, r:r + 1], accum_out=sums[:, i % 2, r:r + 1])
                        e.then_inc(ex_ev.sem, 1)
                    if i >= 1:
                        j = i - 1
                        w = (j // H + 1) * P
                        act.wait_ge(t_pe.sem, t_pe.at(l, j + 1))
                        if j >= 2:
                            act.wait_ge(pv_pe.sem, pv_pe.at(l, j - 1))
                        copy(PT[:, j % 2, :, 0:j // H + 1, :],
                             ps[:, 6 + j % 2, :].rearrange("p (r k x) -> p r k x", r=2, k=2)[:, :, 0:j // H + 1, :]
                             ).then_inc(pt_ev.sem, 1)
                        if j % 2 == 1:
                            gate_sigmoid(2 + j // 2, 2 + j // 2 % 2)
                for q in range(hq):
                    act.wait_ge(pv_pe.sem, pv_pe.at(l, H * (q + 1)))
                    copy(oNT[:, :, q * P:q * P + P], ps[:, q, :].rearrange("p (g x) -> p g x", g=G)).then_inc(on_ev.sem, 1)
                for t in range(2):
                    for i in range(2):
                        act.wait_ge(skt_pe.sem, skt_pe.at(l, 4 * t + i + 1))
                        copy(kTs[:, 0, 2 * i:2 * i + 2, :], ps[:, 2 + i, :].rearrange("p (b x) -> p b x", b=2)
                             ).then_inc(skt_a.sem, 1)
                    act.wait_ge(snm_ev.sem, snm_ev.at(l, t + 1))
                    fn(Psc[:, 0:NC_BLK], Psc[:, 0:NC_BLK], ACT.Exp, bias=snm[:, 0:1], accum_out=ssm[:, 0:1])
                    for r in range(2):
                        e = fn(Ps[:, r, :], Ps[:, r, :], ACT.Exp, bias=snm[:, 1 + r:2 + r], accum_out=ssm[:, 1 + r:2 + r])
                    e.then_inc(sex_ev.sem, 1)
                    gate_sigmoid((10, 14)[t], 3)
                    act.wait_ge(st_pe.sem, st_pe.at(l, t + 1))
                    copy(PT[:, 0, :, :, :], ps[:, 0, :].rearrange("p (r k x) -> p r k x", r=2, k=2))
                    copy(PTn[0:NS, 0:2 * P], ps[0:NS, 1, 0:2 * P])
                    copy(PTn[0:16, 2 * P:3 * P], ps[0:16, 1, 2 * P:3 * P]).then_inc(spt_ev.sem, 1)
                    gate_sigmoid((11, 15)[t], 4)
                    if t == 0:
                        gate_sigmoid(12, 3)
                        gate_sigmoid(13, 5)
                act.wait_ge(rt_pe.sem, rt_pe.at(l))
                copy(RT[:, 0:2, :], ps[:, 6, 0:2 * P].rearrange("p (m x) -> p m x", m=2))
                copy(RT[0:NS, 2, :], ps[0:NS, 6, 2 * P:3 * P]).then_inc(rt_ev.sem, 1)
                copy(wcb[:, :, :], ps[:, 7, 0:NS].rearrange("p (h b) -> p h b", h=MH))
                copy(C0[:, :, :, 128], ps[:, 7, 64:96].rearrange("p (b h) -> p b h", b=NB)).then_inc(wcb_ev.sem, 1)
                for m in range(3):
                    act.wait_ge(vt_pe.sem, vt_pe.at(l, m + 1))
                    n = ROWS[m]
                    copy(mv[0:n, m, :, 0:MD], ps[0:n, m, :].rearrange("p (h e) -> p h e", h=MH)).then_inc(vt_ev.sem, 1)
                for h in range(MH):
                    act.wait_ge(md_ev.sem, md_ev.at(l, h + 1))
                    fn(Db[:, 0:T], Db[:, 0:T], ACT.Exp, scale=-1.0, bias=RT[:, 0, 32 + h:33 + h])
                    fn(Db[:, T:T + P], Db[:, T:T + P], ACT.Exp, scale=-1.0, bias=RT[:, 1, 32 + h:33 + h])
                    fn(Db[0:NS, 384:416], Db[0:NS, 384:416], ACT.Exp, scale=-1.0, bias=RT[0:NS, 2, 32 + h:33 + h]
                       ).then_inc(me_ev.sem, 1)
                act.wait_ge(cp_pe.sem, cp_pe.at(l))
                copy(Cp[:, 0:3, :], ps[:, 4, 0:387].rearrange("p (h e) -> p h e", h=3))
                copy(Cp[:, 3, :], ps[:, 1, 0:129]).then_inc(cp_ev.sem, 1)
                act.wait_ge(var2_ev.sem, var2_ev.at(l))
                fn(ssr[:, :, :], ssr[:, :, :], ACT.Sqrt).then_inc(sd2_ev.sem, 1)
                act.wait_ge(no_pe.sem, no_pe.at(l))
                copy(nout[0:NS, 0:P], ps[0:NS, 4, 0:P])
                copy(nout[0:MH, P:2 * P], ps[0:MH, 4, P:2 * P])
                copy(cvo[0:27, :], ps[0:27, 5, :]).then_inc(no_ev.sem, 1)
                if l == 0:
                    norm(1, wo_ev)
                    act.wait_ge(st_state.sem, st_state.at(0))
                    for f in range(22):
                        act.wait_ge(ff_pe.sem, ff_pe.at(0, f + 1))
                        if f >= 2:
                            act.wait_ge(ff_g.sem, ff_g.at(0, f - 1))
                        fn(sil[:, f % 2, 0, :], ps[:, 1 + 2 * (f % 3), 0:N], ACT.Silu).then_inc(ff_sil.sem, 1)
                else:
                    norm(3, wo_ev)
                    act.wait_ge(lg_pe.sem, lg_pe.at(0))
                    act.wait_ge(st_kv.sem, st_kv.at(1))
                    act.wait_ge(st_state.sem, st_state.at(1))
                    for m in range(3):
                        n = ROWS[m]
                        i = copy(h2h[0:n, m, :].rearrange("p (b x) -> p b x", b=2), ps[0:n, 2 + 2 * m:4 + 2 * m, :])
                    i.then_inc(h2_ev.sem, 1)
                    act.wait_ge(lgx_d.sem, lgx_d.at(0))
                    fn(gx[:, :, :], gx[:, :, :], ACT.Exp).then_inc(lgx_a.sem, 1)
                    act.wait_ge(tp_pe.sem, tp_pe.at(0))
                    copy(posT[0:NE, :], ps[0:NE, 2, 0:N])
                    copy(gateT[0:NE, :], ps[0:NE, 3, 0:N]).then_inc(tp_ev.sem, 1)
                    act.wait_ge(items.sem, items.at(0))
                    n_items = act.value_load(itemi[0:1, NITEM:NITEM + 1], min_val=1, max_val=NITEM)
                    with act.Fori(0, n_items) as w:
                        def high(i):
                            s = i % NRAW
                            uses = 6 if s < 3 else 5
                            act.wait_ge(raw_in[s].sem, w * (32 * uses) + 32 * (i // NRAW + 1))
                            act.wait_ge(used.sem, NU * w + NU + i - 2)
                            copy(Wh[i % 3], raw[s].rearrange("p (k n) -> p k n", k=4)).then_inc(hi.sem, 1)

                        high(0)
                        high(1)
                        act.wait_ge(g_pe.sem, 2 * w + 1)
                        for x, part in enumerate((Xh, Xl)):
                            i = copy(part.rearrange("p (b k) s -> p b (k s)", b=2), ps[:, 2 + 2 * x:4 + 2 * x, :])
                        i.then_inc(g_ev.sem, 1)
                        high(2)
                        for ch in range(FCH):
                            b = UNIT_AT["B", ch]
                            act.wait_ge(used.sem, NU * w + NU + b + 1)
                            if ch >= 2:
                                act.wait_ge(m_g.sem, FCH * w + ch - 1)
                            fn(sl[:, ch % 2, :], ps[:, 2 + ch % 2, 0:256], ACT.Silu).then_inc(m_sil.sem, 1)
                            if ch < FCH - 1:
                                high(b + (2 if ch == 0 else 3))
                            if ch == 0:
                                high(UNIT_AT["C", 0])
                            act.wait_ge(m_t.sem, FCH * w + ch + 1)
                            copy(gTh[:, ch % 2, :, :], ps[:, 4 + ch % 2, 0:256].rearrange("p (f x) -> p f x", f=2)
                                 ).then_inc(m_gh.sem, 1)
                            if ch == 0:
                                act.wait_ge(g_pe.sem, 2 * w + 2)
                                copy(SelT[:, :], ps[:, 1, 0:N])
                            if ch < FCH - 1:
                                if ch > 0:
                                    high(UNIT_AT["C", ch])
                                if ch < FCH - 2:
                                    high(UNIT_AT["A", ch + 2])
                                else:
                                    high(NU - 1)
                        act.wait_ge(used.sem, NU * w + 2 * NU)
                        copy(yS[:, :].rearrange("p (b x) -> p b x", b=2), ps[:, 6:8, :]).then_inc(yS_ev.sem, 1)
            norm(4)
            act.wait_ge(y_pe.sem, y_pe.at(0))
            for m in range(3):
                n = ROWS[m]
                e = copy(ytok[0:n, m, :].rearrange("p (b x) -> p b x", b=2), ps[0:n, 1 + 2 * m:3 + 2 * m, :])
            e.then_inc(y_ev.sem, 1)

        @block.vector
        def _(dve):
            V = nc.vector

            def tt(out, x, y, op):
                return V.tensor_tensor(out, x, y, op)

            def bc(x, n):
                return bass.AP(x.tensor, x.offset, list(x.ap[:-1]) + [[0, n]]) if x.ap[-1][1] == 1 else x

            def rep(x, n):
                return bass.AP(x.tensor, x.offset, list(x.ap) + [[0, n]])

            def norm(idx, col):
                dve.wait_ge(ss_pe0.sem, ss_pe0.at(idx))
                V.tensor_scalar(srow, ps[:, 4, 0:N], 1.0 / D, EPS, ALU.mult, ALU.add).then_inc(var_ev.sem, 1)
                dve.wait_ge(sd_ev.sem, sd_ev.at(idx))
                V.reciprocal(srow, srow)
                dve.drain()
                for k in range(KD):
                    V.scalar_tensor_tensor(out=hT[:, k, :], in0=xT[:, k, :], scalar=vT[:, col + k:col + k + 1],
                                               in1=srow, op0=ALU.mult, op1=ALU.mult).then_inc(h_ev.sem, 1)

            def x_is_done():
                dve.drain()
                dve.sem_inc(x_done.sem, 1)

            dve.wait_ge(w8_pe.sem, w8_pe.at(0))
            for i in range(2):
                m = tt(w8[0:H, 272 * i:272 * i + 272], ps[0:H, i, 0:272], c("future")[0:H, 272 * i:272 * i + 272], ALU.add)
            m.then_inc(w8_ev.sem, 1)
            V.memset(ssum[:, :, :], 1.0)
            V.memset(R, 0.0)
            V.memset(Qz[:, :, :], 0.0)
            dve.wait_ge(bp1_pe.sem, bp1_pe.at(0))
            own = c("own").rearrange("p (m x) -> p m x", m=2)
            for t in range(2):
                V.tensor_copy(biasS[:, t, 0:PAST], ps[:, 3, 0:PAST])
                tt(biasS[:, t, PAST:N], ps[:, 3, PAST:N], own[:, t, :], ALU.add)
            V.tensor_copy(biasSc, ps[:, 3, N:N + NC_BLK]).then_inc(bp_ev.sem, 1)
            dve.wait_ge(xt_ev.sem, xt_ev.at(0, 8))
            dve.sem_inc(x_done.sem, 1)
            dve.wait_ge(bp2_pe.sem, bp2_pe.at(0))
            V.tensor_copy(biasP[:, :, :].rearrange("p (i h) x -> p i (h x)", i=4), ps[:, 4:8, :]).then_inc(bp_ev.sem, 1)
            dve.wait_ge(bp3_pe.sem, bp3_pe.at(0))
            for q in range(2):
                m = V.tensor_copy(biasC[:, q, :, :], ps[:, 3, 256 * q:256 * q + 120].rearrange("p (h n) -> p h n", h=H))
            m.then_inc(bp_ev.sem, 1)
            V.memset(uext[:, :, 0:3], 0.0)

            for l in range(2):
                dve.wait_ge(vt_ev0.sem, vt_ev0.at(0))
                norm(2 * l, V_MIX + 8 * l)
                if l == 1:
                    dve.wait_ge(st_kv.sem, st_kv.at(0))
                for f in range(2):
                    for m in range(3):
                        dve.wait_ge(kv_pe.sem, kv_pe.at(l, 3 * f + m + 1))
                        n = ROWS[m]
                        V.tensor_copy(kv[0:n, m, KV_HALF * f:KV_HALF * f + KV_HALF],
                                      ps[0:n, (4 + 3 * f + m) % 8, 0:KV_HALF]).then_inc(kv_ev.sem, 1)
                for h in range(MH):
                    dve.wait_ge(u_pe.sem, u_pe.at(l, h + 1))
                    V.tensor_copy(uext[:, h, 3:3 + T], ps[:, 2 + h, 0:T])
                    V.tensor_copy(sview(None, h)[:, :, 3:7], ps[:, 2 + h, T:N].rearrange("p (b t) -> p b t", b=NB)
                                  ).then_inc(u_ev.sem, 1)
                dve.wait_ge(cv_ev.sem, cv_ev.at(l))
                dve.drain()
                for h in range(MH):
                    V.tensor_copy(us[:, h, :].rearrange("p (b t) -> p b t", b=NB), sview(None, h)[:, :, 3:7])
                    x = uext[:, h, T:T + 3]
                    i = V.tensor_copy(cstage[:, h, :].rearrange("p (s x) -> p s x", x=3),
                                      bass.AP(x.tensor, x.offset, [x.ap[0], [7, NB + 1], [1, 3]]))
                i.then_inc(cst_ev.sem, 1)
                for j in range(4):
                    for h in range(MH):
                        w = vT[:, V_CW + (4 * l + j) * 4 + h:V_CW + (4 * l + j) * 4 + h + 1]
                        uq = ucT[:, h, T:N].rearrange("p (b t) -> p b t", b=NB)
                        if j == 0:
                            b = vT[:, V_CB + 4 * l + h:V_CB + 4 * l + h + 1]
                            V.tensor_scalar(ucT[:, h, 0:T], uext[:, h, 0:T], w, b, ALU.mult, ALU.add)
                            i = V.tensor_scalar(uq, sview(None, h)[:, :, 0:4], w, b, ALU.mult, ALU.add)
                        else:
                            V.scalar_tensor_tensor(out=ucT[:, h, 0:T], in0=uext[:, h, j:j + T], scalar=w,
                                                   in1=ucT[:, h, 0:T], op0=ALU.mult, op1=ALU.add)
                            i = V.scalar_tensor_tensor(out=uq, in0=sview(None, h)[:, :, j:j + 4], scalar=w,
                                                       in1=uq, op0=ALU.mult, op1=ALU.add)
                    if j < 3:
                        dve.drain()
                i.then_inc(uc_d.sem, 1)
                dve.wait_ge(if_pe.sem, if_pe.at(l))
                V.tensor_scalar(srow[0:MH, :], ps[0:MH, 2, 0:N], gbias[0:MH, 2 * l:2 * l + 1], None, ALU.add)
                V.tensor_scalar(Mrow[0:MH, :], ps[0:MH, 3, 0:N], gbias[0:MH, 2 * l + 1:2 * l + 2], None, ALU.add
                                ).then_inc(if_ev.sem, 1)
                dve.wait_ge(q_ev.sem, q_ev.at(l))
                for t in range(2):
                    for v in range(KVH):
                        rr = slice(64 * v, 64 * v + 64)
                        i = V.tensor_copy(Qz[rr, t, :].rearrange("p (b v g) -> p b v g", v=KVH, g=G)[:, :, v, :],
                                          qT[rr, :, T + 16 * t:T + 16 * t + 16].rearrange("p g b -> p b g"))
                i.then_inc(qz_ev.sem, 1)
                V.memset(pc[:, :, :], 0.0)
                V.memset(hid[:, :, :, 15:16], 0.0)
                li, f = srow[0:MH, :], Mrow[0:MH, :]
                r = [rows[0:MH, i, :] for i in range(7)]
                dve.drain()
                V.tensor_scalar(r[0], f, 0.0, None, ALU.min)
                V.scalar_tensor_tensor(out=r[1], in0=f, scalar=-1.0, in1=f, op0=ALU.mult, op1=ALU.max).then_inc(lf_d.sem, 1)
                dve.wait_ge(lf_a.sem, lf_a.at(l))
                V.tensor_scalar(r[1], r[1], 1.0, None, ALU.add).then_inc(lf_d2.sem, 1)
                dve.wait_ge(m0_in.sem, m0_in.at(l))
                V.memset(r[4][:, 0:T], 0.0)
                V.tensor_copy(r[4][:, T:N].rearrange("p (b t) -> p b t", b=NB), rep(m0c[0:MH, :], TS))
                kvu = take(4 * 9 * P, Y_at).rearrange("p (u s x) -> p u s x", u=4, s=9)
                for s in range(1, 9, 2):
                    dve.wait_ge(ct_pe.sem, ct_pe.at(l, s + 1))
                    V.tensor_copy(kvu[:, :, s, :], ps[:, 5, :].rearrange("p (u x) -> p u x", u=4)).then_inc(ct_d.sem, 1)
                dve.wait_ge(lf_a2.sem, lf_a2.at(l))
                tt(r[0], r[0], r[1], ALU.subtract)
                dve.drain()
                V.tensor_tensor_scan(r[2], c("keep")[0:MH, :], r[0], 0.0, ALU.mult, ALU.add)
                dve.drain()
                tt(r[3], li, r[2], ALU.subtract)
                dve.drain()
                tt(r[5], r[3], r[4], ALU.max)
                dve.drain()
                V.tensor_tensor_scan(f, c("reset")[0:MH, :], r[5], 0.0, ALU.add, ALU.max)
                dve.drain()
                tt(r[6], r[2], f, ALU.add)
                tt(r[1], r[4], f, ALU.subtract)
                V.tensor_scalar(r[5][:, 0:T], r[3][:, 0:T], f[:, T - 1:T], None, ALU.subtract)
                last = f[:, T + TS - 1:N:TS]
                tt(r[5][:, T:N].rearrange("p (b t) -> p b t", b=NB), r[3][:, T:N].rearrange("p (b t) -> p b t", b=NB),
                   rep(last, TS), ALU.subtract).then_inc(row_d.sem, 1)
                for v in range(2):
                    dve.wait_ge(hid_pe.sem, hid_pe.at(l, v + 1))
                    V.tensor_copy(cvec[:, v:v + 1], ps[:, 6 + v, 300:301]).then_inc(c_ev.sem, 1)
                dve.wait_ge(hid_ev.sem, hid_ev.at(l))
                x = hid[:, 1, 8:18:9, :]
                V.tensor_copy(hidr[:, :, :].rearrange("p h (g n) -> p h g n", g=G),
                              bass.AP(x.tensor, x.offset, [x.ap[0], x.ap[1], [0, G], x.ap[2]])).then_inc(hidr_ev.sem, 1)
                dve.wait_ge(kc_pe.sem, kc_pe.at(l))
                x, y = ps[:, 7, 0:64], c("hrow")
                tt(VcZ[:, :, :], bass.AP(x.tensor, x.offset, [x.ap[0], [0, H], x.ap[1]]), rep(y, 64), ALU.mult
                   ).then_inc(kc_d.sem, 1)
                dve.drain()
                dve.wait_ge(gs_ev.sem, gs_ev.at(l))
                for q in range(hq):
                    x = pc[:, q, :].rearrange("p (h n) -> p h n", h=H)[:, :, 0:NC_BLK]
                    dve.wait_ge(cs_pe.sem, cs_pe.at(l, q + 1))
                    tt(x, ps[:, 2 + q, 0:P].rearrange("p (h n) -> p h n", h=H)[:, :, 0:NC_BLK], biasC[:, q, :, :], ALU.add)
                    dve.drain()
                    V.tensor_reduce(cmx, x, AX.X, ALU.max)
                    dve.drain()
                    tt(x, x, rep(cmx, NC_BLK), ALU.subtract).then_inc(cx_d.sem, 1)
                    dve.wait_ge(cx_a.sem, cx_a.at(l, q + 1))
                    V.tensor_reduce(csm, x, AX.X, ALU.add)
                    dve.drain()
                    V.reciprocal(csm, csm)
                    dve.drain()
                    V.scalar_tensor_tensor(out=csm, in0=csm, scalar=c("cvalid")[:, q:q + 1], in1=gns[:, q, 0:24:3],
                                           op0=ALU.mult, op1=ALU.mult)
                    dve.drain()
                    tt(x, x, rep(csm, NC_BLK), ALU.mult).then_inc(cx_n.sem, 1)
                    dve.drain()

                def add(i):
                    q, h = i // H, i % H
                    ext = (q + 1) * P
                    dve.wait_ge(s_pe.sem, s_pe.at(l, i + 1))
                    if i >= 2:
                        dve.wait_ge(t_pe.sem, t_pe.at(l, i - 1))
                    x = Pb[:, i % 2, :, 0:ext]
                    b = biasP[:, h, T - ext:T]
                    tt(x, ps[:, 4 + i % 2, :].rearrange("p (r x) -> p r x", r=2)[:, :, 0:ext],
                       bass.AP(b.tensor, b.offset, [b.ap[0], [0, 2], b.ap[1]]), ALU.add).then_inc(sa_ev.sem, 1)
                    dve.drain()
                    V.tensor_reduce(nm[:, i % 2, :], x, AX.X, ALU.max, negate=True).then_inc(nm_ev.sem, 1)

                def scale(i):
                    q, h = i // H, i % H
                    g = gg[:, i % 2, :]
                    x = Pb[:, i % 2, :, 0:(q + 1) * P]
                    dve.wait_ge(ex_ev.sem, ex_ev.at(l, i + 1))
                    V.reciprocal(g, sums[:, i % 2, :])
                    dve.drain()
                    tt(g, g, gns[:, q, 3 * h + 1:3 * h + 3], ALU.mult)
                    dve.drain()
                    tt(x, x, rep(g, (q + 1) * P), ALU.mult).then_inc(p_ev.sem, 1)

                add(0)
                for i in range(16):
                    if i < 15:
                        add(i + 1)
                    scale(i)
                dve.wait_ge(gsS_in.sem, gsS_in.at(l))
                for t in range(2):
                    for i in range(2):
                        dve.wait_ge(skt_pe.sem, skt_pe.at(l, 4 * t + i + 3))
                        V.tensor_copy(kTs[:, 1, 2 * i:2 * i + 2, :], ps[:, 4 + i, :].rearrange("p (b x) -> p b x", b=2)
                                      ).then_inc(skt_d.sem, 1)
                    dve.wait_ge(ss_pe.sem, ss_pe.at(l, t + 1))
                    dve.drain()
                    V.memset(Psc[:, 15:16], 0.0)
                    b = biasS[:, t, :]
                    tt(Ps[:, :, :], ps[:, 6:8, 0:N], bass.AP(b.tensor, b.offset, [b.ap[0], [0, 2], b.ap[1]]), ALU.add)
                    tt(Psc[:, 0:NC_BLK], ps[:, 7, N:N + NC_BLK], biasSc, ALU.add).then_inc(sadd.sem, 1)
                    dve.drain()
                    V.tensor_reduce(snm[:, 1:3], Ps[:, :, :], AX.X, ALU.max, negate=True)
                    V.tensor_reduce(snm[:, 0:1], Psc[:, 0:NC_BLK], AX.X, ALU.max, negate=True).then_inc(snm_ev.sem, 1)
                    dve.wait_ge(sex_ev.sem, sex_ev.at(l, t + 1))
                    V.reciprocal(sgg, ssm)
                    dve.drain()
                    tt(sgg, sgg, gS[:, t, :], ALU.mult)
                    dve.drain()
                    tt(Ps[:, :, :], Ps[:, :, :], rep(sgg[:, 1:3], N), ALU.mult)
                    V.tensor_scalar(Psc[:, 0:NC_BLK], Psc[:, 0:NC_BLK], sgg[:, 0:1], None, ALU.mult).then_inc(sps_ev.sem, 1)
                    dve.wait_ge(spv_pe.sem, spv_pe.at(l, t + 1))
                    for v in range(KVH):
                        rr = slice(64 * v, 64 * v + 64)
                        i = V.tensor_copy(oNT[rr, :, T + 16 * t:T + 16 * t + 16].rearrange("p g b -> p b g"),
                                          ps[rr, 2, 0:P].rearrange("p (b v g) -> p b v g", v=KVH, g=G)[:, :, v, :])
                    i.then_inc(son_ev.sem, 1)
                dve.wait_ge(rt_ev.sem, rt_ev.at(l))
                for m in range(3):
                    n = ROWS[m]
                    dve.wait_ge(vt_pe.sem, vt_pe.at(l, 4 + m))
                    if m == 0:
                        V.memset(mv[:, :, :, 128:129], 1.0)
                    tt(mk[0:n, m, :, :], ps[0:n, 3 + m, :].rearrange("p (h e) -> p h e", h=MH),
                       rep(RT[0:n, m, 96:96 + MH], MD), ALU.mult).then_inc(ktk_ev.sem, 1)
                cau, caus = c("causal"), c("causal_s")[0:NS, :]

                def decay(h):
                    dve.wait_ge(mb_pe.sem, mb_pe.at(l, h + 1))
                    dve.drain()
                    tt(Db[:, 0:P], ps[:, 6, 0:P], cau, ALU.add)
                    V.tensor_copy(Db[:, P:T], ps[:, 6, P:T])
                    tt(Db[:, T:T + P], ps[:, 6, P:T], cau, ALU.add)
                    tt(Db[0:NS, 384:416], ps[0:NS, 6, T:N], caus, ALU.add).then_inc(md_ev.sem, 1)

                def weight(h):
                    dve.wait_ge(me_ev.sem, me_ev.at(l, h + 1))
                    if h >= 1:
                        dve.wait_ge(num_pe.sem, num_pe.at(l, h))
                    tt(Ab[:, 0:384], ps[:, 7, 0:384], Db[:, 0:384], ALU.mult)
                    tt(Ab[0:NS, 384:416], ps[0:NS, 7, 384:416], Db[0:NS, 384:416], ALU.mult).then_inc(ma_ev.sem, 1)

                decay(0)
                weight(0)
                for h in range(MH):
                    if h + 1 < MH:
                        decay(h + 1)
                        weight(h + 1)
                    dve.wait_ge(num_pe.sem, num_pe.at(l, h + 1))
                    n = 2 * (h % 2)
                    nd = ps[:, n, 0:258].rearrange("p (m e) -> p m e", m=2)
                    dve.drain()
                    V.tensor_copy(stmp[0:NS, 0:129], ps[0:NS, n + 1, 0:129])
                    V.scalar_tensor_tensor(out=dn[:, 0:2], in0=nd[:, :, 128], scalar=-1.0, in1=RT[:, 0:2, 64 + h],
                                           op0=ALU.mult, op1=ALU.max)
                    dve.drain()
                    V.scalar_tensor_tensor(out=stmp[0:NS, 0:129], in0=ps[0:NS, n + 1, 129:258], scalar=RT[0:NS, 2, h:h + 1],
                                           in1=stmp[0:NS, 0:129], op0=ALU.mult, op1=ALU.add)
                    dve.drain()
                    V.scalar_tensor_tensor(out=dn[0:NS, 2:3], in0=stmp[0:NS, 128:129], scalar=-1.0,
                                           in1=RT[0:NS, 2, 64 + h:65 + h], op0=ALU.mult, op1=ALU.max)
                    tt(dn2[:, 0:2], dn[:, 0:2], nd[:, :, 128], ALU.max)
                    dve.drain()
                    tt(dn2[0:NS, 2:3], dn[0:NS, 2:3], stmp[0:NS, 128:129], ALU.max)
                    dve.drain()
                    V.reciprocal(dn3[:, 0:2], dn2[:, 0:2])
                    V.reciprocal(dn3[0:NS, 2:3], dn2[0:NS, 2:3])
                    dve.drain()
                    V.tensor_scalar(hm[0:NS, 2, h, :], stmp[0:NS, 0:128], dn3[0:NS, 2:3], None, ALU.mult)
                    tt(hm[:, 0:2, h, :], nd[:, :, 0:128], rep(dn3[:, 0:2], MD), ALU.mult).then_inc(mh_ev.sem, 1)
                dve.drain()
                tt(hsq[:, 0:2, :, :], hm[:, 0:2, :, :], hm[:, 0:2, :, :], ALU.mult)
                tt(hsq[0:NS, 2, :, :], hm[0:NS, 2, :, :], hm[0:NS, 2, :, :], ALU.mult)
                dve.drain()
                V.tensor_reduce(ssum[:, 0:2, :], hsq[:, 0:2, :, :], AX.X, ALU.add)
                V.tensor_reduce(ssum[0:NS, 2, :], hsq[0:NS, 2, :, :], AX.X, ALU.add)
                dve.drain()
                V.tensor_scalar(ssr[:, :, :], ssum[:, :, :], 1.0 / MD, EPS, ALU.mult, ALU.add).then_inc(var2_ev.sem, 1)
                dve.wait_ge(wcb_ev.sem, wcb_ev.at(l))
                for h in range(MH):
                    dve.wait_ge(cn_pe.sem, cn_pe.at(l, h + 1))
                    dve.wait_ge(cs_ev.sem, cs_ev.at(l))
                    for i, (b0, b1) in enumerate(((0, 3), (3, 6), (6, 8))):
                        x = C0[:, b0:b1, h, :]
                        m = tt(x, x, ps[:, CN_BANK[h % 2][i], 0:129 * (b1 - b0)].rearrange("p (b e) -> p b e", e=129), ALU.add)
                    m.then_inc(cn_ev.sem, 1)
                dve.wait_ge(sd2_ev.sem, sd2_ev.at(l))
                V.reciprocal(ssi[:, :, :], ssr[:, :, :])
                dve.drain()
                tt(hm[:, 0:2, :, :], hm[:, 0:2, :, :], rep(ssi[:, 0:2, :], MD), ALU.mult)
                tt(hm[0:NS, 2, :, :], hm[0:NS, 2, :, :], rep(ssi[0:NS, 2, :], MD), ALU.mult).then_inc(hn_ev.sem, 1)
                dve.wait_ge(o_ev.sem, o_ev.at(l))
                for h in range(MH):
                    dve.wait_ge(om_pe.sem, om_pe.at(l, h + 1))
                    V.scalar_tensor_tensor(out=omT[:, h, :], in0=ps[:, h, 0:N], scalar=vT[:, V_MN + 4 * l + h:V_MN + 4 * l + h + 1],
                                           in1=oT[:, h, :], op0=ALU.mult, op1=ALU.mult).then_inc(om_ev.sem, 1)
                dve.wait_ge(gt_ev.sem, gt_ev.at(l))
                for d in range(8):
                    dve.wait_ge(f_pe.sem, f_pe.at(l, d + 1))
                    b = 2 * (d % 4)
                    x = gsig[d // 4][:, :, d % 4, :]
                    tt(x, x, ps[:, b:b + 2, 0:N], ALU.mult)
                    dve.drain()
                    tt(merged[:, d, :], x[:, 0, :], x[:, 1, :], ALU.add).then_inc(f_ev.sem, 1)
                for d in range(8):
                    dve.wait_ge(wo_pe.sem, wo_pe.at(l, d + 1))
                    tt(xT[:, d, :], xT[:, d, :], ps[:, d % 4, 0:N], ALU.add).then_inc(wo_ev.sem, 1)
                dve.drain()
                if l == 0:
                    norm(1, V_FFN)
                    dve.wait_ge(st_state.sem, st_state.at(0))
                    for f in range(22):
                        dve.wait_ge(ff_sil.sem, ff_sil.at(0, f + 1))
                        tt(gT[:, f, :], sil[:, f % 2, 0, :], ps[:, 2 + 2 * (f % 3), 0:N], ALU.mult).then_inc(ff_g.sem, 1)
                    for d in range(8):
                        dve.wait_ge(fy_pe.sem, fy_pe.at(0, d + 1))
                        tt(xT[:, d, :], xT[:, d, :], ps[:, d % 4, 0:N], ALU.add).then_inc(fy_ev.sem, 1)
                    dve.drain()
                else:
                    norm(3, V_FFN + 8)
                    dve.wait_ge(st_state.sem, st_state.at(1))
                    dve.wait_ge(st_kv.sem, st_kv.at(1))

                    def mid(x, n):
                        return bass.AP(x.tensor, x.offset, [x.ap[0], x.ap[1], [0, n], x.ap[2]])

                    dve.wait_ge(h2_ev.sem, 1)
                    for m in range(3):
                        n = ROWS[m]
                        i = tt(h2l[0:n, m, :].rearrange("p (b x) -> p b x", b=2), ps[0:n, 2 + 2 * m:4 + 2 * m, :],
                               h2h[0:n, m, :].bitcast(F32).rearrange("p (b x) -> p b x", b=2), ALU.subtract)
                    i.then_inc(h2l_ev.sem, 1)
                    V.memset(lg[:, :, :], 0.0)
                    dve.drain()
                    dve.wait_ge(lg_pe.sem, lg_pe.at(0))
                    V.tensor_copy(lg[:, 0:2, :], ps[:, 1, 0:16].rearrange("p (m e) -> p m e", m=2))
                    V.tensor_copy(lg[0:NS, 2, :], ps[0:NS, 1, 16:24])
                    dve.drain()
                    low = c("elow").rearrange("p (e j) -> p e j", e=NE)
                    tt(gt[:, :, :, :], mid(lg[:, :, :], NE), rep(lg[:, :, :], NE), ALU.is_gt)
                    tt(eq[:, :, :, :], mid(lg[:, :, :], NE), rep(lg[:, :, :], NE), ALU.is_equal)
                    V.tensor_reduce(gmx, lg[:, :, :], AX.X, ALU.max)
                    dve.drain()
                    for m in range(3):
                        tt(eq[:, m, :, :], eq[:, m, :, :], low, ALU.mult)
                    tt(gx[:, :, :], lg[:, :, :], rep(gmx, NE), ALU.subtract).then_inc(lgx_d.sem, 1)
                    dve.drain()
                    tt(gt[:, :, :, :], gt[:, :, :, :], eq[:, :, :, :], ALU.add)
                    dve.drain()
                    V.tensor_reduce(rank[:, :, :], gt[:, :, :, :], AX.X, ALU.add)
                    dve.drain()
                    V.tensor_scalar(sel[:, :, :], rank[:, :, :], 1.5, None, ALU.is_lt)
                    dve.drain()
                    tt(sel[:, :, :], sel[:, :, :], rep(c("valid"), NE), ALU.mult).then_inc(sel_d.sem, 1)
                    dve.wait_ge(lgx_a.sem, lgx_a.at(0))
                    dve.drain()
                    tt(gate[:, :, :], gx[:, :, :], sel[:, :, :], ALU.mult)
                    dve.drain()
                    V.tensor_reduce(gsum, gate[:, :, :], AX.X, ALU.add)
                    dve.drain()
                    V.tensor_scalar(gsum, gsum, 0.5, None, ALU.max)
                    dve.drain()
                    V.reciprocal(gsum, gsum)
                    dve.drain()
                    tt(gate[:, :, :], gate[:, :, :], rep(gsum, NE), ALU.mult)
                    dve.wait_ge(pos_pe.sem, pos_pe.at(0))
                    V.tensor_scalar(posm[:, :, :], sel[:, :, :], 1e6, -1e6, ALU.mult, ALU.add)
                    dve.drain()
                    tt(posm[:, 0:2, :], posm[:, 0:2, :], ps[:, 1, 64:80].rearrange("p (m e) -> p m e", m=2), ALU.add)
                    tt(posm[0:NS, 2, :], posm[0:NS, 2, :], ps[0:NS, 1, 80:88], ALU.add)
                    cn = cnt[0:NE, :]
                    V.tensor_copy(cn, ps[0:NE, 1, 96:97])
                    dve.drain()
                    V.tensor_scalar(nblk[0:NE, :], cn, 0.5, None, ALU.is_gt)
                    V.tensor_scalar(nb2[0:NE, :], cn, P + 0.5, None, ALU.is_gt)
                    V.tensor_scalar(eend[0:NE, :], cn, 2 * P + 0.5, None, ALU.is_gt)
                    dve.drain()
                    tt(nb2[0:NE, :], nb2[0:NE, :], eend[0:NE, :], ALU.add)
                    dve.drain()
                    tt(nblk[0:NE, :], nblk[0:NE, :], nb2[0:NE, :], ALU.add).then_inc(pos_d.sem, 1)
                    dve.wait_ge(nb_pe.sem, nb_pe.at(0))
                    V.tensor_copy(estart[0:NE, :], ps[0:NE, 1, 100:101])
                    dve.drain()
                    tt(eend[0:NE, :], estart[0:NE, :], nblk[0:NE, :], ALU.add)
                    V.tensor_scalar(ge1[0:NE, :], c("item")[0:NE, :], estart[0:NE, :], None, ALU.is_ge)
                    V.tensor_scalar(off[0:NE, :], c("item")[0:NE, :], estart[0:NE, :], -float(P), ALU.subtract, ALU.mult)
                    dve.drain()
                    V.tensor_scalar(ge2[0:NE, :], c("item")[0:NE, :], eend[0:NE, :], None, ALU.is_ge)
                    dve.drain()
                    tt(Mw[0:NE, :], ge1[0:NE, :], ge2[0:NE, :], ALU.subtract)
                    dve.drain()
                    tt(off[0:NE, :], off[0:NE, :], Mw[0:NE, :], ALU.mult).then_inc(nb_d.sem, 1)
                    V.memset(posI[:, :, NITEM:NITEM + 1], 0.0)
                    V.memset(gateI[:, :, NITEM:NITEM + 1], 0.0)
                    dve.wait_ge(it_pe.sem, it_pe.at(0))
                    for m in range(3):
                        n = ROWS[m]
                        V.tensor_copy(posI[0:n, m, 0:NITEM], ps[0:n, 4, 16 * m:16 * m + NITEM])
                        V.tensor_copy(gateI[0:n, m, 0:NITEM], ps[0:n, 4, 64 + 16 * m:64 + 16 * m + NITEM])
                    V.tensor_copy(itemi[0:1, 0:NITEM + 1], ps[0:1, 4, 128:129 + NITEM]).then_inc(items.sem, 1)
                    dve.drain()
                    dve.sem_inc(lo.sem, NU)
                    dve.wait_ge(items.sem, items.at(0))
                    n_items = dve.value_load(itemi[0:1, NITEM:NITEM + 1], min_val=1, max_val=NITEM)

                    def select(at):
                        for m in range(3):
                            n = ROWS[m]
                            V.tensor_scalar(Sel[0:n, m, :], c("iota")[0:n, :], posI[0:n, m, at], None, ALU.is_equal)
                            i = V.tensor_scalar(SelG[0:n, m, :], c("iota")[0:n, :], posI[0:n, m, at], gateI[0:n, m, at],
                                                ALU.is_equal, ALU.mult)
                        i.then_inc(g_sel.sem, 1)

                    select(slice(0, 1))

                    def add_item(w):
                        for d in range(KD):
                            dve.wait_ge(cmb_pe.sem, 8 * w + d + 1)
                            tt(xT[:, d, :], xT[:, d, :], ps[:, CMB_BANK[d % 4], 0:N], ALU.add).then_inc(cmb_ev.sem, 1)
                        dve.drain()

                    V.memset(yS[:, :], 0.0)
                    V.memset(SelT[:, :], 0.0)
                    dve.drain()
                    dve.sem_inc(yS_ev.sem, 1)
                    with dve.Fori(0, n_items) as w:
                        def low(i):
                            dve.wait_ge(hi.sem, NU * w + i + 1)
                            tt(Wl[i % 3], raw[i % NRAW].rearrange("p (k n) -> p k n", k=4), Wh[i % 3].bitcast(F32),
                               ALU.subtract).then_inc(lo.sem, 1)

                        low(0)
                        low(1)
                        add_item(w)
                        low(2)
                        for ch in range(FCH):
                            b = UNIT_AT["B", ch]
                            dve.wait_ge(m_sil.sem, FCH * w + ch + 1)
                            if ch >= 2:
                                dve.wait_ge(m_t.sem, FCH * w + ch - 1)
                            tt(gm[:, ch % 2, :], sl[:, ch % 2, :], ps[:, 2 + ch % 2, 256:512], ALU.mult).then_inc(m_g.sem, 1)
                            if ch < FCH - 1:
                                low(b + (2 if ch == 0 else 3))
                            if ch == 0:
                                low(UNIT_AT["C", 0])
                            dve.wait_ge(m_gh.sem, FCH * w + ch + 1)
                            tt(gTl[:, ch % 2, :, :], ps[:, 4 + ch % 2, 0:256].rearrange("p (f x) -> p f x", f=2),
                               gTh[:, ch % 2, :, :].bitcast(F32), ALU.subtract).then_inc(m_gl.sem, 1)
                            if ch < FCH - 1:
                                if ch > 0:
                                    low(UNIT_AT["C", ch])
                                low(UNIT_AT["A", ch + 2] if ch < FCH - 2 else NU - 1)
                            if ch == 1:
                                select(bass.ds(w + 1, 1))
                    add_item(n_items)
                    x_is_done()
            norm(4, V_FIN)

        @block.gpsimd
        def _(pool):
            pool.dma_start(pti[:, :], a["pages"]).then_inc(pt_in.sem, 16)
            pool.wait_ge(pt_in.sem, 16)

            cmpQ = cmpN.rearrange("p s (u q d) -> p s u q d", u=4, q=2)

            def pairs(x):
                return x.rearrange("(r q) (u d) -> r q u d", q=2, u=4)

            def page(l, cache, b, g):
                v = pool.value_load(pti[0:1, 2 * b + g:2 * b + g + 1], min_val=0, max_val=a[cache].shape[1] - 1)
                return a[cache][l, v]

            for l in range(2):
                if l == 1:
                    pool.wait_ge(st_state.sem, st_state.at(0))
                    pool.wait_ge(fy_pe.sem, fy_pe.at(0))
                pool.dma_start(cvp[0:24, :], a["state_conv"][l].rearrange("b j c -> (b j) c")).then_inc(cvp_in.sem, 16)
                if l == 0:
                    pool.wait_ge(xt_pe.sem, xt_pe.at(0, 8))
                    pool.wait_ge(bp3_pe.sem, bp3_pe.at(0))
                for b in range(NB):
                    for g in range(2):
                        src = pairs(page(l, "cache_cmp", b, g))
                        for q in range(2):
                            pool.dma_start(cmpQ[64 * g:64 * g + 64, b, :, q, :], src[:, q]).then_inc(cmp_in.sem, 16)
                pool.dma_start(m0c[0:MH, :], a["state_m"][l].rearrange("b h -> h b")).then_inc(m0_in.sem, 16)
                pool.dma_start(nld[0:NS, :], a["state_n"][l].rearrange("b h d -> (b h) d")).then_inc(n0_in.sem, 16)
                pool.wait_ge(kv_ev.sem, kv_ev.at(l))
                for k, name in enumerate(("p_cmp", "p_slc", "p_win")):
                    s = (st_cmp if k == 0 else st_kv).sem
                    pool.dma_start(outs[name][l].rearrange("(m p) c -> p m c", p=P), kv[:, 0:2, 256 * k:256 * k + 256]
                                   ).then_inc(s, 16)
                for k, name in enumerate(("s_cmp", "s_slc")):
                    pool.dma_start(outs[name][l].rearrange("b t c -> (b t) c"), kv[0:NS, 2, 256 * k:256 * k + 256]
                                   ).then_inc(st_kv.sem, 16)
                for b in range(NB):
                    pool.dma_start(outs["s_win"][l, b, PAST - TS:PAST, :], kv[TS * b:TS * b + TS, 2, 512:768]
                                   ).then_inc(st_kv.sem, 16)
                pool.dma_start(outs["s_win"][l, :, 0:PAST - TS, :], a["cache_win"][l, :, TS:PAST, :]).then_inc(st_win.sem, 16)
                pool.wait_ge(st_cmp.sem, st_cmp.at(l))
                src = pairs(outs["p_cmp"][l])
                for q in range(2):
                    pool.dma_start(cmpQ[:, 8, :, q, :], src[:, q]).then_inc(cmp_in.sem, 16)
                pool.wait_ge(gs_ev.sem, gs_ev.at(l))
                pool.dma_start(gscr[l], gns[0:NS, 2, :]).then_inc(gsS_st.sem, 16)
                pool.wait_ge(gsS_st.sem, gsS_st.at(l))
                pool.dma_start(gS[:, :, :], gscr[l].rearrange("n (h c) -> (n h) c", c=3).rearrange("(m p) c -> p m c", p=P)
                               ).then_inc(gsS_in.sem, 16)
                for t in range(2):
                    if t == 0:
                        pool.wait_ge(ct_pe.sem, ct_pe.at(l))
                    else:
                        pool.wait_ge(spv_pe.sem, spv_pe.at(l, 1))
                    for b in range(4):
                        for g in range(2):
                            pool.dma_start(sw[:, 0, b, g, :], page(l, "cache_slc", 4 * t + b, g)).then_inc(sw_in.sem, 16)
                    pool.dma_start(sw[:, 1, :, :, :].rearrange("p b g c -> p (b g) c"),
                                   a["cache_win"][l, 4 * t:4 * t + 4].rearrange("b (g p) c -> p (b g) c", p=P)
                                   ).then_inc(sw_in.sem, 16)
                    if t == 0:
                        pool.wait_ge(hid_pe.sem, hid_pe.at(l))
                        pool.dma_start(C0[:, :, :, 0:MD].rearrange("p b h e -> p (b h) e"),
                                       a["state_C"][l].rearrange("b h d e -> d (b h) e")).then_inc(c0_in.sem, 16)
                pool.wait_ge(spv_pe.sem, spv_pe.at(l))
                pool.wait_ge(mqk_ev.sem, mqk_ev.at(l))
                nc.gpsimd.memset(mqz[:, :, :, :], 0.0)
                pool.drain()
                for h in range(MH):
                    x = mqz[:, h, 0, 0:TS]
                    i = nc.gpsimd.tensor_copy(bass.AP(x.tensor, x.offset, [x.ap[0], [NS + TS, NB], [1, TS]]),
                                              mqT[:, h, T:N].rearrange("p (b t) -> p b t", b=NB))
                i.then_inc(mz_ev.sem, 1)
                pool.wait_ge(row_a.sem, row_a.at(l))
                pool.wait_ge(vt_ev.sem, vt_ev.at(l))
                pool.wait_ge(ktk_ev.sem, ktk_ev.at(l))

                def own_values(h):
                    if h >= 2:
                        pool.wait_ge(cn_pe.sem, cn_pe.at(l, h - 1))
                    y, z = mv[0:NS, 2, h, :], c("bsel")[0:NS, :]
                    nc.gpsimd.tensor_tensor(mvz[h % 2][0:NS, :, :], bass.AP(y.tensor, y.offset, [y.ap[0], [0, NB], y.ap[1]]),
                                            bass.AP(z.tensor, z.offset, [z.ap[0], z.ap[1], [0, 129]]), ALU.mult
                                            ).then_inc(vz_ev.sem, 1)

                own_values(0)
                own_values(1)
                pool.wait_ge(wcb_ev.sem, wcb_ev.at(l))
                for h in range(MH):
                    pool.wait_ge(num_pe.sem, num_pe.at(l, h + 1))
                    x, y = C0[:, :, h, :], wcb[:, h, :]
                    i = nc.gpsimd.tensor_tensor(x, x, bass.AP(y.tensor, y.offset, [y.ap[0], y.ap[1], [0, 129]]), ALU.mult)
                i.then_inc(cs_ev.sem, 1)
                for h in range(2, MH):
                    own_values(h)
                pool.wait_ge(cp_ev.sem, cp_ev.at(l))
                pool.dma_start(outs["p_C"][l, 0].rearrange("h d e -> d h e"), Cp[:, :, 0:MD]).then_inc(st_state.sem, 16)
                pool.wait_ge(cn_ev.sem, cn_ev.at(l))
                pool.dma_start(outs["s_C"][l].rearrange("b h d e -> d (b h) e"),
                               C0[:, :, :, 0:MD].rearrange("p b h e -> p (b h) e")).then_inc(st_state.sem, 16)
                pool.dma_start(outs["p_m"][l].rearrange("b h -> h b"), mout[0:MH, 0:1]).then_inc(st_state.sem, 16)
                pool.dma_start(outs["s_m"][l].rearrange("b h -> h b"), mout[0:MH, 1:9]).then_inc(st_state.sem, 16)
                pool.wait_ge(no_ev.sem, no_ev.at(l))
                pool.dma_start(outs["s_n"][l].rearrange("b h d -> (b h) d"), nout[0:NS, 0:P]).then_inc(st_state.sem, 16)
                pool.dma_start(outs["p_n"][l, 0], nout[0:MH, P:2 * P]).then_inc(st_state.sem, 16)
                pool.dma_start(outs["p_conv"][l, 0], cvo[0:3, :]).then_inc(st_state.sem, 16)
                pool.dma_start(outs["s_conv"][l].rearrange("b j c -> (b j) c"), cvo[3:27, :]).then_inc(st_state.sem, 16)
            pool.wait_ge(y_ev.sem, y_ev.at(0))
            pool.dma_start(outs["y_p"][0].rearrange("(m p) c -> p m c", p=P), ytok[:, 0:2, :]).then_inc(y_st.sem, 16)
            pool.dma_start(outs["y_s"].rearrange("b t c -> (b t) c"), ytok[0:NS, 2, :]).then_inc(y_st.sem, 16)
            pool.wait_ge(st_state.sem, st_state.at(1))
            pool.wait_ge(st_kv.sem, st_kv.at(1))
            pool.wait_ge(st_win.sem, st_win.at(1))
            pool.wait_ge(y_st.sem, 32)


OUTS = [("y_p", (1, T, D)), ("y_s", (NB, TS, D)),
        ("p_cmp", (2, T, 256)), ("p_slc", (2, T, 256)), ("p_win", (2, T, 256)),
        ("p_C", (2, 1, MH, MD, MD)), ("p_n", (2, 1, MH, MD)), ("p_m", (2, 1, MH)), ("p_conv", (2, 1, 3, 512)),
        ("s_cmp", (2, NB, TS, 256)), ("s_slc", (2, NB, TS, 256)), ("s_win", (2, NB, PAST, 256)),
        ("s_C", (2, NB, MH, MD, MD)), ("s_n", (2, NB, MH, MD)), ("s_m", (2, NB, MH)), ("s_conv", (2, NB, 3, 512))]
RETURN_SHAPES = [(1, T, D), (NB, TS, D), (2, 1, T, 2, 2, 64), (2, 1, T, 2, 2, 64), (2, 1, T, 2, 2, 64),
                 (2, 1, MH, MD, MD), (2, 1, MH, MD), (2, 1, MH), (2, 1, 3, 512),
                 (2, NB, TS, 2, 2, 64), (2, NB, TS, 2, 2, 64), (2, NB, PAST, 2, 2, 64),
                 (2, NB, MH, MD, MD), (2, NB, MH, MD), (2, NB, MH), (2, NB, 3, 512)]


def kernel(**inputs):
    import concourse.bacc as bacc
    from concourse.bass_utils import run_bass_kernel_spmd

    x = {k: np.asarray(v) for k, v in inputs.items()}
    n_phys = x["cache_cmp_kv"].shape[1]
    vecs = np.concatenate([x[k].reshape(-1, P) for k in
                           ("norm_mix", "norm_ffn", "norm_final", "m_conv_w", "m_conv_b", "m_norm", "cmp_pe")])
    arrays = {
        "const": CONST, "table": x["rel_bias_table"], "vecs": vecs, "x_prompt": x["x_prompt"],
        "x_sample": x["x_sample"], "gate_bias": x["m_gate_bias"],
        "cache_cmp": x["cache_cmp_kv"].reshape(2, n_phys, P, 256), "cache_slc": x["cache_slc_kv"].reshape(2, n_phys, P, 256),
        "cache_win": x["cache_win_kv"].reshape(2, NB, PAST, 256), "state_C": x["state_mlstm_C"],
        "state_n": x["state_mlstm_n"], "state_m": x["state_mlstm_m"], "state_conv": x["state_mlstm_conv"],
        "pages": x["page_table"].reshape(1, -1), "w_in": x["w_in"], "cmp_w1": x["cmp_w1"].reshape(2, 2, 2048, P),
        "cmp_w2": x["cmp_w2"], "m_qkv": x["m_qkv"], "w_up_a": x["w_up_a"], "w_up_b": x["w_up_b"], "w_out": x["w_out"],
        "ffn_w1": x["ffn_w1"], "ffn_w3": x["ffn_w3"], "ffn_w2": x["ffn_w2"], "router": x["moe_router"],
        "moe_w1": x["moe_w1"], "moe_w3": x["moe_w3"], "moe_w2": x["moe_w2"],
    }
    nc = bacc.Bacc("TRN2", target_bir_lowering=False, num_devices=1)
    feeds, a = {}, {}
    for name, v in arrays.items():
        v = np.ascontiguousarray(v)
        feeds["in_" + name] = v
        a[name] = nc.dram_tensor("in_" + name, v.shape, mybir.dt.from_np(v.dtype), kind="ExternalInput").ap()
    outs = {n: nc.dram_tensor("out_" + n, s, F32, kind="ExternalOutput").ap() for n, s in OUTS}
    build(nc, a, outs)
    r = run_bass_kernel_spmd(nc, [feeds], core_ids=[0])
    return tuple(r.results[0]["out_" + n].reshape(s) for (n, _), s in zip(OUTS, RETURN_SHAPES))
```
